# Optimizing a Trainium2 kernel written in Bass

```python
import jax, jax.numpy as jnp
from jax import lax
import numpy as np
import math

D_MODEL = 1024
BATCH = 1
SEQ = 256
DEPTH = 1

ATT_HEADS = 8
ATT_KV_HEADS = 2
ATT_HEAD_DIM = 64
ATT_GROUP = ATT_HEADS // ATT_KV_HEADS
WINDOW = 128
ATT_BLOCK = 128
RET_HEADS = 4
RET_KEY_DIM = 128
RET_VAL_DIM = 256
RET_CHUNK = 128
D_FF = -(-8 * D_MODEL // (3 * 256)) * 256
EPS = 1e-6

ATT_Q_W = ATT_HEADS * ATT_HEAD_DIM
ATT_KV_W = ATT_KV_HEADS * ATT_HEAD_DIM
RET_QK_W = RET_HEADS * RET_KEY_DIM
RET_V_W = RET_HEADS * RET_VAL_DIM
IN_WIDTHS = (ATT_Q_W, ATT_KV_W, ATT_KV_W, RET_QK_W, RET_QK_W, RET_V_W, RET_V_W, D_MODEL, D_MODEL)
D_IN = sum(IN_WIDTHS)


def rms_norm(x, g):
    xf = x.astype(jnp.float32)
    y = xf * lax.rsqrt(jnp.mean(xf * xf, axis=-1, keepdims=True) + EPS) * g.astype(jnp.float32)
    return y.astype(x.dtype)

def alibi_slopes(n_heads):
    return jnp.exp2(-8.0 * (jnp.arange(n_heads, dtype=jnp.float32) + 1.0) / n_heads)

def sliding_window_attention(q, k, v, sinks):
    b, s, _, hd = q.shape
    nb = s // ATT_BLOCK
    f32 = jnp.float32
    qb = q.astype(f32).reshape(b, nb, ATT_BLOCK, ATT_KV_HEADS, ATT_GROUP, hd) * (hd ** -0.5)

    def band(t):
        tp = jnp.pad(t.astype(f32), ((0, 0), (ATT_BLOCK, 0), (0, 0), (0, 0)))
        prev = tp[:, :s].reshape(b, nb, ATT_BLOCK, ATT_KV_HEADS, hd)
        cur = tp[:, ATT_BLOCK:].reshape(b, nb, ATT_BLOCK, ATT_KV_HEADS, hd)
        return jnp.concatenate([prev, cur], axis=2)

    kb, vb = band(k), band(v)
    i = jnp.arange(ATT_BLOCK)[:, None]
    j = jnp.arange(2 * ATT_BLOCK)[None, :]
    dist = i + ATT_BLOCK - j
    key_pos = jnp.arange(nb)[:, None, None] * ATT_BLOCK - ATT_BLOCK + j[None]
    valid = (dist >= 0) & (dist < WINDOW) & (key_pos >= 0)
    slopes = alibi_slopes(ATT_HEADS).reshape(ATT_KV_HEADS, ATT_GROUP)
    scores = jnp.einsum('bnikgd,bnjkd->bnkgij', qb, kb) - slopes[:, :, None, None] * dist.astype(f32)
    scores = jnp.where(valid[None, :, None, None], scores, -jnp.inf)
    sink = jnp.broadcast_to(sinks.astype(f32).reshape(ATT_KV_HEADS, ATT_GROUP)[None, None, :, :, None, None],
                            scores.shape[:-1] + (1,))
    probs = jax.nn.softmax(jnp.concatenate([scores, sink], axis=-1), axis=-1)[..., :-1]
    out = jnp.einsum('bnkgij,bnjkd->bnikgd', probs, vb)
    return out.reshape(b, s, ATT_Q_W)

def retention_chunkwise(q, k, v):
    b, s, h, dk = q.shape
    dv = v.shape[-1]
    nc = s // RET_CHUNK
    f32 = jnp.float32
    log_g = jnp.log(1.0 - jnp.exp2(-5.0 - jnp.arange(h, dtype=f32)))
    idx = jnp.arange(RET_CHUNK, dtype=f32)
    diff = idx[:, None] - idx[None, :]
    decay_intra = jnp.where(diff >= 0, jnp.exp(log_g[:, None, None] * jnp.maximum(diff, 0.0)), 0.0)
    decay_q = jnp.exp(log_g[:, None] * (idx + 1.0)).T[None, :, :, None]
    decay_k = jnp.exp(log_g[:, None] * (RET_CHUNK - 1.0 - idx)).T[None, :, :, None]
    decay_chunk = jnp.exp(log_g * RET_CHUNK)[None, :, None, None]

    def to_chunks(t):
        return t.astype(f32).reshape(b, nc, RET_CHUNK, h, t.shape[-1]).transpose(1, 0, 2, 3, 4)

    qc, kc, vc = to_chunks(q), to_chunks(k * (dk ** -0.5)), to_chunks(v)

    def step(state, inp):
        qi, ki, vi = inp
        scores = jnp.einsum('bihd,bjhd->bhij', qi, ki) * decay_intra
        o = jnp.einsum('bhij,bjhv->bihv', scores, vi)
        o = o + jnp.einsum('bihd,bhdv->bihv', qi, state) * decay_q
        state = decay_chunk * state + jnp.einsum('bjhd,bjhv->bhdv', ki * decay_k, vi)
        return state, o

    state0 = jnp.zeros((b, h, dk, dv), f32)
    _, o = lax.scan(step, state0, (qc, kc, vc))
    return o.transpose(1, 0, 2, 3, 4).reshape(b, s, h, dv)

def head_group_norm(o, gain):
    b, s, h, dv = o.shape
    mu = jnp.mean(o, axis=-1, keepdims=True)
    var = jnp.mean(jnp.square(o - mu), axis=-1, keepdims=True)
    return ((o - mu) * lax.rsqrt(var + EPS)).reshape(b, s, h * dv) * gain.astype(jnp.float32)

def first_inputs(seed: int = 0) -> dict:
    key = jax.random.key(seed)
    ks = jax.random.split(key, 16)
    f32 = jnp.float32

    def w(k, shape, fan_in):
        return jax.random.normal(k, shape, f32) * (fan_in ** -0.5)

    return {
        "x": jax.random.normal(ks[0], (BATCH, SEQ, D_MODEL), f32),
        "norm_mix": 1.0 + 0.02 * jax.random.normal(ks[1], (DEPTH, D_MODEL), f32),
        "w_in": w(ks[2], (DEPTH, D_MODEL, D_IN), D_MODEL),
        "att_sinks": 0.5 * jax.random.normal(ks[3], (DEPTH, ATT_HEADS), f32),
        "ret_gn_gain": 1.0 + 0.02 * jax.random.normal(ks[4], (DEPTH, RET_V_W), f32),
        "w_att_o": w(ks[5], (DEPTH, ATT_Q_W, D_MODEL), ATT_Q_W),
        "w_ret_o": w(ks[6], (DEPTH, RET_V_W, D_MODEL), RET_V_W),
        "w_out": w(ks[7], (DEPTH, D_MODEL, D_MODEL), D_MODEL),
        "norm_ffn": 1.0 + 0.02 * jax.random.normal(ks[8], (DEPTH, D_MODEL), f32),
        "w_gate": w(ks[9], (DEPTH, D_MODEL, D_FF), D_MODEL),
        "w_up": w(ks[10], (DEPTH, D_MODEL, D_FF), D_MODEL),
        "w_down": w(ks[11], (DEPTH, D_FF, D_MODEL), D_FF),
        "final_norm": 1.0 + 0.02 * jax.random.normal(ks[12], (D_MODEL,), f32),
    }

def first_block(x, norm_mix, w_in, att_sinks, ret_gn_gain, w_att_o, w_ret_o, w_out,
              norm_ffn, w_gate, w_up, w_down, final_norm):
    b, s, _ = x.shape
    offsets = [int(o) for o in np.cumsum(IN_WIDTHS)[:-1]]
    for l in range(DEPTH):
        h = rms_norm(x, norm_mix[l])
        proj = h @ w_in[l]
        aq, ak, av, rq, rk, rv, rg, ga, gr = jnp.split(proj, offsets, axis=-1)
        att = sliding_window_attention(
            aq.reshape(b, s, ATT_HEADS, ATT_HEAD_DIM),
            ak.reshape(b, s, ATT_KV_HEADS, ATT_HEAD_DIM),
            av.reshape(b, s, ATT_KV_HEADS, ATT_HEAD_DIM),
            att_sinks[l]).astype(x.dtype)
        ret = retention_chunkwise(
            rq.reshape(b, s, RET_HEADS, RET_KEY_DIM),
            rk.reshape(b, s, RET_HEADS, RET_KEY_DIM),
            rv.reshape(b, s, RET_HEADS, RET_VAL_DIM))
        ret = head_group_norm(ret, ret_gn_gain[l]).astype(x.dtype) * jax.nn.silu(rg)
        merged = jax.nn.sigmoid(ga) * (att @ w_att_o[l]) + jax.nn.sigmoid(gr) * (ret @ w_ret_o[l])
        x = x + merged @ w_out[l]
        h = rms_norm(x, norm_ffn[l])
        x = x + (jax.nn.silu(h @ w_gate[l]) * (h @ w_up[l])) @ w_down[l]
    return rms_norm(x, final_norm)


CHUNK = 64
MIX_A_WIDTH = D_MODEL // 2
MIX_B_WIDTH = D_MODEL - MIX_A_WIDTH
A_GROUPS = 8
A_GROUP_DIM = MIX_A_WIDTH // A_GROUPS
A_BLOCK = 128
B_HEADS = 8
B_HEAD_DIM = MIX_B_WIDTH // B_HEADS
B_LEFT_CHUNKS = 8
B_BAND = (B_LEFT_CHUNKS + 1) * CHUNK
REL_CLIP = 128
PEER_HEADS = 8
PEER_NKEYS = 128
PEER_EXPERTS = PEER_NKEYS * PEER_NKEYS
PEER_QDIM = 256
PEER_HALF = PEER_QDIM // 2
PEER_TOPK = 16
PEER_TOKEN_BLOCK = 128
IN_COLS = 2 * MIX_A_WIDTH + 3 * MIX_B_WIDTH
NEG_INF = -1e30


def rms_norm_2(x, g):
    xf = x.astype(jnp.float32)
    y = xf * lax.rsqrt(jnp.mean(xf * xf, axis=-1, keepdims=True) + EPS)
    return (y * g.astype(jnp.float32)).astype(x.dtype)

def gmlp_spatial_gating(u, v, norm_g, w_s, b_s):
    bsz, s, _ = u.shape
    u = jax.nn.gelu(u)
    v = rms_norm_2(jax.nn.gelu(v), norm_g)
    nblk = s // A_BLOCK
    v = v.reshape(bsz, nblk, A_BLOCK, A_GROUPS, A_GROUP_DIM)
    pos = jnp.arange(A_BLOCK)
    mask = (pos[None, :] // CHUNK) <= (pos[:, None] // CHUNK)
    w = jnp.where(mask[None], w_s, jnp.zeros_like(w_s)).astype(v.dtype)
    sp = jnp.einsum('gij,bnjgc->bnigc', w, v) + b_s.T.astype(v.dtype)[None, None, :, :, None]
    return u * sp.reshape(bsz, s, MIX_A_WIDTH)

def banded_chunk_attention(q, k, v, q_g, k_g, rel_bias):
    bsz, s, _ = q.shape
    nc = s // CHUNK
    pad = B_LEFT_CHUNKS * CHUNK
    q = rms_norm_2(q.reshape(bsz, nc, CHUNK, B_HEADS, B_HEAD_DIM), q_g)
    k = rms_norm_2(k.reshape(bsz, s, B_HEADS, B_HEAD_DIM), k_g)
    v = v.reshape(bsz, s, B_HEADS, B_HEAD_DIM)
    padw = ((0, 0), (pad, 0), (0, 0), (0, 0))
    kp = jnp.pad(k, padw).reshape(bsz, nc + B_LEFT_CHUNKS, CHUNK, B_HEADS, B_HEAD_DIM)
    vp = jnp.pad(v, padw).reshape(bsz, nc + B_LEFT_CHUNKS, CHUNK, B_HEADS, B_HEAD_DIM)
    band_idx = jnp.arange(nc)[:, None] + jnp.arange(B_LEFT_CHUNKS + 1)[None, :]
    kb = kp[:, band_idx].reshape(bsz, nc, B_BAND, B_HEADS, B_HEAD_DIM)
    vb = vp[:, band_idx].reshape(bsz, nc, B_BAND, B_HEADS, B_HEAD_DIM)
    scores = jnp.einsum('bcihd,bcjhd->bhcij', q, kb).astype(jnp.float32) * (B_HEAD_DIM ** -0.5)
    qi = jnp.arange(CHUNK)[:, None] + pad
    kj = jnp.arange(B_BAND)[None, :]
    rel_idx = jnp.clip(qi - kj, -REL_CLIP, REL_CLIP) + REL_CLIP
    bias = rel_bias.astype(jnp.float32)[:, rel_idx]
    valid = kj >= (pad - jnp.arange(nc)[:, None] * CHUNK)
    scores = scores + bias[None, :, None]
    scores = jnp.where(valid[None, None, :, None, :], scores, NEG_INF)
    p = jax.nn.softmax(scores, axis=-1).astype(v.dtype)
    out = jnp.einsum('bhcij,bcjhd->bcihd', p, vb)
    return out.reshape(bsz, s, MIX_B_WIDTH)

def peer_ffn(x, w_query, sub_keys, expert_u, expert_v):
    bsz, s, d = x.shape
    tokens = x.reshape(-1, PEER_TOKEN_BLOCK, d)

    def block(xb):
        q = (xb @ w_query).reshape(PEER_TOKEN_BLOCK, PEER_HEADS, 2, PEER_HALF)
        sc = jnp.einsum('thpd,hpkd->thpk', q, sub_keys).astype(jnp.float32)
        s_top, i_top = lax.top_k(sc, PEER_TOPK)
        cand = s_top[:, :, 0, :, None] + s_top[:, :, 1, None, :]
        cand_idx = i_top[:, :, 0, :, None] * PEER_NKEYS + i_top[:, :, 1, None, :]
        cand = cand.reshape(PEER_TOKEN_BLOCK, PEER_HEADS, PEER_TOPK * PEER_TOPK)
        cand_idx = cand_idx.reshape(PEER_TOKEN_BLOCK, PEER_HEADS, PEER_TOPK * PEER_TOPK)
        best, pos = lax.top_k(cand, PEER_TOPK)
        eidx = jnp.take_along_axis(cand_idx, pos, axis=-1)
        g = jax.nn.softmax(best, axis=-1)
        u = jnp.take(expert_u, eidx, axis=0)
        h = jax.nn.gelu(jnp.einsum('thkd,td->thk', u, xb))
        vv = jnp.take(expert_v, eidx, axis=0)
        return jnp.einsum('thk,thkd->td', (g * h.astype(jnp.float32)).astype(xb.dtype), vv)

    return lax.map(block, tokens).reshape(bsz, s, d)

def second_inputs(seed: int = 0) -> dict:
    key = jax.random.key(seed)
    ks = jax.random.split(key, 16)
    f32 = jnp.float32
    nrm = lambda k, shape, sc: jax.random.normal(k, shape, f32) * sc
    return {
        "x": nrm(ks[0], (BATCH, SEQ, D_MODEL), 1.0),
        "ln_mix_g": 1.0 + nrm(ks[1], (DEPTH, D_MODEL), 0.02),
        "w_in": nrm(ks[2], (DEPTH, D_MODEL, IN_COLS), D_MODEL ** -0.5),
        "gmlp_norm_g": 1.0 + nrm(ks[3], (DEPTH, MIX_A_WIDTH), 0.02),
        "gmlp_w_s": nrm(ks[4], (DEPTH, A_GROUPS, A_BLOCK, A_BLOCK), A_BLOCK ** -0.5),
        "gmlp_b_s": 1.0 + nrm(ks[5], (DEPTH, A_GROUPS, A_BLOCK), 0.1),
        "q_norm_g": 1.0 + nrm(ks[6], (DEPTH, B_HEAD_DIM), 0.02),
        "k_norm_g": 1.0 + nrm(ks[7], (DEPTH, B_HEAD_DIM), 0.02),
        "rel_bias": nrm(ks[8], (DEPTH, B_HEADS, 2 * REL_CLIP + 1), 0.1),
        "w_out": nrm(ks[9], (DEPTH, D_MODEL, D_MODEL), D_MODEL ** -0.5),
        "ln_ffn_g": 1.0 + nrm(ks[10], (DEPTH, D_MODEL), 0.02),
        "peer_w_query": nrm(ks[11], (DEPTH, D_MODEL, PEER_HEADS * PEER_QDIM), D_MODEL ** -0.5),
        "peer_sub_keys": nrm(ks[12], (DEPTH, PEER_HEADS, 2, PEER_NKEYS, PEER_HALF), PEER_HALF ** -0.5),
        "peer_u": nrm(ks[13], (DEPTH, PEER_EXPERTS, D_MODEL), D_MODEL ** -0.5),
        "peer_v": nrm(ks[14], (DEPTH, PEER_EXPERTS, D_MODEL), 0.1),
    }

def second_block(x, ln_mix_g, w_in, gmlp_norm_g, gmlp_w_s, gmlp_b_s, q_norm_g, k_norm_g, rel_bias,
              w_out, ln_ffn_g, peer_w_query, peer_sub_keys, peer_u, peer_v):
    a0, a1 = MIX_A_WIDTH, 2 * MIX_A_WIDTH
    q0, k0, v0 = a1, a1 + MIX_B_WIDTH, a1 + 2 * MIX_B_WIDTH
    for l in range(DEPTH):
        xn = rms_norm_2(x, ln_mix_g[l])
        proj = xn @ w_in[l]
        a_out = gmlp_spatial_gating(proj[..., :a0], proj[..., a0:a1],
                                    gmlp_norm_g[l], gmlp_w_s[l], gmlp_b_s[l])
        b_out = banded_chunk_attention(proj[..., q0:k0], proj[..., k0:v0], proj[..., v0:],
                                       q_norm_g[l], k_norm_g[l], rel_bias[l])
        x = x + jnp.concatenate([a_out, b_out], axis=-1) @ w_out[l]
        x = x + peer_ffn(rms_norm_2(x, ln_ffn_g[l]), peer_w_query[l], peer_sub_keys[l],
                         peer_u[l], peer_v[l])
    return x


def setup_inputs(seed=0):
    out = dict(first_inputs(seed))
    for name, value in second_inputs(seed + 1).items():
        if name != "x":
            out[name + "_2"] = value
    return out


def reference(
    x, norm_mix, w_in, att_sinks, ret_gn_gain, w_att_o, w_ret_o, w_out, norm_ffn, w_gate, w_up,
    w_down, final_norm, ln_mix_g_2, w_in_2, gmlp_norm_g_2, gmlp_w_s_2, gmlp_b_s_2, q_norm_g_2,
    k_norm_g_2, rel_bias_2, w_out_2, ln_ffn_g_2, peer_w_query_2, peer_sub_keys_2, peer_u_2,
    peer_v_2,
):
    x = first_block(
        x, norm_mix, w_in, att_sinks, ret_gn_gain, w_att_o, w_ret_o, w_out, norm_ffn, w_gate,
        w_up, w_down, final_norm,
    )
    return second_block(
        x, ln_mix_g_2, w_in_2, gmlp_norm_g_2, gmlp_w_s_2, gmlp_b_s_2, q_norm_g_2, k_norm_g_2,
        rel_bias_2, w_out_2, ln_ffn_g_2, peer_w_query_2, peer_sub_keys_2, peer_u_2, peer_v_2,
    )


_drawn_inputs = setup_inputs


def setup_inputs(seed=0):
    import zlib

    import numpy as np

    out = dict(_drawn_inputs(seed))
    spreads = {}
    factors = {'norm_mix': 3.041,
     'att_sinks': 9.862,
     'ret_gn_gain': 6.869,
     'norm_ffn': 3.694,
     'ln_mix_g_2': 3.991,
     'gmlp_norm_g_2': 20.04,
     'q_norm_g_2': 8.0,
     'k_norm_g_2': 8.0,
     'rel_bias_2': 22.477,
     'ln_ffn_g_2': 64.0,
     'gmlp_b_s_2': 3.485}
    for name, (base, spread) in spreads.items():
        noise = np.random.default_rng([zlib.crc32(name.encode()), seed]).standard_normal(out[name].shape)
        drawn = base * np.exp(spread * noise) if base else spread * noise
        out[name] = __import__('jax').numpy.asarray(drawn.astype(out[name].dtype))
    for name, factor in factors.items():
        out[name] = (out[name] * factor).astype(out[name].dtype)
    return out
```

```python
import math
from contextlib import ExitStack

import concourse.bass as bass
from concourse import mybir


def two_block_kernel(
    nc, x, norm_mix, w_in, att_sinks, ret_gn_gain, w_att_o, w_ret_o, w_out, norm_ffn, w_gate, w_up, w_down,
    final_norm, ln_mix_g_2, w_in_2, gmlp_norm_g_2, gmlp_w_s_2, gmlp_b_s_2, q_norm_g_2, k_norm_g_2, rel_bias_2,
    w_out_2, ln_ffn_g_2, peer_w_query_2, peer_sub_keys_2, peer_u_2, peer_v_2, out,
):
    f32, u32 = mybir.dt.float32, mybir.dt.uint32
    ALU, ACT, AX = mybir.AluOpType, mybir.ActivationFunctionType, mybir.AxisListType
    ds = bass.ds

    P = 128
    S, D = x.shape[1], x.shape[2]
    TB = S // P
    KD = D // P
    EPS = 1e-6
    MASKED = -1e30
    HEADS, KV_HEADS, HD = 8, 2, 64
    GROUP = HEADS // KV_HEADS
    RH, RK, RV = 4, 128, 256
    FF = w_gate.shape[2]
    IN2 = w_in_2.shape[2]
    HALF = D // 2
    NKEYS, TOPK, PEER_HEADS = 128, 16, 8
    HP = 2 * PEER_HEADS
    REL = rel_bias_2.shape[2]
    CHUNK = 512

    AQ, AK, AV, RQ, RKO, RVO = 0, 512, 640, 768, 1280, 1792
    RG, GA, GR = 2816, 3840, 4864
    IN1 = w_in.shape[2]

    slopes = [2.0 ** (-8.0 * (h + 1) / HEADS) for h in range(HEADS)]
    log_decay = [math.log(1.0 - 2.0 ** (-5.0 - h)) for h in range(RH)]
    RET_SCALE = RK ** -0.5
    HD_SCALE = HD ** -0.5

    C_IN, C_ATT, C_RET, C_OUT, C_FF, C_DOWN, C_IN2, C_OUT2, C_QUERY, C_END = 0, 12, 14, 16, 18, 29, 40, 45, 47, 51
    N_FF = FF // 256
    assert N_FF == C_DOWN - C_FF == C_IN2 - C_DOWN

    def numbered(*groups):
        at, first = 0, {}
        for name, count in groups:
            first[name] = at
            at += count
        return first

    TR = numbered(("gains", 1), ("ws", 2), ("keys", 4), ("norm1", 4), ("q_att", 4), ("k_att", 1), ("p_att", 6),
                  ("att", 2), ("ret_qk", 4), ("ret", 4), ("merged", 4), ("norm2", 4), ("ff", 11), ("norm3", 4),
                  ("qk_band", 8), ("p_band", 6), ("mixed", 4), ("norm4", 4), ("query", 8))
    MM = numbered(("s_att", 6), ("o_att", 2), ("ret_s", 4), ("ret_state", 2), ("ret_o", 4), ("gate", 2),
                  ("s_band", 6), ("o_band", 2), ("peer_s", 8))
    RS = numbered(("norm1", 1), ("ret", 1), ("norm2", 1), ("final", 1), ("norm3", 1), ("gate", 1), ("band", 1), ("norm4", 1))
    SCORE_JOBS = [(0, 0, 4), (0, 4, 4), (1, 0, 2), (1, 2, 2), (1, 4, 2), (1, 6, 2)]
    G_MIX, G_FFN, G_MIX2, G_RET, G_BS, G_Q, G_K, G_ROWS = 0, 8, 16, 24, 32, 40, 41, 42

    RING = 8

    ctx = ExitStack()
    with ctx:
        def sb(name, shape, dt=f32):
            return ctx.enter_context(nc.sbuf_tensor(name, shape, dt))

        def sem(name):
            return ctx.enter_context(nc.semaphore(name))

        x_sb = sb("x_sb", [P, TB, D])
        xn = sb("xn", [P, TB, D])
        hT = sb("hT", [P, KD, S])
        big = sb("big", [P, 2 * KD * CHUNK + TB * IN1])
        wslot = [big[:, s * KD * CHUNK:(s + 1) * KD * CHUNK] for s in range(2)]
        big2 = big[:, 2 * KD * CHUNK:]
        proj = big2.rearrange("p (b n) -> p b n", b=TB)
        proj2 = big2[:, 0:TB * IN2].rearrange("p (b n) -> p b n", b=TB)
        qp = big2[:, 0:TB * HP * P].rearrange("p (b n) -> p b n", b=TB)
        rel_toep = big2[:, TB * IN2:TB * IN2 + HEADS * 256].rearrange("p (h m) -> p h m", h=HEADS)
        u_ring = [big[:, s * D:(s + 1) * D] for s in range(RING)]
        v_ring = [big[:, (RING + s) * D:(RING + s + 1) * D] for s in range(RING)]
        arena = sb("arena", [P, 11776])
        probs = arena[:, 0:3072]
        probs_t = arena[:, 3072:6144].rearrange("p (n i) -> p n i", i=P)
        probs_of = [probs[:, 0:1024].rearrange("p (h j) -> p h j", h=HEADS),
                    probs[:, 1024:3072].rearrange("p (h j) -> p h j", h=HEADS)]
        qT = arena[0:HD, 6144:8192].rearrange("p (h t) -> p h t", h=HEADS)
        kT = arena[0:HD, 8192:8192 + KV_HEADS * S].rearrange("p (h t) -> p h t", h=KV_HEADS)
        ret_qk = arena[:, 8704:10752].rearrange("p (h a t) -> p h a t", h=RH, a=2)
        attT = arena[:, 10752:11776].rearrange("p (k t) -> p k t", k=4)
        ret_s = xn[:, 0, :].rearrange("p (h c i) -> p h c i", h=RH, c=TB)
        state = xn[:, 1, :].rearrange("p (h v) -> p h v", h=RH)
        retT = hT
        mergedT = arena[:, 3072:3072 + KD * S].rearrange("p (k t) -> p k t", k=KD)
        ffT = arena[:, 0:22 * S].rearrange("p (k t) -> p k t", k=22)
        ff_rows = arena[:, 22 * S:22 * S + 1024].rearrange("p (a b n) -> p a b n", a=2, b=TB)
        ff_silu = arena[:, 22 * S + 1024:22 * S + 2048].rearrange("p (a b n) -> p a b n", a=2, b=TB)
        kT2 = arena[0:HD, 8192:10240].rearrange("p (h t) -> p h t", h=HEADS)
        sq = arena[:, 10240:11264]
        qpT = arena[:, 0:HP * S].rearrange("p (n t) -> p n t", n=HP)
        peer_sc = arena[:, 4096:4096 + TB * HP * P].rearrange("p (n k) -> p n k", k=2 * P)
        raw_ws = arena[:, 0:1024].rearrange("p (g j) -> p g j", g=8)
        raw_keys = arena[:, 1024:3072].rearrange("p (n d) -> p n d", n=HP)
        ident = sb("ident", [P, P])
        zeros = sb("zeros", [P, P])
        gain_rows = sb("gain_rows", [G_ROWS, P])
        gains = sb("gains", [P, G_ROWS])
        neg_dist = sb("neg_dist", [P, 2 * P])
        age = sb("age", [P, P])
        q_pos = sb("q_pos", [P, P])
        k_age = sb("k_age", [P, 1])
        decay_t = sb("decay_t", [P, RH, P])
        decay_q = sb("decay_q", [P, RH, P])
        decay_k = sb("decay_k", [P, RH])
        sinks = sb("sinks", [P, HEADS])
        iota16 = sb("iota16", [P, TOPK])
        final_g = sb("final_g", [P, D])
        peer_g = sb("peer_g", [P, D])
        gate_g = sb("gate_g", [P, HALF])
        ws_t = sb("ws_t", [P, 8, P])
        keys_t = sb("keys_t", [P, HP, P])
        rel_ext = sb("rel_ext", [HEADS, 512])
        rel_dram = nc.dram_tensor("rel_ext_dram", [HEADS, 512], f32)
        ss = sb("ss", [P, 32])
        var = sb("var", [P, 32])
        sd = sb("sd", [P, 32])
        rstd = sb("rstd", [P, 32])
        newton = sb("newton", [P, 32])
        mx = sb("mx", [P, TB, HEADS])
        neg_mx = sb("neg_mx", [P, TB, HEADS])
        sink_e = sb("sink_e", [P, TB, HEADS])
        den = sb("den", [P, TB, HEADS])
        bn = sb("bn", [P, TB * RH, 6])
        mv = sb("mv", [P, TB * RH, 2])
        tk_work = sb("tk_work", [P, 2 * P])
        tk_rest = sb("tk_rest", [P, 2 * P])
        tk_top = sb("tk_top", [P, 2, TOPK])
        tk_ix = sb("tk_ix", [P, 2, TOPK], u32)
        tk_ixf = sb("tk_ixf", [P, 2, TOPK])
        cand = sb("cand", [P, TOPK * TOPK])
        cand_rest = sb("cand_rest", [P, TOPK * TOPK])
        best = sb("best", [P, TOPK])
        pos = sb("pos", [P, TOPK], u32)
        pos_ij = sb("pos_ij", [P, 2, TOPK], u32)
        pos_f = sb("pos_f", [P, 2, TOPK])
        hit = sb("hit", [P, TOPK, TOPK])
        picked = sb("picked", [P, 2, TOPK])
        eidx_f = sb("eidx_f", [P, TOPK])
        expert = sb("expert", [P, TB * PEER_HEADS, TOPK], u32)
        neg_best = sb("neg_best", [P, 1])
        g_exp = sb("g_exp", [P, TOPK])
        g_sum = sb("g_sum", [P, 1])
        g_inv = sb("g_inv", [P, 1])
        gate_w = sb("gate_w", [P, TB * PEER_HEADS, TOPK])
        ix_now = [sb(f"ix_now{i}", [P, TOPK], u32) for i in range(2)]
        hid = [sb(f"hid{i}", [P, TOPK]) for i in range(2)]
        hid_g = [sb(f"hid_g{i}", [P, TOPK]) for i in range(2)]
        wgt = [sb(f"wgt{i}", [P, TOPK]) for i in range(2)]
        diag = [sb(f"diag{i}", [P, P]) for i in range(4)]

        gemm = [ctx.enter_context(nc.psum_tensor(f"gemm{i}", [P, CHUNK], f32)) for i in range(4)]
        trb = [ctx.enter_context(nc.psum_tensor(f"trb{i}", [P, CHUNK], f32)) for i in range(2)]
        mmb = [ctx.enter_context(nc.psum_tensor(f"mmb{i}", [P, CHUNK], f32)) for i in range(2)]

        x_landed, gains_landed, aux_landed, rows_landed = sem("x_landed"), sem("gains_landed"), sem("aux_landed"), sem("rows_landed")
        w_landed = [sem("w_landed0"), sem("w_landed1")]
        g_filled = sem("g_filled")
        g_free = [sem(f"g_free{i}") for i in range(4)]
        tr_filled = sem("tr_filled")
        tr_out = [sem("tr_out0"), sem("tr_out1")]
        mm_filled = sem("mm_filled")
        mm_out = [sem("mm_out0"), sem("mm_out1")]
        consts_made, decay_made, decay_masked, gains_zeroed = sem("consts_made"), sem("decay_made"), sem("decay_masked"), sem("gains_zeroed")
        var_ready, sd_ready = sem("var_ready"), sem("sd_ready")
        normed = sem("normed")
        max_ready, exp_done, probs_ready = sem("max_ready"), sem("exp_done"), sem("probs_ready")
        sink_ready = sem("sink_ready")
        ret_kd_ready, ret_qd_ready, ret_ready = sem("ret_kd_ready"), sem("ret_qd_ready"), sem("ret_ready")
        merged_ready, ff_silu_ready, ff_ready = sem("merged_ready"), sem("ff_silu_ready"), sem("ff_ready")
        gate_v_ready, mixed_a_ready, qk_normed = sem("gate_v_ready"), sem("mixed_a_ready"), sem("qk_normed")
        rel_filled, rel_stored, rel_loaded, rel_ready = sem("rel_filled"), sem("rel_stored"), sem("rel_loaded"), sem("rel_ready")
        expert_ready, best_ready, gexp_done = sem("expert_ready"), sem("best_ready"), sem("gexp_done")
        u_free, v_free = sem("u_free"), sem("v_free")
        u_landed = [sem(f"u_landed{i}") for i in range(RING)]
        v_landed = [sem(f"v_landed{i}") for i in range(RING)]
        gelu_done, wgt_ready, diag_ready = sem("gelu_done"), sem("wgt_ready"), sem("diag_ready")
        peer_summed, out_ready, stored = sem("peer_summed"), sem("out_ready"), sem("stored")
        pool_held, dve_held = sem("pool_held"), sem("dve_held")
        dve_step, act_step, pool_step = sem("dve_step"), sem("act_step"), sem("pool_step")

        class Steps:

            def __init__(self, engine, own):
                self.engine, self.own, self.n = engine, own, 0

            def put(self, ins):
                ins.then_inc(self.own, 1)
                self.n = self.n + 1

            def settle(self):
                self.engine.wait_ge(self.own, self.n)

            def link(self, ins):
                self.put(ins)
                self.settle()

            def enter(self, i, per, first=0):
                self.before = self.n
                self.n = self.n + (i - first) * per if first else self.n + i * per

            def leave(self, trips, per):
                self.n = self.before + trips * per

        block = ctx.enter_context(nc.Block())

        @block.sync
        def _(sp):
            sp.dma_start(x_sb[:], x[0].rearrange("(b p) d -> p b d", p=P)).then_inc(x_landed, 16)

            def load(c, slot, pieces):
                if not (isinstance(c, int) and c < 2):
                    sp.wait_ge(g_filled, 2 * (c - 2) + 2)
                for dst, src in pieces:
                    sp.dma_start(dst, src).then_inc(w_landed[slot], 16 // len(pieces) if len(pieces) > 1 else 16)

            def cols(w, k, at, width, slot, off=0, total=CHUNK):
                view = wslot[slot][:, 0:k * total].rearrange("p (k n) -> p k n", k=k)
                return view[:, :, off:off + width], w.rearrange("(k p) n -> p k n", p=P)[:, :, ds(at, width)]

            w1, wa, wr, wo = w_in[0], w_att_o[0], w_ret_o[0], w_out[0]
            load(0, 0, [cols(w1, KD, 0, CHUNK, 0)])
            load(1, 1, [cols(w1, KD, AK, 256, 1, total=256)])
            with sp.Fori(0, 5) as i:
                for j in range(2):
                    load(i * 2 + (2 + j), j, [cols(w1, KD, i * (2 * CHUNK) + (RQ + j * CHUNK), CHUNK, j)])
            for n in range(2):
                load(C_ATT + n, n, [cols(wa, 4, n * CHUNK, CHUNK, n)])
            for n in range(2):
                load(C_RET + n, n, [cols(wr, KD, n * CHUNK, CHUNK, n)])
            for n in range(2):
                load(C_OUT + n, n, [cols(wo, KD, n * CHUNK, CHUNK, n)])

            def load_ff(c, slot, at):
                sp.wait_ge(g_filled, 2 * (c - 2) + 2)
                for off, w in ((0, w_gate[0]), (256, w_up[0])):
                    dst, src = cols(w, KD, at, 256, slot, off)
                    sp.dma_start(dst, src).then_inc(w_landed[slot], 16)

            with sp.Fori(0, 5) as i:
                for j in range(2):
                    load_ff(i * 2 + (C_FF + j), j, i * 512 + 256 * j)
            load_ff(C_FF + 10, 0, 10 * 256)

            def load_down(c, slot, kk):
                sp.wait_ge(g_filled, 2 * (c - 2) + 2)
                sp.dma_start(wslot[slot][:, 0:2 * D].rearrange("p (k n) -> p k n", k=2),
                             w_down[0].rearrange("(k p) n -> p k n", p=P)[:, ds(kk, 2), :]).then_inc(w_landed[slot], 16)

            load_down(C_DOWN, 1, 0)
            with sp.Fori(0, 5) as i:
                for j in range(2):
                    load_down(i * 2 + (C_DOWN + 1 + j), j, i * 4 + (2 + 2 * j))
            with sp.Fori(0, 2) as i:
                for j in range(2):
                    load(i * 2 + (C_IN2 + j), j, [cols(w_in_2[0], KD, i * (2 * CHUNK) + j * CHUNK, CHUNK, j)])
            load(C_IN2 + 4, 0, [cols(w_in_2[0], KD, 4 * CHUNK, CHUNK, 0)])
            for n in range(2):
                load(C_OUT2 + n, (C_OUT2 + n) % 2, [cols(w_out_2[0], KD, n * CHUNK, CHUNK, (C_OUT2 + n) % 2)])
            for n in range(4):
                load(C_QUERY + n, (C_QUERY + n) % 2, [cols(peer_w_query_2[0], KD, n * CHUNK, CHUNK, (C_QUERY + n) % 2)])
            for b in range(TB):
                sp.wait_ge(out_ready, b + 1)
                sp.dma_start(out[0, b * P:(b + 1) * P, :], xn[:, b, :]).then_inc(stored, 16)
            sp.wait_ge(stored, 16 * TB)

        def landed(c):
            ff_before = len([k for k in range(C_FF, C_DOWN) if k % 2 == c % 2 and k <= c])
            return 16 * (c // 2 + 1) + 16 * ff_before

        @block.gpsimd
        def _(pool):
            me = Steps(pool, pool_step)
            me.put(nc.gpsimd.memset(ident[:], 0.0))
            nc.gpsimd.memset(zeros[:], 0.0).then_inc(consts_made, 1)
            nc.gpsimd.iota(age[:], pattern=[[1, P]], base=0, channel_multiplier=-1, allow_small_or_imprecise_dtypes=True).then_inc(consts_made, 1)
            nc.gpsimd.iota(q_pos[:], pattern=[[1, P]], base=1, channel_multiplier=0, allow_small_or_imprecise_dtypes=True).then_inc(consts_made, 1)
            nc.gpsimd.iota(k_age[:], pattern=[[0, 1]], base=P - 1, channel_multiplier=-1, allow_small_or_imprecise_dtypes=True).then_inc(consts_made, 1)
            nc.gpsimd.iota(iota16[:], pattern=[[1, TOPK]], base=0, channel_multiplier=0, allow_small_or_imprecise_dtypes=True).then_inc(consts_made, 1)
            me.put(nc.gpsimd.iota(neg_dist[:], pattern=[[1, 2 * P]], base=-P, channel_multiplier=-1, allow_small_or_imprecise_dtypes=True))
            me.settle()
            nc.gpsimd.affine_select(out=ident[:], in_=ident[:], compare_op=ALU.not_equal, fill=1.0, base=0,
                                    pattern=[[-1, P]], channel_multiplier=1).then_inc(consts_made, 1)
            me.link(nc.gpsimd.affine_select(out=neg_dist[:], in_=neg_dist[:], compare_op=ALU.is_ge, fill=MASKED, base=P,
                                            pattern=[[-1, 2 * P]], channel_multiplier=1))
            nc.gpsimd.affine_select(out=neg_dist[:], in_=neg_dist[:], compare_op=ALU.is_gt, fill=MASKED, base=0,
                                    pattern=[[1, 2 * P]], channel_multiplier=-1).then_inc(consts_made, 1)
            pool.wait_ge(decay_made, RH)
            nc.gpsimd.affine_select(out=decay_t[:], in_=decay_t[:], compare_op=ALU.is_ge, fill=0.0, base=0,
                                    pattern=[[0, RH], [1, P]], channel_multiplier=-1).then_inc(decay_masked, 1)
            pool.wait_ge(rel_filled, 1)
            pool.dma_start(rel_dram[:], rel_ext[:]).then_inc(rel_stored, 16)
            pool.wait_ge(rel_stored, 16)
            pool.wait_ge(merged_ready, TB)
            pool.wait_ge(g_filled, 2 * C_OUT)
            pool.dma_start(rel_toep, bass.AP(tensor=rel_dram, offset=P, ap=[[1, P], [512, HEADS], [1, 256]])).then_inc(rel_ready, 16)

            def gather(n, par):
                pool.wait_ge(expert_ready, n + 1)
                me.link(nc.gpsimd.tensor_copy(ix_now[par][:], expert[:, ds(n, 1), :].rearrange("p a k -> p (a k)")))
                for table, ring, free, there in ((peer_u_2, u_ring, u_free, u_landed), (peer_v_2, v_ring, v_free, v_landed)):
                    for k in range(TOPK):
                        pool.wait_ge(free, n * TOPK + (k + 1))
                        pool.sem_inc(pool_held, 1)
                        nc.gpsimd.indirect_dma_start(
                            out=ring[k % RING], out_offset=None, in_=table[0],
                            in_offset=bass.IndirectOffsetOnAxis(ap=ix_now[par][:, k:k + 1], axis=0),
                        ).then_inc(there[k % RING], 16)

            with pool.Fori(0, TB * PEER_HEADS // 2) as i:
                me.enter(i, 2)
                for par in range(2):
                    gather(i * 2 + par, par)
            me.leave(TB * PEER_HEADS // 2, 2)

        @block.scalar
        def _(act):
            me = Steps(act, act_step)
            act.wait_ge(gains_zeroed, 1)
            for at, src in ((G_MIX, norm_mix[0].rearrange("(k p) -> k p", p=P)), (G_FFN, norm_ffn[0].rearrange("(k p) -> k p", p=P)),
                            (G_MIX2, ln_mix_g_2[0].rearrange("(k p) -> k p", p=P)), (G_RET, ret_gn_gain[0].rearrange("(k p) -> k p", p=P)),
                            (G_BS, gmlp_b_s_2[0])):
                act.dma_start(gain_rows[at:at + 8, :], src).then_inc(gains_landed, 16)
            act.dma_start(gain_rows[G_Q:G_Q + 1, 0:HD], q_norm_g_2).then_inc(gains_landed, 16)
            act.dma_start(gain_rows[G_K:G_K + 1, 0:HD], k_norm_g_2).then_inc(gains_landed, 16)
            act.dma_start(raw_ws, gmlp_w_s_2[0].rearrange("g i j -> i g j")).then_inc(aux_landed, 16)
            act.dma_start(raw_keys, peer_sub_keys_2[0].rearrange("h a k d -> k (h a) d")).then_inc(aux_landed, 16)
            act.dma_start(rel_ext[:, 127:127 + REL], rel_bias_2[0]).then_inc(rel_loaded, 16)
            for dst, src in ((sinks, att_sinks[0]), (final_g, final_norm), (peer_g, ln_ffn_g_2[0]), (gate_g, gmlp_norm_g_2[0])):
                act.dma_start(dst[:], src.partition_broadcast(P)).then_inc(rows_landed, 16)

            act.wait_ge(consts_made, 7)
            for h in range(RH):
                nc.scalar.activation(decay_q[:, h, :], q_pos[:], ACT.Exp, scale=log_decay[h])
                nc.scalar.activation(decay_k[:, h:h + 1], k_age[:], ACT.Exp, scale=log_decay[h])
                nc.scalar.activation(decay_t[:, h, :], age[:], ACT.Exp, scale=log_decay[h]).then_inc(decay_made, 1)

            def root(name, width):
                act.wait_ge(var_ready, RS[name] + 1)
                nc.scalar.activation(sd[:, 0:width], var[:, 0:width], ACT.Sqrt).then_inc(sd_ready, 1)

            def product(c, par, dst, func=ACT.Copy, scale=1.0, width=CHUNK):
                for b in range(TB):
                    act.wait_ge(g_filled, c * 2 + (b + 1))
                    nc.scalar.activation(dst(b), gemm[2 * par + b][:, 0:width], func, scale=scale).then_inc(g_free[2 * par + b], 1)

            def softmax_exp(first):
                for b in range(TB):
                    act.wait_ge(max_ready, first + b + 1)
                    for h in range(HEADS):
                        nc.scalar.activation(probs_of[b][:, h, :], probs_of[b][:, h, :], ACT.Exp, bias=neg_mx[:, b, h:h + 1],
                                             accum_out=den[:, b, h:h + 1]).then_inc(exp_done, 1)

            def copy_out(kind, jobs, n, dst, src):
                filled, outs, banks = (tr_filled, tr_out, trb) if kind == "tr" else (mm_filled, mm_out, mmb)
                act.wait_ge(filled, n + 1)
                nc.scalar.activation(dst, src(banks[n % 2]), ACT.Copy).then_inc(outs[n % 2], 1)

            root("norm1", TB)
            product(0, 0, lambda b: proj[:, b, AQ:AQ + CHUNK], scale=HD_SCALE)
            product(1, 1, lambda b: proj[:, b, AK:AK + 256], width=256)
            with act.Fori(0, 2) as i:
                for j in range(2):
                    product(i * 2 + (2 + j), j, lambda b: proj[:, b, ds(i * (2 * CHUNK) + (RQ + j * CHUNK), CHUNK)])
            softmax_exp(0)
            act.wait_ge(sink_ready, 1)
            nc.scalar.activation(sink_e[:], sink_e[:], ACT.Exp).then_inc(exp_done, 1)
            for j in range(2):
                product(6 + j, j, lambda b: proj[:, b, RG + j * CHUNK:RG + (j + 1) * CHUNK], ACT.Silu)
            with act.Fori(0, 2) as i:
                for j in range(2):
                    product(i * 2 + (8 + j), j, lambda b: proj[:, b, ds(i * (2 * CHUNK) + (GA + j * CHUNK), CHUNK)], ACT.Sigmoid)
            for n in range(6):
                copy_out("tr", TR, TR["p_att"] + n, probs_t[:, 4 * n:4 * n + 4, :].rearrange("p n i -> p (n i)"), lambda t: t[:])
            for b in range(TB):
                copy_out("mm", MM, MM["o_att"] + b, proj[:, b, AQ:AQ + CHUNK], lambda t: t[:])
            for b in range(TB):
                copy_out("tr", TR, TR["att"] + b, attT[:, :, b * P:(b + 1) * P], lambda t: t[:].rearrange("p (k t) -> p k t", k=4))
            for h in range(2):
                copy_out("mm", MM, MM["ret_state"] + h, state[:, 2 * h:2 * h + 2, :].rearrange("p h v -> p (h v)"), lambda t: t[:])
            root("ret", TB * RH)
            for n in range(4):
                b, half = n // 2, n % 2
                copy_out("tr", TR, TR["merged"] + n, mergedT[:, 4 * half:4 * half + 4, b * P:(b + 1) * P],
                         lambda t: t[:].rearrange("p (k t) -> p k t", k=4))
            root("norm2", TB)

            def ff_gate(c, par):
                for b in range(TB):
                    act.wait_ge(g_filled, c * 2 + (b + 1))
                    nc.scalar.activation(ff_silu[:, par, b, :], gemm[2 * par + b][:, 0:256], ACT.Silu).then_inc(ff_silu_ready, 1)

            def ff_turn(f, par, odd):
                n_par = (TR["ff"] + par) % 2
                act.wait_ge(tr_filled, f + (TR["ff"] + 1))
                nc.scalar.activation(ffT[:, ds(f * 2, 2), :].rearrange("p k t -> p (k t)"), trb[n_par][:], ACT.Copy).then_inc(tr_out[n_par], 1)

            ff_gate(C_FF, 0)
            with act.Fori(0, 5) as i:
                ff_gate(i * 2 + (C_FF + 1), 1)
                ff_turn(i * 2, 0, 0)
                ff_gate(i * 2 + (C_FF + 2), 0)
                ff_turn(i * 2 + 1, 1, 1)
            ff_turn(10, 0, 0)
            root("final", TB)
            root("norm3", TB)
            for n, func in enumerate((ACT.Gelu_apprx_tanh, ACT.Gelu_apprx_tanh, ACT.Copy, ACT.Copy, ACT.Copy)):
                product(C_IN2 + n, n % 2, lambda b: proj2[:, b, n * CHUNK:(n + 1) * CHUNK], func)
            root("gate", TB)
            root("band", 32)
            softmax_exp(2)
            for n in range(6):
                copy_out("tr", TR, TR["p_band"] + n, probs_t[:, 4 * n:4 * n + 4, :].rearrange("p n i -> p (n i)"), lambda t: t[:])
            for b in range(TB):
                copy_out("mm", MM, MM["o_band"] + b, proj2[:, b, D:D + HALF], lambda t: t[:])
            for n in range(4):
                b, half = n // 2, n % 2
                copy_out("tr", TR, TR["mixed"] + n, hT[:, 4 * half:4 * half + 4, b * P:(b + 1) * P],
                         lambda t: t[:].rearrange("p (k t) -> p k t", k=4))
            root("norm4", TB)
            for n in range(4):
                b, half = n // 2, n % 2
                copy_out("tr", TR, TR["norm4"] + n, hT[:, 4 * half:4 * half + 4, b * P:(b + 1) * P],
                         lambda t: t[:].rearrange("p (k t) -> p k t", k=4))
            for n in range(4):
                c = C_QUERY + n
                product(c, c % 2, lambda b: qp[:, b, n * CHUNK:(n + 1) * CHUNK])
            for n in range(8):
                b, four = n // 4, n % 4
                copy_out("tr", TR, TR["query"] + n, qpT[:, 4 * four:4 * four + 4, b * P:(b + 1) * P],
                         lambda t: t[:].rearrange("p (k t) -> p k t", k=4))
            for n in range(8):
                copy_out("mm", MM, MM["peer_s"] + n, peer_sc[:, 2 * n:2 * n + 2, :].rearrange("p n k -> p (n k)"), lambda t: t[:])

            def best_exp(n):
                act.wait_ge(best_ready, n + 1)
                nc.scalar.activation(g_exp[:], best[:], ACT.Exp, bias=neg_best[:], accum_out=g_sum[:]).then_inc(gexp_done, 1)

            def weigh(n, par):
                act.wait_ge(u_free, n * TOPK + (RING + TOPK))
                nc.scalar.activation(hid_g[par][:], hid[par][:], ACT.Gelu_apprx_tanh).then_inc(gelu_done, 1)
                act.wait_ge(wgt_ready, n + 1)
                for k in range(TOPK):
                    act.wait_ge(v_free, n * TOPK + (RING + k - 3))
                    nc.scalar.activation(diag[k % 4][:], ident[:], ACT.Copy, scale=wgt[par][:, k:k + 1]).then_inc(diag_ready, 1)

            best_exp(0)
            with act.Fori(0, 7) as i:
                for par in range(2):
                    best_exp(i * 2 + (1 + par))
                    weigh(i * 2 + par, par)
            best_exp(15)
            weigh(14, 0)
            weigh(15, 1)

        @block.vector
        def _(dve):
            me = Steps(dve, dve_step)
            V = nc.vector
            V.memset(gain_rows[:], 0.0).then_inc(gains_zeroed, 1)

            def copy_out_tr(n, dst, src, times=None, scale=None):
                dve.wait_ge(tr_filled, n + 1)
                if times is None:
                    V.tensor_copy(dst, src).then_inc(tr_out[n % 2], 1)
                else:
                    V.tensor_tensor(dst, src, times, ALU.mult).then_inc(tr_out[n % 2], 1)

            dve.wait_ge(tr_filled, TR["gains"] + 1)
            V.tensor_copy(gains[:], trb[TR["gains"] % 2][:, 0:G_ROWS]).then_inc(tr_out[TR["gains"] % 2], 1)
            dve.wait_ge(tr_out[TR["gains"] % 2], TR["gains"] // 2 + 1)
            dve.wait_ge(rel_loaded, 16)
            V.tensor_copy(rel_ext[:, 0:127], rel_ext[:, 127:128].to_broadcast([HEADS, 127]))
            V.tensor_copy(rel_ext[:, 127 + REL:512], rel_ext[:, 126 + REL:127 + REL].to_broadcast([HEADS, 512 - 127 - REL])).then_inc(rel_filled, 1)
            for n in range(2):
                t = TR["ws"] + n
                dve.wait_ge(tr_filled, t + 1)
                me.put(V.tensor_copy(ws_t[:, 4 * n:4 * n + 4, :].rearrange("p g i -> p (g i)"), trb[t % 2][:]))
                me.settle()
                V.memset(ws_t[64:P, 4 * n:4 * n + 4, 0:64], 0.0).then_inc(tr_out[t % 2], 1)
            for n in range(4):
                copy_out_tr(TR["keys"] + n, keys_t[:, 4 * n:4 * n + 4, :].rearrange("p n k -> p (n k)"), trb[(TR["keys"] + n) % 2][:])

            def inverse_root(name, width):
                dve.wait_ge(sd_ready, RS[name] + 1)
                r, t, v = rstd[:, 0:width], newton[:, 0:width], var[:, 0:width]
                me.link(V.reciprocal(r, sd[:, 0:width]))
                me.link(V.tensor_tensor(t, r, r, ALU.mult))
                me.link(V.tensor_tensor(t, t, v, ALU.mult))
                me.link(V.tensor_scalar(t, t, -0.5, 1.5, ALU.mult, ALU.add))
                me.link(V.tensor_tensor(r, r, t, ALU.mult))

            def row_norm(name, src, width, scratch):
                for b in range(TB):
                    me.put(V.tensor_tensor_reduce(out=scratch(b), in0=src(b), in1=src(b), scale=1.0, scalar=0.0, op0=ALU.mult,
                                                  op1=ALU.add, accum_out=ss[:, b:b + 1]))
                me.settle()
                V.tensor_scalar(var[:, 0:TB], ss[:, 0:TB], 1.0 / width, EPS, ALU.mult, ALU.add).then_inc(var_ready, 1)
                inverse_root(name, TB)

            NORMS = numbered(("norm1", 1), ("norm2", 1), ("norm3", 1), ("norm4", 1))

            def norm_to_columns(name, gain):
                row_norm(name, lambda b: x_sb[:, b, :], D, lambda b: xn[:, b, :])
                for b in range(TB):
                    V.tensor_scalar(xn[:, b, :], x_sb[:, b, :], rstd[:, b:b + 1], None, ALU.mult).then_inc(normed, 1)
                for n in range(4):
                    b, half = n // 2, n % 2
                    t = TR[name] + n
                    copy_out_tr(t, hT[:, 4 * half:4 * half + 4, b * P:(b + 1) * P], trb[t % 2][:].rearrange("p (k t) -> p k t", k=4),
                                gains[:, gain + 4 * half:gain + 4 * half + 4].unsqueeze(2).to_broadcast([P, 4, P]))

            dve.wait_ge(x_landed, 16)
            norm_to_columns("norm1", G_MIX)

            for n in range(4):
                b, four = n // 2, n % 2
                t = TR["q_att"] + n
                copy_out_tr(t, qT[:, 4 * four:4 * four + 4, b * P:(b + 1) * P], trb[t % 2][0:HD, :].rearrange("p (h t) -> p h t", h=4))
            t = TR["k_att"]
            copy_out_tr(t, kT.rearrange("p h t -> p (h t)"), trb[t % 2][0:HD, :])

            def finish_softmax(first):
                for b in range(TB):
                    w = (b + 1) * P
                    V.tensor_tensor(probs_of[b], probs_of[b], den[:, b, :].unsqueeze(2).to_broadcast([P, HEADS, w]),
                                    ALU.mult).then_inc(probs_ready, 1)

            dve.wait_ge(consts_made, 7)
            dve.wait_ge(rows_landed, 64)
            for n, (b, h0, hn) in enumerate(SCORE_JOBS):
                m, w = MM["s_att"] + n, (b + 1) * P
                dve.wait_ge(mm_filled, m + 1)
                for h in range(hn):
                    ins = V.scalar_tensor_tensor(out=probs_of[b][:, h0 + h, :], in0=neg_dist[:, 2 * P - w:2 * P], scalar=slopes[h0 + h],
                                                 in1=mmb[m % 2][:, h * w:(h + 1) * w], op0=ALU.mult, op1=ALU.add)
                    if h < hn - 1:
                        me.put(ins)
                    else:
                        ins.then_inc(mm_out[m % 2], 1)
            for p in range(2):
                dve.wait_ge(mm_out[p], (MM["s_att"] + 6) // 2)
            for b in range(TB):
                me.link(V.tensor_reduce(mx[:, b, :], probs_of[b], axis=AX.X, op=ALU.max))
                me.link(V.tensor_tensor(mx[:, b, :], mx[:, b, :], sinks[:], ALU.max))
                V.tensor_scalar(neg_mx[:, b, :], mx[:, b, :], -1.0, None, ALU.mult).then_inc(max_ready, 1)
            for b in range(TB):
                ins = V.tensor_tensor(sink_e[:, b, :], sinks[:], mx[:, b, :], ALU.subtract)
                if b < TB - 1:
                    me.put(ins)
            ins.then_inc(sink_ready, 1)
            dve.wait_ge(exp_done, TB * HEADS + 1)
            me.link(V.tensor_tensor(den[:], den[:], sink_e[:], ALU.add))
            me.link(V.reciprocal(den[:], den[:]))
            finish_softmax(0)

            dve.wait_ge(decay_masked, 1)
            for j in range(2):
                for b in range(TB):
                    dve.wait_ge(g_free[2 * j + b], 2)
            for h in range(RH):
                k_cols = proj[:, 0, RKO + h * RK:RKO + (h + 1) * RK]
                t = TR["ret_qk"] + h
                copy_out_tr(t, ret_qk[:, h, :, :].rearrange("p a t -> p (a t)"), trb[t % 2][:])
                V.tensor_scalar(k_cols, k_cols, decay_k[:, h:h + 1], RET_SCALE, ALU.mult, ALU.mult).then_inc(ret_kd_ready, 1)
            for h in range(RH):
                m = MM["ret_s"] + h
                dve.wait_ge(mm_filled, m + 1)
                for c in range(TB):
                    ins = V.scalar_tensor_tensor(out=ret_s[:, h, c, :], in0=mmb[m % 2][:, c * P:(c + 1) * P], scalar=RET_SCALE,
                                                 in1=decay_t[:, h, :], op0=ALU.mult, op1=ALU.mult)
                    if c < TB - 1:
                        me.put(ins)
                ins.then_inc(mm_out[m % 2], 1)
                q2 = ret_qk[:, h, 0, P:2 * P]
                V.tensor_tensor(q2, q2, decay_q[:, h, :], ALU.mult).then_inc(ret_qd_ready, 1)
            for h in range(RH):
                m = MM["ret_o"] + h
                dve.wait_ge(mm_filled, m + 1)
                for c in range(TB):
                    me.put(V.bn_stats(bn[:, 2 * h + c, :], mmb[m % 2][:, c * RV:(c + 1) * RV]))
                V.tensor_copy(proj[:, :, RVO + h * RV:RVO + (h + 1) * RV], mmb[m % 2][:].rearrange("p (c v) -> p c v", c=TB)).then_inc(mm_out[m % 2], 1)
            me.settle()
            for n in range(TB * RH):
                me.put(V.bn_aggr(mv[:, n, :], bn[:, n, :]))
            me.settle()
            V.tensor_scalar(var[:, 0:TB * RH], mv[:, :, 1], EPS, None, ALU.add).then_inc(var_ready, 1)
            inverse_root("ret", TB * RH)
            for p in range(2):
                dve.wait_ge(mm_out[p], (MM["ret_o"] + RH) // 2)
            for h in range(RH):
                for c in range(TB):
                    o = proj[:, c, RVO + h * RV:RVO + (h + 1) * RV]
                    n = 2 * h + c
                    me.put(V.tensor_scalar(o, o, mv[:, n, 0:1], rstd[:, n:n + 1], ALU.subtract, ALU.mult))
            me.settle()
            for j in range(2):
                for b in range(TB):
                    dve.wait_ge(g_free[2 * j + b], 4)
            for b in range(TB):
                o = proj[:, b, RVO:RVO + D]
                V.tensor_tensor(o, o, proj[:, b, RG:RG + D], ALU.mult).then_inc(ret_ready, 1)
            for n in range(2):
                for b in range(TB):
                    dve.wait_ge(g_filled, 2 * (C_ATT + n) + b + 1)
                    ga = proj[:, b, GA + n * CHUNK:GA + (n + 1) * CHUNK]
                    V.tensor_tensor(ga, gemm[2 * n + b][:], ga, ALU.mult).then_inc(g_free[2 * n + b], 1)
            for n in range(4):
                b, half = n // 2, n % 2
                t = TR["ret"] + n
                copy_out_tr(t, retT[:, 4 * half:4 * half + 4, b * P:(b + 1) * P], trb[t % 2][:].rearrange("p (k t) -> p k t", k=4),
                            gains[:, G_RET + 4 * half:G_RET + 4 * half + 4].unsqueeze(2).to_broadcast([P, 4, P]))
            for n in range(2):
                for b in range(TB):
                    dve.wait_ge(g_filled, 2 * (C_RET + n) + b + 1)
                    gr = proj[:, b, GR + n * CHUNK:GR + (n + 1) * CHUNK]
                    V.tensor_tensor(gr, gemm[2 * n + b][:], gr, ALU.mult).then_inc(g_free[2 * n + b], 1)
            for n in range(2):
                for b in range(TB):
                    dve.wait_ge(g_free[2 * n + b], (C_RET + n) // 2 + 1)
            for b in range(TB):
                V.tensor_tensor(proj[:, b, GA:GA + D], proj[:, b, GA:GA + D], proj[:, b, GR:GR + D], ALU.add).then_inc(merged_ready, 1)

            def residual(c, n):
                p = c % 2
                for b in range(TB):
                    dve.wait_ge(g_filled, 2 * c + b + 1)
                    xs = x_sb[:, b, n * CHUNK:(n + 1) * CHUNK]
                    V.tensor_tensor(xs, gemm[2 * p + b][:], xs, ALU.add).then_inc(g_free[2 * p + b], 1)

            for n in range(2):
                residual(C_OUT + n, n)
            for i in range(4):
                dve.wait_ge(g_free[i], C_OUT // 2 + 1)

            norm_to_columns("norm2", G_FFN)

            def ff_up(c, par):
                for b in range(TB):
                    dve.wait_ge(ff_silu_ready, (c - C_FF) * 2 + (b + 1))
                    V.tensor_tensor(ff_rows[:, par, b, :], gemm[2 * par + b][:, 256:512], ff_silu[:, par, b, :], ALU.mult).then_inc(g_free[2 * par + b], 1)

            ff_up(C_FF, 0)
            ff_up(C_FF + 1, 1)
            n_ff = TR["ff"]
            with dve.Fori(1, 5) as i:
                for j in range(2):
                    dve.wait_ge(tr_filled, i * 2 + (n_ff - 1 + j))
                    ff_up(i * 2 + (C_FF + j), j)
            dve.wait_ge(tr_filled, n_ff + 9)
            ff_up(C_FF + 10, 0)
            for b in range(TB):
                for n in range(2):
                    dve.wait_ge(g_filled, 2 * C_IN2 - 1 + b)
                    xs = x_sb[:, b, n * CHUNK:(n + 1) * CHUNK]
                    V.tensor_tensor(xs, gemm[2 * n + b][:], xs, ALU.add).then_inc(g_free[2 * n + b], len([c for c in range(C_DOWN, C_IN2) if c % 2 == n]))
            for n in range(2):
                for b in range(TB):
                    dve.wait_ge(g_free[2 * n + b], (C_IN2 - 2 + n) // 2 + 1)

            row_norm("final", lambda b: x_sb[:, b, :], D, lambda b: xn[:, b, :])
            for b in range(TB):
                me.put(V.scalar_tensor_tensor(out=x_sb[:, b, :], in0=x_sb[:, b, :], scalar=rstd[:, b:b + 1], in1=final_g[:],
                                              op0=ALU.mult, op1=ALU.mult))
            me.settle()
            norm_to_columns("norm3", G_MIX2)

            for n in range(2):
                for b in range(TB):
                    dve.wait_ge(g_free[2 * n + b], (C_IN2 + n) // 2 + 1)
            row_norm("gate", lambda b: proj2[:, b, HALF:D], HALF, lambda b: sq[:, b * HALF:(b + 1) * HALF])
            for b in range(TB):
                V.scalar_tensor_tensor(out=proj2[:, b, HALF:D], in0=proj2[:, b, HALF:D], scalar=rstd[:, b:b + 1], in1=gate_g[:],
                                       op0=ALU.mult, op1=ALU.mult).then_inc(gate_v_ready, 1)
            for n in range(2):
                for b in range(TB):
                    dve.wait_ge(g_free[2 * n + b], (C_IN2 + 2 + n) // 2 + 1)
            for b in range(TB):
                qk = proj2[:, b, D:2 * D]
                me.link(V.tensor_tensor(sq, qk, qk, ALU.mult))
                me.link(V.tensor_reduce(ss[:, 16 * b:16 * b + 16], sq.rearrange("p (h d) -> p h d", d=HD), axis=AX.X, op=ALU.add))
            V.tensor_scalar(var[:, 0:32], ss[:, 0:32], 1.0 / HD, EPS, ALU.mult, ALU.add).then_inc(var_ready, 1)
            inverse_root("band", 32)
            for b in range(TB):
                qk = proj2[:, b, D:2 * D].rearrange("p (h d) -> p h d", d=HD)
                V.tensor_tensor(qk, qk, rstd[:, 16 * b:16 * b + 16].unsqueeze(2).to_broadcast([P, 16, HD]), ALU.mult).then_inc(qk_normed, 1)
            for n in range(8):
                b, is_k, four = n // 4, (n // 2) % 2, n % 2
                t = TR["qk_band"] + n
                dve.wait_ge(tr_filled, t + 1)
                dst = (kT2 if is_k else qT)[:, 4 * four:4 * four + 4, b * P:(b + 1) * P]
                g = G_K if is_k else G_Q
                V.tensor_scalar(dst, trb[t % 2][0:HD, :].rearrange("p (h t) -> p h t", h=4), gains[0:HD, g:g + 1],
                                1.0 if is_k else HD_SCALE, ALU.mult, ALU.mult).then_inc(tr_out[t % 2], 1)
            for b in range(TB):
                m = MM["gate"] + b
                dve.wait_ge(mm_filled, m + 1)
                bank = mmb[m % 2][:].rearrange("p (g c) -> p g c", g=8)
                V.tensor_tensor(sq[:, b * HALF:(b + 1) * HALF].rearrange("p (g c) -> p g c", g=8), bank,
                                gains[:, G_BS:G_BS + 8].unsqueeze(2).to_broadcast([P, 8, HD]), ALU.add).then_inc(mm_out[m % 2], 1)
                dve.wait_ge(mm_out[m % 2], m // 2 + 1)
                V.tensor_tensor(proj2[:, b, 0:HALF], proj2[:, b, 0:HALF], sq[:, b * HALF:(b + 1) * HALF], ALU.mult).then_inc(mixed_a_ready, 1)
            dve.wait_ge(rel_ready, 16)
            for n, (b, h0, hn) in enumerate(SCORE_JOBS):
                m, w = MM["s_band"] + n, (b + 1) * P
                dve.wait_ge(mm_filled, m + 1)
                V.tensor_tensor(probs_of[b][:, h0:h0 + hn, :], mmb[m % 2][:].rearrange("p (h j) -> p h j", h=hn),
                                rel_toep[:, h0:h0 + hn, w - 1::-1] if w < 256 else rel_toep[:, h0:h0 + hn, ::-1], ALU.add).then_inc(mm_out[m % 2], 1)
            for p in range(2):
                dve.wait_ge(mm_out[p], (MM["s_band"] + 6) // 2)
            for b in range(TB):
                w = (b + 1) * P
                me.link(V.memset(probs_of[b][0:64, :, w - 64:w], MASKED))
                me.link(V.tensor_reduce(mx[:, b, :], probs_of[b], axis=AX.X, op=ALU.max))
                V.tensor_scalar(neg_mx[:, b, :], mx[:, b, :], -1.0, None, ALU.mult).then_inc(max_ready, 1)
            dve.wait_ge(exp_done, 2 * TB * HEADS + 1)
            me.link(V.reciprocal(den[:], den[:]))
            finish_softmax(2)
            for n in range(2):
                residual(C_OUT2 + n, n)
            for i in range(4):
                dve.wait_ge(g_free[i], (C_OUT2 + (i // 2 == 0)) // 2 + 1)

            row_norm("norm4", lambda b: x_sb[:, b, :], D, lambda b: xn[:, b, :])
            for b in range(TB):
                V.scalar_tensor_tensor(out=xn[:, b, :], in0=x_sb[:, b, :], scalar=rstd[:, b:b + 1], in1=peer_g[:],
                                       op0=ALU.mult, op1=ALU.mult).then_inc(normed, 1)
            for p in range(2):
                dve.wait_ge(mm_out[p], (MM["peer_s"] + 8) // 2)
            dve.sem_inc(u_free, RING)
            dve.sem_inc(v_free, RING)

            def top16(values, rest, top, ix):
                me.settle()
                dve.sem_inc(dve_held, 1)
                me.put(V.max(top[:, 0:8], values))
                me.settle()
                dve.sem_inc(dve_held, 1)
                me.put(V.max_index(ix[:, 0:8], top[:, 0:8], values))
                me.put(V.match_replace(rest, top[:, 0:8], values, -3.0e38))
                me.settle()
                dve.sem_inc(dve_held, 1)
                me.put(V.max(top[:, 8:16], rest))
                me.settle()
                dve.sem_inc(dve_held, 1)
                me.put(V.max_index(ix[:, 8:16], top[:, 8:16], rest))

            def select(n):
                me.put(V.tensor_copy(tk_work[:], peer_sc[:, ds(n, 1), :].rearrange("p a k -> p (a k)")))
                for a in range(2):
                    top16(tk_work[:, a * P:(a + 1) * P], tk_rest[:, a * P:(a + 1) * P], tk_top[:, a, :], tk_ix[:, a, :])
                me.settle()
                me.put(V.tensor_copy(tk_ixf[:], tk_ix[:]))
                me.put(V.tensor_tensor(cand[:].rearrange("p (i j) -> p i j", i=TOPK), tk_top[:, 0, :].unsqueeze(2).to_broadcast([P, TOPK, TOPK]),
                                        tk_top[:, 1, :].unsqueeze(1).to_broadcast([P, TOPK, TOPK]), ALU.add))
                top16(cand[:], cand_rest[:], best[:], pos[:])
                me.settle()
                V.tensor_scalar(neg_best[:], best[:, 0:1], -1.0, None, ALU.mult).then_inc(best_ready, 1)
                me.put(V.tensor_scalar(pos_ij[:, 0, :], pos[:], 4, None, ALU.logical_shift_right))
                me.link(V.tensor_scalar(pos_ij[:, 1, :], pos[:], TOPK - 1, None, ALU.bitwise_and))
                me.link(V.tensor_copy(pos_f[:], pos_ij[:]))
                for a in range(2):
                    me.link(V.tensor_tensor(hit[:], iota16[:].unsqueeze(1).to_broadcast([P, TOPK, TOPK]),
                                            pos_f[:, a, :].unsqueeze(2).to_broadcast([P, TOPK, TOPK]), ALU.is_equal))
                    me.link(V.tensor_tensor(hit[:], hit[:], tk_ixf[:, a, :].unsqueeze(1).to_broadcast([P, TOPK, TOPK]), ALU.mult))
                    me.link(V.tensor_reduce(picked[:, a, :], hit[:], axis=AX.X, op=ALU.add))
                me.link(V.scalar_tensor_tensor(out=eidx_f[:], in0=picked[:, 0, :], scalar=float(NKEYS), in1=picked[:, 1, :], op0=ALU.mult, op1=ALU.add))
                V.tensor_copy(expert[:, ds(n, 1), :].rearrange("p a k -> p (a k)"), eidx_f[:]).then_inc(expert_ready, 1)
                dve.wait_ge(gexp_done, n + 1)
                me.link(V.reciprocal(g_inv[:], g_sum[:]))
                me.link(V.tensor_scalar(gate_w[:, ds(n, 1), :].rearrange("p a k -> p (a k)"), g_exp[:], g_inv[:], None, ALU.mult))

            def hidden(n, par, b):
                for k in range(TOPK):
                    dve.wait_ge(u_landed[k % RING], n * 32 + 16 * (k // RING + 1))
                    V.tensor_tensor_reduce(out=u_ring[k % RING], in0=u_ring[k % RING], in1=xn[:, b, :], scale=1.0, scalar=0.0, op0=ALU.mult,
                                           op1=ALU.add, accum_out=hid[par][:, k:k + 1]).then_inc(u_free, 1)
                dve.wait_ge(gelu_done, n + 1)
                V.tensor_tensor(wgt[par][:], hid_g[par][:], gate_w[:, ds(n, 1), :].rearrange("p a k -> p (a k)"), ALU.mult).then_inc(wgt_ready, 1)

            steps = me.n
            select(0)
            PER = me.n - steps
            with dve.Fori(0, 4) as i:
                me.enter(i, 2 * PER)
                for par in range(2):
                    select(i * 2 + (par + 1))
                    hidden(i * 2 + par, par, 0)
            me.leave(4, 2 * PER)
            with dve.Fori(0, 3) as i:
                me.enter(i, 2 * PER)
                for par in range(2):
                    select(i * 2 + (par + 9))
                    hidden(i * 2 + (8 + par), par, 1)
            me.leave(3, 2 * PER)
            select(15)
            hidden(14, 0, 1)
            hidden(15, 1, 1)
            for b in range(TB):
                dve.wait_ge(peer_summed, b + 1)
                if b == 0:
                    dve.wait_ge(u_free, RING + TB * PEER_HEADS * TOPK)
                for n in range(2):
                    ins = V.tensor_copy(xn[:, b, n * CHUNK:(n + 1) * CHUNK], gemm[2 * b + n][:])
                    if n == 0:
                        me.put(ins)
                ins.then_inc(out_ready, 1)

        @block.tensor
        def _(pe):
            def tr_bank(n):
                if n >= 2:
                    pe.wait_ge(tr_out[n % 2], n // 2)
                return trb[n % 2]

            def mm_bank(n):
                if n >= 2:
                    pe.wait_ge(mm_out[n % 2], n // 2)
                return mmb[n % 2]

            def tr_ready(n):
                pe.wait_ge(tr_out[n % 2], n // 2 + 1)

            def mm_ready(n):
                pe.wait_ge(mm_out[n % 2], n // 2 + 1)

            def turn(n, sources, rows=P):
                bank = tr_bank(n)
                for i, src in enumerate(sources):
                    last = nc.tensor.transpose(bank[0:rows, i * P:i * P + src.shape[0]], src, ident[0:src.shape[0], 0:src.shape[0]])
                last.then_inc(tr_filled, 1)

            pe.wait_ge(consts_made, 7)
            pe.wait_ge(gains_landed, 7 * 16)
            turn(TR["gains"], [gain_rows[:]])
            pe.wait_ge(aux_landed, 32)
            for n in range(2):
                turn(TR["ws"] + n, [raw_ws[:, 4 * n + i, :] for i in range(4)])
            for n in range(4):
                turn(TR["keys"] + n, [raw_keys[:, 4 * n + i, :] for i in range(4)])

            def turn_rows(name, rows):
                for n in range(4):
                    b, half = n // 2, n % 2
                    turn(TR[name] + n, [rows(b)[:, (4 * half + i) * P:(4 * half + i + 1) * P] for i in range(4)])

            def product(c, par, landed_at, lhs=hT, k_tiles=KD, width=CHUNK, c_half=None):
                w = wslot[par][:, 0:k_tiles * width].rearrange("p (k n) -> p k n", k=k_tiles)
                pe.wait_ge(w_landed[par], landed_at)
                for b in range(TB):
                    if not (isinstance(c_half, int) and c_half == 0):
                        pe.wait_ge(g_free[2 * par + b], c_half)
                    for k in range(k_tiles):
                        last = nc.tensor.matmul(gemm[2 * par + b][:, 0:width], lhs[:, k, b * P:(b + 1) * P], w[:, k, :],
                                                start=(k == 0), stop=(k == k_tiles - 1))
                    last.then_inc(g_filled, 1)

            def product_at(c, **kw):
                product(c, c % 2, landed(c), c_half=c // 2, **kw)

            def norm_in(name, count):
                for b in range(TB):
                    pe.wait_ge(normed, TB * count + b + 1)
                    for half in range(2):
                        turn(TR[name] + 2 * b + half, [xn[:, b, (4 * half + i) * P:(4 * half + i + 1) * P] for i in range(4)])
                for n in range(2, 4):
                    tr_ready(TR[name] + n)

            norm_in("norm1", 0)
            product_at(0)
            product_at(1, width=256)
            for b in range(TB):
                pe.wait_ge(g_free[b], 1)
            for n in range(4):
                b, four = n // 2, n % 2
                turn(TR["q_att"] + n, [proj[:, b, AQ + (4 * four + i) * HD:AQ + (4 * four + i + 1) * HD] for i in range(4)], rows=HD)
            for b in range(TB):
                pe.wait_ge(g_free[2 + b], 1)
            turn(TR["k_att"], [proj[:, b, AK + g * HD:AK + (g + 1) * HD] for g in range(KV_HEADS) for b in range(TB)], rows=HD)
            for n in range(4):
                tr_ready(TR["q_att"] + n)
            tr_ready(TR["k_att"])

            def scores(name, keys):
                for n, (b, h0, hn) in enumerate(SCORE_JOBS):
                    bank, w = mm_bank(MM[name] + n), (b + 1) * P
                    for h in range(hn):
                        last = nc.tensor.matmul(bank[:, h * w:(h + 1) * w], qT[:, h0 + h, b * P:(b + 1) * P], keys(h0 + h)[:, 0:w],
                                                start=True, stop=True)
                    last.then_inc(mm_filled, 1)

            scores("s_att", lambda h: kT[:, h // GROUP, :])
            with pe.Fori(0, 5) as i:
                for j in range(2):
                    product(None, j, i * 16 + 32, c_half=i + 1)

            def mix_values(p_name, o_name, first, values):
                for n, (b, h0, hn) in enumerate(SCORE_JOBS):
                    if n in (0, 2):
                        pe.wait_ge(probs_ready, first + b + 1)
                    turn(TR[p_name] + n, [probs_of[b][:, h0 + h, kb * P:(kb + 1) * P] for h in range(hn) for kb in range(b + 1)])
                for b in range(TB):
                    for n in ((0, 1), (2, 3, 4, 5))[b]:
                        tr_ready(TR[p_name] + n)
                    bank = mm_bank(MM[o_name] + b)
                    for h in range(HEADS):
                        for kb in range(b + 1):
                            last = nc.tensor.matmul(bank[:, h * HD:(h + 1) * HD], probs_t[:, (h if b == 0 else 8 + 2 * h + kb), :],
                                                    values(kb, h), start=(kb == 0), stop=(kb == b))
                    last.then_inc(mm_filled, 1)

            mix_values("p_att", "o_att", 0, lambda kb, h: proj[:, kb, AV + (h // GROUP) * HD:AV + (h // GROUP + 1) * HD])
            for b in range(TB):
                mm_ready(MM["o_att"] + b)
                turn(TR["att"] + b, [proj[:, b, i * P:(i + 1) * P] for i in range(4)])

            for j in range(2):
                for b in range(TB):
                    pe.wait_ge(g_free[2 * j + b], 3)
            for h in range(RH):
                turn(TR["ret_qk"] + h, [proj[:, b, at + h * RK:at + (h + 1) * RK] for at in (RQ, RKO) for b in range(TB)])
            for h in range(RH):
                tr_ready(TR["ret_qk"] + h)
                bank = mm_bank(MM["ret_s"] + h)
                for c in range(TB):
                    last = nc.tensor.matmul(bank[:, c * P:(c + 1) * P], ret_qk[:, h, 1, c * P:(c + 1) * P], ret_qk[:, h, 0, c * P:(c + 1) * P],
                                            start=True, stop=True)
                last.then_inc(mm_filled, 1)
            pe.wait_ge(ret_kd_ready, RH)
            for n in range(2):
                bank = mm_bank(MM["ret_state"] + n)
                for i in range(2):
                    h = 2 * n + i
                    last = nc.tensor.matmul(bank[:, i * RV:(i + 1) * RV], proj[:, 0, RKO + h * RK:RKO + (h + 1) * RK],
                                            proj[:, 0, RVO + h * RV:RVO + (h + 1) * RV], start=True, stop=True)
                last.then_inc(mm_filled, 1)
            for n in range(2):
                mm_ready(MM["ret_state"] + n)
            pe.wait_ge(ret_qd_ready, RH)
            for h in range(RH):
                mm_ready(MM["ret_s"] + h)
                bank = mm_bank(MM["ret_o"] + h)
                for c in range(TB):
                    last = nc.tensor.matmul(bank[:, c * RV:(c + 1) * RV], ret_s[:, h, c, :], proj[:, c, RVO + h * RV:RVO + (h + 1) * RV],
                                            start=True, stop=(c == 0))
                last = nc.tensor.matmul(bank[:, RV:2 * RV], ret_qk[:, h, 0, P:2 * P], state[:, h, :], start=False, stop=True)
                last.then_inc(mm_filled, 1)
            for b in range(TB):
                tr_ready(TR["att"] + b)
            for n in range(2):
                product_at(C_ATT + n, lhs=attT, k_tiles=4)
            for b in range(TB):
                pe.wait_ge(ret_ready, b + 1)
                for half in range(2):
                    turn(TR["ret"] + 2 * b + half, [proj[:, b, RVO + (4 * half + i) * P:RVO + (4 * half + i + 1) * P] for i in range(4)])
            for n in range(4):
                tr_ready(TR["ret"] + n)
            for n in range(2):
                product_at(C_RET + n, lhs=retT)
            for b in range(TB):
                pe.wait_ge(merged_ready, b + 1)
                for half in range(2):
                    turn(TR["merged"] + 2 * b + half, [proj[:, b, GA + (4 * half + i) * P:GA + (4 * half + i + 1) * P] for i in range(4)])
            for n in range(4):
                tr_ready(TR["merged"] + n)
            for n in range(2):
                product_at(C_OUT + n, lhs=mergedT)

            norm_in("norm2", 1)
            n_ff = TR["ff"]

            def ff_turn(f, par, first=False):
                p = (n_ff + par) % 2
                for b in range(TB):
                    pe.wait_ge(g_free[2 * par + b], (C_FF // 2 + 1) + f // 2 if isinstance(f, int) else f)
                return p

            def ff_turn_into(p, par):
                for fk in range(2):
                    for b in range(TB):
                        at = fk * S + b * P
                        last = nc.tensor.transpose(trb[p][:, at:at + P], ff_rows[:, par, b, fk * P:(fk + 1) * P], ident[:])
                last.then_inc(tr_filled, 1)

            def ff_rows_turned(i, par):
                p = (n_ff + par) % 2
                for b in range(TB):
                    pe.wait_ge(g_free[2 * par + b], i + (C_FF // 2 + 1))
                pe.wait_ge(tr_out[p], i + (n_ff + par) // 2)
                ff_turn_into(p, par)

            product_at(C_FF)
            with pe.Fori(0, 5) as i:
                product(None, 1, i * 32 + landed(C_FF + 1), c_half=i + (C_FF + 1) // 2)
                ff_rows_turned(i, 0)
                product(None, 0, i * 32 + landed(C_FF + 2), c_half=i + (C_FF + 2) // 2)
                ff_rows_turned(i, 1)
            ff_rows_turned(5, 0)
            for n in range(9, 11):
                tr_ready(n_ff + n)
            for p in range(4):
                pe.wait_ge(g_free[p], (C_DOWN - (1 if p < 2 else 2)) // 2 + 1)

            def down(par, landed_at, k0, first=False, last_one=False):
                w = wslot[par][:, 0:2 * D].rearrange("p (k n) -> p k n", k=2)
                pe.wait_ge(w_landed[par], landed_at)
                for b in range(TB):
                    for k in range(2):
                        for n in range(2):
                            last = nc.tensor.matmul(gemm[2 * n + b][:], ffT[:, k0 + k, b * P:(b + 1) * P], w[:, k, n * CHUNK:(n + 1) * CHUNK],
                                                    start=(first and k == 0), stop=(last_one and k == 1))
                    last.then_inc(g_filled, 1)

            for f in range(N_FF):
                c = C_DOWN + f
                down(c % 2, landed(c), 2 * f, first=(f == 0), last_one=(f == N_FF - 1))

            norm_in("norm3", 2)
            with pe.Fori(0, 2) as i:
                for j in range(2):
                    product(None, j, i * 16 + landed(C_IN2 + j), c_half=i + (C_IN2 + j) // 2)
            product_at(C_IN2 + 4)
            pe.wait_ge(gate_v_ready, TB)
            for b in range(TB):
                bank = mm_bank(MM["gate"] + b)
                for g in range(8):
                    last = nc.tensor.matmul(bank[:, g * HD:(g + 1) * HD], ws_t[:, g, :], proj2[:, b, HALF + g * HD:HALF + (g + 1) * HD],
                                            start=True, stop=True)
                last.then_inc(mm_filled, 1)
            for n in range(8):
                b, is_k, four = n // 4, (n // 2) % 2, n % 2
                if n % 4 == 0:
                    pe.wait_ge(qk_normed, b + 1)
                at = D + HALF * is_k + 4 * four * HD
                turn(TR["qk_band"] + n, [proj2[:, b, at + i * HD:at + (i + 1) * HD] for i in range(4)], rows=HD)
            for n in range(6, 8):
                tr_ready(TR["qk_band"] + n)
            scores("s_band", lambda h: kT2[:, h, :])
            for b in range(TB):
                pe.wait_ge(g_free[b], (C_IN2 + 4) // 2 + 1)
            mix_values("p_band", "o_band", 2, lambda kb, h: proj2[:, kb, 2 * D + h * HD:2 * D + (h + 1) * HD])
            for b in range(TB):
                mm_ready(MM["o_band"] + b)
                pe.wait_ge(mixed_a_ready, b + 1)
                for half in range(2):
                    turn(TR["mixed"] + 2 * b + half, [proj2[:, b, D * half + i * P:D * half + (i + 1) * P] for i in range(4)])
            for n in range(4):
                tr_ready(TR["mixed"] + n)
            for n in range(2):
                product_at(C_OUT2 + n)
            norm_in("norm4", 3)
            for n in range(4):
                product_at(C_QUERY + n)
            for n in range(8):
                b, four = n // 4, n % 4
                c = C_QUERY + four
                pe.wait_ge(g_free[2 * (c % 2) + b], c // 2 + 1)
                turn(TR["query"] + n, [qp[:, b, (4 * four + i) * P:(4 * four + i + 1) * P] for i in range(4)])
            for n in range(8):
                b, four = n // 4, n % 4
                tr_ready(TR["query"] + n)
                bank = mm_bank(MM["peer_s"] + n)
                for i in range(4):
                    last = nc.tensor.matmul(bank[:, i * P:(i + 1) * P], qpT[:, 4 * four + i, b * P:(b + 1) * P], keys_t[:, 4 * four + i, :],
                                            start=True, stop=True)
                last.then_inc(mm_filled, 1)

            for c in range(2):
                for b in range(TB):
                    pe.wait_ge(g_free[2 * c + b], (C_END - 1 - (1 - c if (C_END - 1) % 2 else c)) // 2 + 1)
            for b in range(TB):
                for n in range(2):
                    nc.tensor.matmul(gemm[2 * b + n][:], zeros[:], x_sb[:, b, n * CHUNK:(n + 1) * CHUNK], start=True, stop=False)
                with pe.Fori(0, PEER_HEADS) as i:
                    for k in range(TOPK):
                        pe.wait_ge(diag_ready, i * TOPK + (b * PEER_HEADS * TOPK + k + 1))
                        pe.wait_ge(v_landed[k % RING], i * 32 + (b * PEER_HEADS * 32 + 16 * (k // RING + 1)))
                        for n in range(2):
                            last = nc.tensor.matmul(gemm[2 * b + n][:], diag[k % 4][:], v_ring[k % RING][:, n * CHUNK:(n + 1) * CHUNK],
                                                    start=False, stop=False)
                        last.then_inc(v_free, 1)
                for n in range(2):
                    last = nc.tensor.matmul(gemm[2 * b + n][:], ident[:], x_sb[:, b, n * CHUNK:(n + 1) * CHUNK], start=False, stop=True)
                last.then_inc(peer_summed, 1)


NAMES = ["x", "norm_mix", "w_in", "att_sinks", "ret_gn_gain", "w_att_o", "w_ret_o", "w_out", "norm_ffn", "w_gate", "w_up", "w_down",
         "final_norm", "ln_mix_g_2", "w_in_2", "gmlp_norm_g_2", "gmlp_w_s_2", "gmlp_b_s_2", "q_norm_g_2", "k_norm_g_2", "rel_bias_2",
         "w_out_2", "ln_ffn_g_2", "peer_w_query_2", "peer_sub_keys_2", "peer_u_2", "peer_v_2"]


def kernel(**inputs):
    import numpy as np
    import concourse.bacc as bacc
    from concourse.bass_utils import run_bass_kernel_spmd

    nc = bacc.Bacc("TRN2", target_bir_lowering=False, num_devices=1)
    arrays, args = {}, []
    for name in NAMES:
        a = np.ascontiguousarray(inputs[name])
        arrays[f"in_{name}"] = a
        args.append(nc.dram_tensor(f"in_{name}", a.shape, mybir.dt.from_np(a.dtype), kind="ExternalInput").ap())
    out = nc.dram_tensor("out", inputs["x"].shape, mybir.dt.float32, kind="ExternalOutput").ap()
    two_block_kernel(nc, *args, out)
    result = run_bass_kernel_spmd(nc, [arrays], core_ids=[0])
    return result.results[0]["out"]
```

```python
import math
from contextlib import ExitStack

import concourse.bass as bass
from concourse import mybir


def two_block_kernel(
    nc, x, norm_mix, w_in, att_sinks, ret_gn_gain, w_att_o, w_ret_o, w_out, norm_ffn, w_gate, w_up, w_down,
    final_norm, ln_mix_g_2, w_in_2, gmlp_norm_g_2, gmlp_w_s_2, gmlp_b_s_2, q_norm_g_2, k_norm_g_2, rel_bias_2,
    w_out_2, ln_ffn_g_2, peer_w_query_2, peer_sub_keys_2, peer_u_2, peer_v_2, out,
):
    f32, f32r, u32 = mybir.dt.float32, mybir.dt.float32r, mybir.dt.uint32
    ALU, ACT, AX = mybir.AluOpType, mybir.ActivationFunctionType, mybir.AxisListType
    ds = bass.ds

    P = 128
    S, D = x.shape[1], x.shape[2]
    TB = S // P
    KD = D // P
    EPS = 1e-6
    MASKED = -1e30
    HEADS, KV_HEADS, HD = 8, 2, 64
    GROUP = HEADS // KV_HEADS
    RH, RK, RV = 4, 128, 256
    FF = w_gate.shape[2]
    IN2 = w_in_2.shape[2]
    HALF = D // 2
    NKEYS, TOPK, PEER_HEADS = 128, 16, 8
    HP = 2 * PEER_HEADS
    REL = rel_bias_2.shape[2]
    CHUNK = 512

    AQ, AK, AV, RQ, RKO, RVO = 0, 512, 640, 768, 1280, 1792
    RG, GA, GR = 2816, 3840, 4864
    IN1 = w_in.shape[2]

    slopes = [2.0 ** (-8.0 * (h + 1) / HEADS) for h in range(HEADS)]
    log_decay = [math.log(1.0 - 2.0 ** (-5.0 - h)) for h in range(RH)]
    RET_SCALE = RK ** -0.5
    HD_SCALE = HD ** -0.5

    C_IN, C_ATT, C_RET, C_OUT, C_FF, C_DOWN, C_IN2, C_OUT2, C_QUERY, C_END = 0, 12, 14, 16, 18, 29, 40, 45, 47, 51
    N_FF = FF // 256
    assert N_FF == C_DOWN - C_FF == C_IN2 - C_DOWN

    def numbered(*groups):
        at, first = 0, {}
        for name, count in groups:
            first[name] = at
            at += count
        return first

    TR = numbered(("norm1", 4), ("gains", 1), ("ws", 2), ("q_att", 4), ("k_att", 1), ("ret_qk", 4), ("p_att", 6),
                  ("att", 2), ("ret", 4), ("merged", 4), ("norm2", 4), ("ff", 11), ("keys", 4), ("norm3", 4),
                  ("qk_band", 8), ("p_band", 6), ("mixed", 4), ("norm4", 4), ("query", 8))
    SPLIT = numbered(("norm1", 4), ("att", 2), ("ret", 4), ("merged", 4), ("norm2", 4), ("ff", 11), ("norm3", 4), ("mixed", 4), ("norm4", 4))
    MM = numbered(("s_att", 6), ("ret_s", 4), ("o_att", 2), ("ret_state", 2), ("ret_o", 4),
                  ("s_band", 6), ("gate", 2), ("o_band", 2), ("peer_s", 8))
    RS = numbered(("norm1", 2), ("ret", 1), ("norm2", 2), ("final", 2), ("norm3", 2), ("band", 1), ("gate", 1), ("norm4", 2))
    NORM = numbered(("norm1", 1), ("norm2", 1), ("norm3", 1), ("norm4", 1))
    SCORE_JOBS = [(0, 0, 4), (0, 4, 4), (1, 0, 2), (1, 2, 2), (1, 4, 2), (1, 6, 2)]
    G_RET, G_BS, G_Q, G_K, G_ROWS = 0, 8, 16, 17, 18

    RING = 8

    ctx = ExitStack()
    with ctx:
        def sb(name, shape, dt=f32):
            return ctx.enter_context(nc.sbuf_tensor(name, shape, dt))

        def sem(name):
            return ctx.enter_context(nc.semaphore(name))

        RAW, BIG, ARENA = 4 * 2048, TB * IN1, 11776
        AT_RAW = 0
        AT_BIG = AT_RAW + RAW
        AT_ARENA = AT_BIG + BIG
        SLAB = AT_ARENA + ARENA
        slab_at = nc.sbuf_base + (-nc.sbuf_base) % 32
        ctx.enter_context(nc.sbuf_tensor("slab", [P, SLAB], f32))

        def at(name, offset, shape, dt=f32):
            return nc.alloc_sbuf_tensor_at(name, shape, dt, offset=slab_at + 4 * offset)

        x_sb = sb("x_sb", [P, TB, D])
        xn = sb("xn", [P, TB, D])
        hT = [sb("hT_hi", [P, KD, S], f32r), sb("hT_lo", [P, KD, S], f32r)]
        w_split = [sb("w_hi", [P, 4, 1024], f32r), sb("w_lo", [P, 4, 1024], f32r)]
        raw = at("raw", AT_RAW, [P, 2, 2, 2048])
        v_ring = at("v_ring", AT_RAW, [P, RING, D])
        proj = at("proj", AT_BIG, [P, TB, IN1])
        mix_row = at("mix_row", AT_BIG, [P, D])
        proj2 = at("proj2", AT_BIG, [P, TB, IN2])
        raw_keys = at("raw_keys", AT_BIG, [P, HP, P])
        ffn_row = at("ffn_row", AT_BIG + 2048, [P, D])
        mix2_row = at("mix2_row", AT_BIG + 3072, [P, D])
        rel_toep = at("rel_toep", AT_BIG + TB * IN2, [P, HEADS, 256])
        final_row = at("final_row", AT_BIG + 7168, [P, D])
        u_ring = at("u_ring", AT_BIG, [P, RING, D])
        gate_row = at("gate_row", AT_BIG + 8192, [P, HALF])
        peer_row = at("peer_row", AT_BIG + 8704, [P, D])
        keys_t = at("keys_t", AT_BIG + 9728, [P, HP, P])
        raw_ws = at("raw_ws", AT_ARENA, [P, 8, P])
        probs_of = [at("probs0", AT_ARENA, [P, HEADS, P])[:], at("probs1", AT_ARENA + 1024, [P, HEADS, 2 * P])[:]]
        probs_t = at("probs_t", AT_ARENA + 3072, [P, 24, P])
        qT = at("qT", AT_ARENA + 6144, [HD, HEADS, S])
        kT = at("kT", AT_ARENA + 8192, [HD, KV_HEADS, S])
        ret_qk = at("ret_qk", AT_ARENA + 8704, [P, RH, 2, S])
        attT = [at("attT_hi", AT_ARENA + 10752, [P, 4, S], f32r), at("attT_lo", AT_ARENA, [P, 4, S], f32r)]
        ret_s = xn[:, 0, :].rearrange("p (h c i) -> p h c i", h=RH, c=TB)
        state = xn[:, 1, :].rearrange("p (h v) -> p h v", h=RH)
        ffT = [at("ffT_hi", AT_ARENA, [P, 22, S], f32r), at("ffT_lo", AT_ARENA + 22 * S, [P, 22, S], f32r)]
        ff_rows = xn[:, 0, :].rearrange("p (a b n) -> p a b n", a=2, b=TB)
        ff_silu = xn[:, 1, :].rearrange("p (a b n) -> p a b n", a=2, b=TB)
        kT2 = at("kT2", AT_ARENA + 8192, [HD, HEADS, S])
        sq = at("sq", AT_ARENA + 10240, [P, D])
        qp = at("qp", AT_ARENA, [P, 2, TB, CHUNK])
        qpT = at("qpT", AT_ARENA + 2048, [P, 2, 4, S])
        peer_sc = at("peer_sc", AT_ARENA + 4096, [P, TB * PEER_HEADS, 2 * P])
        ident = sb("ident", [P, P])
        zeros = sb("zeros", [P, P])
        gain_rows = sb("gain_rows", [G_ROWS, P])
        gains = sb("gains", [P, G_ROWS])
        neg_dist = sb("neg_dist", [P, 2 * P])
        age = sb("age", [P, P])
        q_pos = sb("q_pos", [P, P])
        k_age = sb("k_age", [P, 1])
        decay_t = sb("decay_t", [P, RH, P])
        decay_q = sb("decay_q", [P, RH, P])
        decay_k = sb("decay_k", [P, RH])
        sinks = sb("sinks", [P, HEADS])
        iota16 = sb("iota16", [P, TOPK])
        ws_t = sb("ws_t", [P, 8, P])
        rel_ext = sb("rel_ext", [HEADS, 512])
        rel_dram = nc.dram_tensor("rel_ext_dram", [HEADS, 512], f32)
        ss = sb("ss", [P, 32])
        var = sb("var", [P, 32])
        sd = sb("sd", [P, 32])
        rstd = sb("rstd", [P, 32])
        newton = sb("newton", [P, 32])
        mx = sb("mx", [P, TB, HEADS])
        neg_mx = sb("neg_mx", [P, TB, HEADS])
        sink_e = sb("sink_e", [P, TB, HEADS])
        den = sb("den", [P, TB, HEADS])
        bn = sb("bn", [P, TB * RH, 6])
        mv = sb("mv", [P, TB * RH, 2])
        T = AT_ARENA + 8192
        tk_work = at("tk_work", T, [P, 2 * P])
        tk_rest = at("tk_rest", T + 256, [P, 2 * P])
        cand = at("cand", T + 512, [P, TOPK * TOPK])
        cand_rest = at("cand_rest", T + 768, [P, TOPK * TOPK])
        hit = at("hit", T + 1024, [P, TOPK, TOPK])
        expert = at("expert", T + 1280, [P, TB * PEER_HEADS, TOPK], u32)
        diag = [at(f"diag{i}", T + 1536 + 128 * i, [P, P]) for i in range(4)]
        tk_top = sb("tk_top", [P, 2, TOPK])
        tk_ix = sb("tk_ix", [P, 2, TOPK], u32)
        tk_ixf = sb("tk_ixf", [P, 2, TOPK])
        best = [sb(f"best{i}", [P, TOPK]) for i in range(2)]
        pos = sb("pos", [P, TOPK], u32)
        pos_ij = sb("pos_ij", [P, 2, TOPK], u32)
        pos_f = sb("pos_f", [P, 2, TOPK])
        picked = sb("picked", [P, 2, TOPK])
        eidx_f = sb("eidx_f", [P, TOPK])
        neg_best = [sb(f"neg_best{i}", [P, 1]) for i in range(2)]
        g_exp = [sb(f"g_exp{i}", [P, TOPK]) for i in range(2)]
        g_sum = [sb(f"g_sum{i}", [P, 1]) for i in range(2)]
        g_inv = sb("g_inv", [P, 1])
        ix_now = [sb(f"ix_now{i}", [P, TOPK], u32) for i in range(2)]
        hid = [sb(f"hid{i}", [P, TOPK]) for i in range(2)]
        hid_g = [sb(f"hid_g{i}", [P, TOPK]) for i in range(2)]
        wgt = [sb(f"wgt{i}", [P, TOPK]) for i in range(2)]

        gemm = [ctx.enter_context(nc.psum_tensor(f"gemm{i}", [P, CHUNK], f32)) for i in range(4)]
        trb = [ctx.enter_context(nc.psum_tensor(f"trb{i}", [P, CHUNK], f32)) for i in range(2)]
        mmb = [ctx.enter_context(nc.psum_tensor(f"mmb{i}", [P, CHUNK], f32)) for i in range(2)]

        x_landed, gains_landed, aux_landed, sinks_landed = sem("x_landed"), sem("gains_landed"), sem("aux_landed"), sem("sinks_landed")
        mix_landed, ffn_landed, late_landed = sem("mix_landed"), sem("ffn_landed"), sem("late_landed")
        w_landed = [[sem(f"w_landed{p}{h}") for h in range(2)] for p in range(2)]
        hi_ready, lo_ready = sem("hi_ready"), sem("lo_ready")
        w_used = sem("w_used")
        g_filled = [sem("g_filled0"), sem("g_filled1")]
        g_free = [sem(f"g_free{i}") for i in range(4)]
        tr_hi = sem("tr_hi")
        tr_filled = sem("tr_filled")
        tr_out = [sem("tr_out0"), sem("tr_out1")]
        mm_filled = sem("mm_filled")
        mm_out = [sem("mm_out0"), sem("mm_out1")]
        consts_made, decay_made, decay_masked, gains_zeroed = sem("consts_made"), sem("decay_made"), sem("decay_masked"), sem("gains_zeroed")
        var_ready, sd_ready = sem("var_ready"), sem("sd_ready")
        normed = sem("normed")
        squared = sem("squared")
        final_ready = sem("final_ready")
        max_ready, exp_done, probs_ready = sem("max_ready"), sem("exp_done"), sem("probs_ready")
        sink_ready = sem("sink_ready")
        ret_kd_ready, ret_qd_ready, ret_ready = sem("ret_kd_ready"), sem("ret_qd_ready"), sem("ret_ready")
        merged_ready, ff_silu_ready, ff_ready = sem("merged_ready"), sem("ff_silu_ready"), sem("ff_ready")
        gate_v_ready, mixed_a_ready, qk_normed = sem("gate_v_ready"), sem("mixed_a_ready"), sem("qk_normed")
        rel_filled, rel_stored, rel_loaded, rel_ready = sem("rel_filled"), sem("rel_stored"), sem("rel_loaded"), sem("rel_ready")
        expert_ready, best_ready, gexp_done = sem("expert_ready"), sem("best_ready"), sem("gexp_done")
        u_free, v_free = sem("u_free"), sem("v_free")
        u_landed = [sem(f"u_landed{i}") for i in range(RING)]
        v_landed = [sem(f"v_landed{i}") for i in range(RING)]
        gelu_done, wgt_ready, diag_ready = sem("gelu_done"), sem("wgt_ready"), sem("diag_ready")
        peer_summed, out_ready, stored = sem("peer_summed"), sem("out_ready"), sem("stored")
        pool_held, dve_held = sem("pool_held"), sem("dve_held")
        dve_step, act_step, pool_step = sem("dve_step"), sem("act_step"), sem("pool_step")

        class Steps:

            def __init__(self, engine, own):
                self.engine, self.own, self.n = engine, own, 0

            def put(self, ins):
                ins.then_inc(self.own, 1)
                self.n = self.n + 1

            def settle(self):
                self.engine.wait_ge(self.own, self.n)

            def link(self, ins):
                self.put(ins)
                self.settle()

            def enter(self, i, per, first=0):
                self.before = self.n
                self.n = self.n + (i - first) * per if first else self.n + i * per

            def leave(self, trips, per):
                self.n = self.before + trips * per

        block = ctx.enter_context(nc.Block())

        def landed(c):
            ffn_so_far = len([k for k in range(C_FF, C_DOWN) if k % 2 == c % 2 and k <= c])
            return 16 * (c // 2 + 1) + 16 * ffn_so_far

        IN2_COLS = [D, D + CHUNK, 2 * D, HALF, 0]

        @block.sync
        def _(sp):
            for b in range(TB):
                sp.dma_start(x_sb[:, b, :], x[0, b * P:(b + 1) * P, :]).then_inc(x_landed, 16)

            def half_free(c, half):
                if not (isinstance(c, int) and c < 2):
                    sp.wait_ge(lo_ready, (c - 2) * 4 + (2 * half + 2))

            def load(c, par, w, at, k_tiles=KD, width=CHUNK):
                kh = k_tiles // 2
                for half in range(2):
                    half_free(c, half)
                    sp.dma_start(raw[:, par, half, 0:kh * width].rearrange("p (k n) -> p k n", k=kh),
                                 w.rearrange("(k p) n -> p k n", p=P)[:, half * kh:(half + 1) * kh, ds(at, width)]).then_inc(w_landed[par][half], 16)

            def load_ff(c, par, at):
                for half in range(2):
                    half_free(c, half)
                    dst = raw[:, par, half, :].rearrange("p (k n) -> p k n", k=KD // 2)
                    for off, w in ((0, w_gate[0]), (256, w_up[0])):
                        sp.dma_start(dst[:, :, off:off + 256], w.rearrange("(k p) n -> p k n", p=P)[:, half * 4:half * 4 + 4, ds(at, 256)]
                                     ).then_inc(w_landed[par][half], 16)

            def load_down(c, par, kk):
                for half in range(2):
                    half_free(c, half)
                    sp.dma_start(raw[:, par, half, 0:D].unsqueeze(1),
                                 w_down[0].rearrange("(k p) n -> p k n", p=P)[:, ds(kk + half, 1), :]).then_inc(w_landed[par][half], 16)

            load(0, 0, w_in[0], 0)
            load(1, 1, w_in[0], AK, width=256)
            with sp.Fori(0, 5) as i:
                for j in range(2):
                    load(i * 2 + (2 + j), j, w_in[0], i * (2 * CHUNK) + (RQ + j * CHUNK))
            for n in range(2):
                load(C_ATT + n, n, w_att_o[0], n * CHUNK, k_tiles=4)
            for n in range(2):
                load(C_RET + n, n, w_ret_o[0], n * CHUNK)
            for n in range(2):
                load(C_OUT + n, n, w_out[0], n * CHUNK)
            with sp.Fori(0, 5) as i:
                for j in range(2):
                    load_ff(i * 2 + (C_FF + j), j, i * 512 + 256 * j)
            load_ff(C_FF + 10, 0, 10 * 256)
            load_down(C_DOWN, 1, 0)
            with sp.Fori(0, 5) as i:
                for j in range(2):
                    load_down(i * 2 + (C_DOWN + 1 + j), j, i * 4 + (2 + 2 * j))
            for n in range(5):
                load(C_IN2 + n, n % 2, w_in_2[0], IN2_COLS[n])
            for n in range(2):
                load(C_OUT2 + n, (C_OUT2 + n) % 2, w_out_2[0], n * CHUNK)
            for n in range(4):
                load(C_QUERY + n, (C_QUERY + n) % 2, peer_w_query_2[0], n * CHUNK)
            for b in range(TB):
                sp.wait_ge(out_ready, b + 1)
                sp.dma_start(out[0, b * P:(b + 1) * P, :], xn[:, b, :]).then_inc(stored, 16)
            sp.wait_ge(stored, 16 * TB)

        @block.gpsimd
        def _(pool):
            me = Steps(pool, pool_step)
            me.put(nc.gpsimd.memset(ident[:], 0.0))
            nc.gpsimd.memset(zeros[:], 0.0).then_inc(consts_made, 1)
            nc.gpsimd.iota(age[:], pattern=[[1, P]], base=0, channel_multiplier=-1, allow_small_or_imprecise_dtypes=True).then_inc(consts_made, 1)
            nc.gpsimd.iota(q_pos[:], pattern=[[1, P]], base=1, channel_multiplier=0, allow_small_or_imprecise_dtypes=True).then_inc(consts_made, 1)
            nc.gpsimd.iota(k_age[:], pattern=[[0, 1]], base=P - 1, channel_multiplier=-1, allow_small_or_imprecise_dtypes=True).then_inc(consts_made, 1)
            nc.gpsimd.iota(iota16[:], pattern=[[1, TOPK]], base=0, channel_multiplier=0, allow_small_or_imprecise_dtypes=True).then_inc(consts_made, 1)
            me.put(nc.gpsimd.iota(neg_dist[:], pattern=[[1, 2 * P]], base=-P, channel_multiplier=-1, allow_small_or_imprecise_dtypes=True))
            me.settle()
            nc.gpsimd.affine_select(out=ident[:], in_=ident[:], compare_op=ALU.not_equal, fill=1.0, base=0,
                                    pattern=[[-1, P]], channel_multiplier=1).then_inc(consts_made, 1)
            me.link(nc.gpsimd.affine_select(out=neg_dist[:], in_=neg_dist[:], compare_op=ALU.is_ge, fill=MASKED, base=P,
                                            pattern=[[-1, 2 * P]], channel_multiplier=1))
            nc.gpsimd.affine_select(out=neg_dist[:], in_=neg_dist[:], compare_op=ALU.is_gt, fill=MASKED, base=0,
                                    pattern=[[1, 2 * P]], channel_multiplier=-1).then_inc(consts_made, 1)
            pool.wait_ge(decay_made, RH)
            nc.gpsimd.affine_select(out=decay_t[:], in_=decay_t[:], compare_op=ALU.is_ge, fill=0.0, base=0,
                                    pattern=[[0, RH], [1, P]], channel_multiplier=-1).then_inc(decay_masked, 1)
            pool.wait_ge(rel_filled, 1)
            pool.dma_start(rel_dram[:], rel_ext[:]).then_inc(rel_stored, 16)
            pool.wait_ge(rel_stored, 16)
            pool.wait_ge(tr_filled, TR["merged"] + 4)
            pool.dma_start(ffn_row[:], norm_ffn[0].partition_broadcast(P)).then_inc(ffn_landed, 16)
            pool.dma_start(raw_keys[:], peer_sub_keys_2[0].rearrange("h a k d -> k (h a) d")).then_inc(late_landed, 16)
            pool.dma_start(rel_toep[:], bass.AP(tensor=rel_dram, offset=P, ap=[[1, P], [512, HEADS], [1, 256]])).then_inc(late_landed, 16)
            for dst, src in ((final_row, final_norm), (mix2_row, ln_mix_g_2[0]), (gate_row, gmlp_norm_g_2[0]), (peer_row, ln_ffn_g_2[0])):
                pool.dma_start(dst[:], src.partition_broadcast(P)).then_inc(late_landed, 16)

            def gather(n, par):
                pool.wait_ge(expert_ready, n + 1)
                me.link(nc.gpsimd.tensor_copy(ix_now[par][:], expert[:, ds(n, 1), :].rearrange("p a k -> p (a k)")))
                for table, ring, free, there in ((peer_u_2, u_ring, u_free, u_landed), (peer_v_2, v_ring, v_free, v_landed)):
                    for k in range(TOPK):
                        pool.wait_ge(free, n * TOPK + (k + 1))
                        pool.sem_inc(pool_held, 1)
                        nc.gpsimd.indirect_dma_start(
                            out=ring[:, k % RING, :], out_offset=None, in_=table[0],
                            in_offset=bass.IndirectOffsetOnAxis(ap=ix_now[par][:, k:k + 1], axis=0),
                        ).then_inc(there[k % RING], 16)

            with pool.Fori(0, TB * PEER_HEADS // 2) as i:
                me.enter(i, 2)
                for par in range(2):
                    gather(i * 2 + par, par)
            me.leave(TB * PEER_HEADS // 2, 2)

        @block.scalar
        def _(act):
            act.dma_start(mix_row[:], norm_mix[0].partition_broadcast(P)).then_inc(mix_landed, 16)
            act.wait_ge(gains_zeroed, 1)
            act.dma_start(gain_rows[G_RET:G_RET + 8, :], ret_gn_gain[0].rearrange("(k p) -> k p", p=P)).then_inc(gains_landed, 16)
            act.dma_start(gain_rows[G_BS:G_BS + 8, :], gmlp_b_s_2[0]).then_inc(gains_landed, 16)
            act.dma_start(gain_rows[G_Q:G_Q + 1, 0:HD], q_norm_g_2).then_inc(gains_landed, 16)
            act.dma_start(gain_rows[G_K:G_K + 1, 0:HD], k_norm_g_2).then_inc(gains_landed, 16)
            act.dma_start(raw_ws[:], gmlp_w_s_2[0].rearrange("g i j -> i g j")).then_inc(aux_landed, 16)
            act.dma_start(rel_ext[:, 127:127 + REL], rel_bias_2[0]).then_inc(rel_loaded, 16)
            act.dma_start(sinks[:], att_sinks[0].partition_broadcast(P)).then_inc(sinks_landed, 16)

            def hi(prev, par, landed_at, n=1024, quarters=range(4)):
                for q in quarters:
                    if q % 2 == 0:
                        act.wait_ge(w_landed[par][q // 2], landed_at)
                    if prev is not None:
                        if q < 3:
                            act.wait_ge(w_used, prev * 3 + (q + 1))
                        else:
                            act.wait_ge(g_filled[1], prev + 1)
                    nc.scalar.activation(w_split[0][:, q, 0:n], raw[:, par, q // 2, (q % 2) * n:(q % 2 + 1) * n], ACT.Copy).then_inc(hi_ready, 1)

            def hi_at(c, **kw):
                hi(c - 1, c % 2, landed(c), **kw)

            def squares(name, half, ready, width=CHUNK, src=x_sb, scale=D ** -0.5):
                for b in range(TB):
                    ready(b)
                    nc.scalar.activation(xn[:, b, half * CHUNK:(half + 1) * CHUNK], x_sb[:, b, half * CHUNK:(half + 1) * CHUNK], ACT.Square,
                                         scale=scale, accum_out=ss[:, 2 * b + half:2 * b + half + 1]).then_inc(squared, 1)

            def residual_in(c):
                return lambda b: act.wait_ge(g_free[2 * (c % 2) + b], c // 2 + 1)

            def roots(name):
                for b in range(TB):
                    act.wait_ge(var_ready, RS[name] + b + 1)
                    nc.scalar.activation(sd[:, b:b + 1], var[:, b:b + 1], ACT.Sqrt).then_inc(sd_ready, 1)

            def root(name, width):
                act.wait_ge(var_ready, RS[name] + 1)
                nc.scalar.activation(sd[:, 0:width], var[:, 0:width], ACT.Sqrt).then_inc(sd_ready, 1)

            def chunk_out(c, par, dst, func=ACT.Copy, scale=1.0, width=CHUNK):
                for b in range(TB):
                    act.wait_ge(g_filled[b], c + 1)
                    nc.scalar.activation(dst(b), gemm[2 * par + b][:, 0:width], func, scale=scale).then_inc(g_free[2 * par + b], 1)

            def softmax_exp(first):
                for b in range(TB):
                    act.wait_ge(max_ready, first + b + 1)
                    for h in range(HEADS):
                        nc.scalar.activation(probs_of[b][:, h, :], probs_of[b][:, h, :], ACT.Exp, bias=neg_mx[:, b, h:h + 1],
                                             accum_out=den[:, b, h:h + 1]).then_inc(exp_done, 1)

            def tr_out_copy(n, dst, rows=P, scale=1.0, tiles=4):
                act.wait_ge(tr_filled, n + 1)
                nc.scalar.activation(dst, trb[n % 2][0:rows, :].rearrange("p (k t) -> p k t", k=tiles), ACT.Copy, scale=scale).then_inc(tr_out[n % 2], 1)

            def mm_out_copy(n, dst):
                act.wait_ge(mm_filled, n + 1)
                nc.scalar.activation(dst, mmb[n % 2][:], ACT.Copy).then_inc(mm_out[n % 2], 1)

            def hi_columns(name, jobs=range(4), dst=hT[0], gain=None):
                for n in jobs:
                    half, b = n // 2, n % 2
                    t = TR[name] + n
                    act.wait_ge(tr_filled, t + 1)
                    if gain is None:
                        nc.scalar.activation(dst[:, 4 * half:4 * half + 4, b * P:(b + 1) * P],
                                             trb[t % 2][:].rearrange("p (k t) -> p k t", k=4), ACT.Copy).then_inc(tr_hi, 1)
                    else:
                        for k in range(4):
                            ins = nc.scalar.activation(dst[:, 4 * half + k, b * P:(b + 1) * P], trb[t % 2][:, k * P:(k + 1) * P], ACT.Copy,
                                                       scale=gains[:, gain + 4 * half + k:gain + 4 * half + k + 1])
                        ins.then_inc(tr_hi, 1)

            act.wait_ge(consts_made, 7)
            for h in range(RH):
                nc.scalar.activation(decay_q[:, h, :], q_pos[:], ACT.Exp, scale=log_decay[h])
                nc.scalar.activation(decay_k[:, h:h + 1], k_age[:], ACT.Exp, scale=log_decay[h])
                nc.scalar.activation(decay_t[:, h, :], age[:], ACT.Exp, scale=log_decay[h]).then_inc(decay_made, 1)
            nc.scalar.preload_act_table(ACT.Sqrt)

            for half in range(2):
                squares("norm1", half, lambda b: act.wait_ge(x_landed, 16 * (b + 1) if b else 32))
            roots("norm1")
            hi(None, 0, landed(0), quarters=(0, 1))
            hi_columns("norm1", (0, 1))
            hi(None, 0, landed(0), quarters=(2, 3))
            hi_columns("norm1", (2, 3))
            hi_at(1, n=512)
            chunk_out(0, 0, lambda b: proj[:, b, AQ:AQ + CHUNK], scale=HD_SCALE)
            hi_at(2)
            chunk_out(1, 1, lambda b: proj[:, b, AK:AK + 256], width=256)
            hi_at(3)
            chunk_out(2, 0, lambda b: proj[:, b, RQ:RQ + CHUNK])
            softmax_exp(0)
            act.wait_ge(sink_ready, 1)
            nc.scalar.activation(sink_e[:], sink_e[:], ACT.Exp).then_inc(exp_done, 1)
            for c in (3, 4, 5):
                hi_at(c + 1)
                chunk_out(c, c % 2, lambda b: proj[:, b, RQ + (c - 2) * CHUNK:RQ + (c - 1) * CHUNK])
            for n in range(6):
                tr_out_copy(TR["p_att"] + n, probs_t[:, 4 * n:4 * n + 4, :])
            hi_at(7)
            chunk_out(6, 0, lambda b: proj[:, b, RG:RG + CHUNK], ACT.Silu)
            for b in range(TB):
                mm_out_copy(MM["o_att"] + b, proj[:, b, AQ:AQ + CHUNK])
            for h in range(2):
                mm_out_copy(MM["ret_state"] + h, state[:, 2 * h:2 * h + 2, :].rearrange("p h v -> p (h v)"))
            hi_at(8)
            chunk_out(7, 1, lambda b: proj[:, b, RG + CHUNK:RG + 2 * CHUNK], ACT.Silu)
            for b in range(TB):
                t = TR["att"] + b
                act.wait_ge(tr_filled, t + 1)
                nc.scalar.activation(attT[0][:, :, b * P:(b + 1) * P], trb[t % 2][:].rearrange("p (k t) -> p k t", k=4), ACT.Copy).then_inc(tr_hi, 1)
            root("ret", TB * RH)
            for c in (8, 9, 10, 11):
                hi_at(c + 1, n=(1024 if c + 1 < C_ATT else 512))
                chunk_out(c, c % 2, lambda b: proj[:, b, GA + (c - 8) * CHUNK:GA + (c - 7) * CHUNK], ACT.Sigmoid)
            hi_columns("ret", gain=G_RET)
            nc.scalar.preload_act_table(ACT.Sqrt)
            hi_at(13, n=512)
            hi_at(14)
            hi_at(15)
            hi_columns("merged", (0, 1))
            hi_at(16)
            hi_columns("merged", (2, 3))
            hi_at(17)
            squares("norm2", 0, residual_in(C_OUT))
            hi_at(18)
            squares("norm2", 1, residual_in(C_OUT + 1))
            roots("norm2")
            hi_columns("norm2")
            nc.scalar.preload_act_table(ACT.Silu)

            def ff_gate(c, par):
                for b in range(TB):
                    act.wait_ge(g_filled[b], c + 1)
                    nc.scalar.activation(ff_silu[:, par, b, :], gemm[2 * par + b][:, 0:256], ACT.Silu).then_inc(ff_silu_ready, 1)

            def ff_hi(f, par):
                p = (TR["ff"] + par) % 2
                act.wait_ge(tr_filled, f + (TR["ff"] + 1))
                nc.scalar.activation(ffT[0][:, ds(f * 2, 2), :].rearrange("p k t -> p (k t)"), trb[p][:], ACT.Copy).then_inc(tr_hi, 1)

            hi_at(C_FF + 1)
            ff_gate(C_FF, 0)
            with act.Fori(0, 4) as i:
                for j in range(2):
                    hi(i * 2 + (C_FF + 1 + j), j, i * 32 + landed(C_FF + 2 + j))
                    ff_gate(i * 2 + (C_FF + 1 + j), 1 - j)
                    ff_hi(i * 2 + j, j)
            hi_at(C_FF + 10)
            ff_gate(C_FF + 9, 1)
            ff_hi(8, 0)
            hi_at(C_DOWN, n=512)
            ff_gate(C_FF + 10, 0)
            ff_hi(9, 1)
            hi_at(C_DOWN + 1, n=512)
            ff_hi(10, 0)
            nc.scalar.preload_act_table(ACT.Sqrt)
            for n in range(2, 4):
                hi_at(C_DOWN + n, n=512)
            for n in range(4):
                tr_out_copy(TR["keys"] + n, keys_t[:, 4 * n:4 * n + 4, :])
            with act.Fori(0, 3) as i:
                for j in range(2):
                    hi(i * 2 + (C_DOWN + 3 + j), (C_DOWN + 4 + j) % 2, i * 16 + landed(C_DOWN + 4 + j), n=512)
            hi_at(C_DOWN + 10, n=512)
            hi_at(C_IN2)
            for half in range(2):
                squares("final", half, lambda b: act.wait_ge(g_free[2 * half + b], (C_IN2 - 2 + half) // 2 + 1))
            roots("final")

            for half in range(2):
                squares("norm3", half, lambda b: act.wait_ge(final_ready, 2 * half + b + 1))
            roots("norm3")
            hi_columns("norm3")
            for n in range(3):
                hi_at(C_IN2 + n + 1)
                chunk_out(C_IN2 + n, n % 2, lambda b: proj2[:, b, IN2_COLS[n]:IN2_COLS[n] + CHUNK])
                if n == 1:
                    root("band", 32)
            for n in range(8):
                b, is_k, four = n // 4, (n // 2) % 2, n % 2
                if is_k:
                    tr_out_copy(TR["qk_band"] + n, kT2[:, 4 * four:4 * four + 4, b * P:(b + 1) * P], rows=HD, scale=gains[0:HD, G_K:G_K + 1])
            hi_at(C_IN2 + 4)
            softmax_exp(2)
            chunk_out(C_IN2 + 3, 1, lambda b: proj2[:, b, HALF:D], ACT.Gelu_apprx_tanh)
            for b in range(TB):
                act.wait_ge(g_free[2 + b], (C_IN2 + 3) // 2 + 1)
                nc.scalar.activation(xn[:, b, 0:HALF], proj2[:, b, HALF:D], ACT.Square, accum_out=ss[:, b:b + 1]).then_inc(squared, 1)
            root("gate", TB)
            nc.scalar.preload_act_table(ACT.Gelu_apprx_tanh)
            hi_at(C_OUT2)
            chunk_out(C_IN2 + 4, 0, lambda b: proj2[:, b, 0:HALF], ACT.Gelu_apprx_tanh)
            for n in range(6):
                tr_out_copy(TR["p_band"] + n, probs_t[:, 4 * n:4 * n + 4, :])
            for b in range(TB):
                mm_out_copy(MM["o_band"] + b, proj2[:, b, D:D + HALF])
            hi_columns("mixed")
            nc.scalar.preload_act_table(ACT.Sqrt)
            hi_at(C_OUT2 + 1)
            squares("norm4", 0, residual_in(C_OUT2))
            hi_at(C_QUERY)
            squares("norm4", 1, residual_in(C_OUT2 + 1))
            roots("norm4")
            hi_columns("norm4")
            for n in range(4):
                c = C_QUERY + n
                if n < 3:
                    hi_at(c + 1)
                chunk_out(c, c % 2, lambda b: qp[:, n % 2, b, :])
                for b in range(TB):
                    tr_out_copy(TR["query"] + 2 * n + b, qpT[:, n % 2, :, b * P:(b + 1) * P])
                for b in range(TB):
                    at = b * PEER_HEADS + 2 * n
                    mm_out_copy(MM["peer_s"] + 2 * n + b, peer_sc[:, at:at + 2, :].rearrange("p n k -> p (n k)"))

            def weigh(n, par):
                act.wait_ge(best_ready, n + 1)
                nc.scalar.activation(g_exp[par][:], best[par][:], ACT.Exp, bias=neg_best[par][:], accum_out=g_sum[par][:]).then_inc(gexp_done, 1)
                act.wait_ge(u_free, n * TOPK + (RING + TOPK))
                nc.scalar.activation(hid_g[par][:], hid[par][:], ACT.Gelu_apprx_tanh).then_inc(gelu_done, 1)
                act.wait_ge(wgt_ready, n + 1)
                for k in range(TOPK):
                    act.wait_ge(v_free, n * TOPK + (RING + k - 3))
                    nc.scalar.activation(diag[k % 4][:], ident[:], ACT.Copy, scale=wgt[par][:, k:k + 1]).then_inc(diag_ready, 1)

            with act.Fori(0, TB * PEER_HEADS // 2) as i:
                for par in range(2):
                    weigh(i * 2 + par, par)

        @block.vector
        def _(dve):
            me = Steps(dve, dve_step)
            V = nc.vector
            V.memset(gain_rows[:], 0.0).then_inc(gains_zeroed, 1)

            def lo(prev, par, n=1024, quarters=range(4)):
                for q in quarters:
                    dve.wait_ge(hi_ready, prev * 4 + (q + 5) if prev is not None else q + 1)
                    V.tensor_tensor(w_split[1][:, q, 0:n], raw[:, par, q // 2, (q % 2) * n:(q % 2 + 1) * n],
                                    w_split[0][:, q, 0:n].bitcast(f32), ALU.subtract).then_inc(lo_ready, 1)

            def lo_at(c, **kw):
                lo(c - 1, c % 2, **kw)

            def lo_columns(name, jobs=range(4), gain=None):
                for n in jobs:
                    half, b = n // 2, n % 2
                    t = TR[name] + n
                    dve.wait_ge(tr_hi, SPLIT[name] + n + 1)
                    if gain is None:
                        V.tensor_tensor(hT[1][:, 4 * half:4 * half + 4, b * P:(b + 1) * P], trb[t % 2][:].rearrange("p (k t) -> p k t", k=4),
                                        hT[0][:, 4 * half:4 * half + 4, b * P:(b + 1) * P].bitcast(f32), ALU.subtract).then_inc(tr_out[t % 2], 1)
                    else:
                        for k in range(4):
                            g = gain + 4 * half + k
                            ins = V.scalar_tensor_tensor(out=hT[1][:, 4 * half + k, b * P:(b + 1) * P], in0=trb[t % 2][:, k * P:(k + 1) * P],
                                                         scalar=gains[:, g:g + 1], in1=hT[0][:, 4 * half + k, b * P:(b + 1) * P].bitcast(f32),
                                                         op0=ALU.mult, op1=ALU.subtract)
                        ins.then_inc(tr_out[t % 2], 1)

            def copy_out_tr(n, dst, src):
                dve.wait_ge(tr_filled, n + 1)
                V.tensor_copy(dst, src).then_inc(tr_out[n % 2], 1)

            def inverse_root(at, width, job):
                dve.wait_ge(sd_ready, job + 1)
                r, t, v = rstd[:, at:at + width], newton[:, at:at + width], var[:, at:at + width]
                me.link(V.reciprocal(r, sd[:, at:at + width]))
                if width == 1:
                    me.link(V.tensor_scalar(t, r, r, v, ALU.mult, ALU.mult))
                else:
                    me.link(V.tensor_tensor(t, r, r, ALU.mult))
                    me.link(V.tensor_tensor(t, t, v, ALU.mult))
                me.link(V.tensor_scalar(t, t, -0.5, 1.5, ALU.mult, ALU.add))
                me.link(V.tensor_tensor(r, r, t, ALU.mult))

            SQUARES = numbered(("norm1", 4), ("norm2", 4), ("final", 4), ("norm3", 4), ("gate", 2), ("norm4", 4))

            def row_norm(name, row, write):
                def rows(half, b):
                    cols = slice(half * CHUNK, (half + 1) * CHUNK)
                    dst, done = write
                    V.scalar_tensor_tensor(out=dst[:, b, cols], in0=x_sb[:, b, cols], scalar=rstd[:, b:b + 1], in1=row[:, cols],
                                           op0=ALU.mult, op1=ALU.mult).then_inc(done, 1)
                for b in range(TB):
                    dve.wait_ge(squared, SQUARES[name] + 3 + b)
                    V.tensor_scalar(var[:, b:b + 1], ss[:, 2 * b:2 * b + 1], ss[:, 2 * b + 1:2 * b + 2], EPS, ALU.add, ALU.add).then_inc(var_ready, 1)
                for b in range(TB):
                    inverse_root(b, 1, RS[name] + b)
                    rows(0, b)
                for b in range(TB):
                    rows(1, b)

            dve.wait_ge(x_landed, 32)
            dve.wait_ge(mix_landed, 16)
            row_norm("norm1", mix_row, (xn, normed))
            lo(None, 0, quarters=(0,))
            lo_columns("norm1", (0, 1))
            lo(None, 0, quarters=(1, 2, 3))
            lo_columns("norm1", (2, 3))
            lo_at(1, n=512)
            dve.wait_ge(tr_filled, TR["gains"] + 1)
            V.tensor_copy(gains[:], trb[TR["gains"] % 2][:, 0:G_ROWS]).then_inc(tr_out[TR["gains"] % 2], 1)
            dve.wait_ge(tr_out[TR["gains"] % 2], TR["gains"] // 2 + 1)
            for n in range(2):
                t = TR["ws"] + n
                dve.wait_ge(tr_filled, t + 1)
                me.link(V.tensor_copy(ws_t[:, 4 * n:4 * n + 4, :].rearrange("p g i -> p (g i)"), trb[t % 2][:]))
                V.memset(ws_t[64:P, 4 * n:4 * n + 4, 0:64], 0.0).then_inc(tr_out[t % 2], 1)
            dve.wait_ge(rel_loaded, 16)
            me.put(V.tensor_copy(rel_ext[:, 0:127], rel_ext[:, 127:128].to_broadcast([HEADS, 127])))
            V.tensor_copy(rel_ext[:, 127 + REL:512], rel_ext[:, 126 + REL:127 + REL].to_broadcast([HEADS, 512 - 127 - REL])).then_inc(rel_filled, 1)
            lo_at(2)

            for n in range(4):
                b, four = n // 2, n % 2
                t = TR["q_att"] + n
                copy_out_tr(t, qT[:, 4 * four:4 * four + 4, b * P:(b + 1) * P], trb[t % 2][0:HD, :].rearrange("p (h t) -> p h t", h=4))
            t = TR["k_att"]
            copy_out_tr(t, kT[:].rearrange("p h t -> p (h t)"), trb[t % 2][0:HD, :])

            def finish_softmax():
                for b in range(TB):
                    w = (b + 1) * P
                    V.tensor_tensor(probs_of[b], probs_of[b], den[:, b, :].unsqueeze(2).to_broadcast([P, HEADS, w]),
                                    ALU.mult).then_inc(probs_ready, 1)

            dve.wait_ge(consts_made, 7)
            dve.wait_ge(sinks_landed, 16)
            for n, (b, h0, hn) in enumerate(SCORE_JOBS):
                m, w = MM["s_att"] + n, (b + 1) * P
                dve.wait_ge(mm_filled, m + 1)
                for h in range(hn):
                    ins = V.scalar_tensor_tensor(out=probs_of[b][:, h0 + h, :], in0=neg_dist[:, 2 * P - w:2 * P], scalar=slopes[h0 + h],
                                                 in1=mmb[m % 2][:, h * w:(h + 1) * w], op0=ALU.mult, op1=ALU.add)
                    if h < hn - 1:
                        me.put(ins)
                    else:
                        ins.then_inc(mm_out[m % 2], 1)
            for p in range(2):
                dve.wait_ge(mm_out[p], (MM["s_att"] + 6) // 2)
            for b in range(TB):
                me.link(V.tensor_reduce(mx[:, b, :], probs_of[b], axis=AX.X, op=ALU.max))
                me.link(V.tensor_tensor(mx[:, b, :], mx[:, b, :], sinks[:], ALU.max))
                V.tensor_scalar(neg_mx[:, b, :], mx[:, b, :], -1.0, None, ALU.mult).then_inc(max_ready, 1)
            for b in range(TB):
                ins = V.tensor_tensor(sink_e[:, b, :], sinks[:], mx[:, b, :], ALU.subtract)
                if b < TB - 1:
                    me.put(ins)
            ins.then_inc(sink_ready, 1)
            lo_at(3)
            dve.wait_ge(exp_done, TB * HEADS + 1)
            me.link(V.tensor_tensor(den[:], den[:], sink_e[:], ALU.add))
            me.link(V.reciprocal(den[:], den[:]))
            finish_softmax()
            for c in (4, 5, 6):
                lo_at(c)

            dve.wait_ge(decay_masked, 1)
            for b in range(TB):
                dve.wait_ge(g_free[2 + b], 2)
            for h in range(RH):
                k_cols = proj[:, 0, RKO + h * RK:RKO + (h + 1) * RK]
                t = TR["ret_qk"] + h
                copy_out_tr(t, ret_qk[:, h, :, :].rearrange("p a t -> p (a t)"), trb[t % 2][:])
                V.tensor_scalar(k_cols, k_cols, decay_k[:, h:h + 1], RET_SCALE, ALU.mult, ALU.mult).then_inc(ret_kd_ready, 1)
            lo_at(7)
            for h in range(RH):
                m = MM["ret_s"] + h
                dve.wait_ge(mm_filled, m + 1)
                for c in range(TB):
                    ins = V.scalar_tensor_tensor(out=ret_s[:, h, c, :], in0=mmb[m % 2][:, c * P:(c + 1) * P], scalar=RET_SCALE,
                                                 in1=decay_t[:, h, :], op0=ALU.mult, op1=ALU.mult)
                    if c < TB - 1:
                        me.put(ins)
                ins.then_inc(mm_out[m % 2], 1)
                q2 = ret_qk[:, h, 0, P:2 * P]
                V.tensor_tensor(q2, q2, decay_q[:, h, :], ALU.mult).then_inc(ret_qd_ready, 1)
            lo_at(8)
            for h in range(RH):
                m = MM["ret_o"] + h
                dve.wait_ge(mm_filled, m + 1)
                for c in range(TB):
                    me.put(V.bn_stats(bn[:, 2 * h + c, :], mmb[m % 2][:, c * RV:(c + 1) * RV]))
                V.tensor_copy(proj[:, :, RVO + h * RV:RVO + (h + 1) * RV], mmb[m % 2][:].rearrange("p (c v) -> p c v", c=TB)).then_inc(mm_out[m % 2], 1)
            for b in range(TB):
                t = TR["att"] + b
                dve.wait_ge(tr_hi, SPLIT["att"] + b + 1)
                V.tensor_tensor(attT[1][:, :, b * P:(b + 1) * P], trb[t % 2][:].rearrange("p (k t) -> p k t", k=4),
                                attT[0][:, :, b * P:(b + 1) * P].bitcast(f32), ALU.subtract).then_inc(tr_out[t % 2], 1)
            me.settle()
            for n in range(TB * RH):
                me.put(V.bn_aggr(mv[:, n, :], bn[:, n, :]))
            me.settle()
            V.tensor_scalar(var[:, 0:TB * RH], mv[:, :, 1], EPS, None, ALU.add).then_inc(var_ready, 1)
            lo_at(9)
            inverse_root(0, TB * RH, RS["ret"])
            for p in range(2):
                dve.wait_ge(mm_out[p], (MM["ret_o"] + RH) // 2)
            for h in range(RH):
                for c in range(TB):
                    o = proj[:, c, RVO + h * RV:RVO + (h + 1) * RV]
                    n = 2 * h + c
                    me.put(V.tensor_scalar(o, o, mv[:, n, 0:1], rstd[:, n:n + 1], ALU.subtract, ALU.mult))
            lo_at(10)
            me.settle()
            for half in range(2):
                for b in range(TB):
                    dve.wait_ge(g_free[2 * half + b], 4)
                    o = proj[:, b, RVO + half * CHUNK:RVO + (half + 1) * CHUNK]
                    V.tensor_tensor(o, o, proj[:, b, RG + half * CHUNK:RG + (half + 1) * CHUNK], ALU.mult).then_inc(ret_ready, 1)
            lo_at(11)
            lo_at(12, n=512)
            lo_columns("ret", gain=G_RET)
            lo_at(13, n=512)
            for n in range(2):
                if n == 1:
                    lo_at(14)
                for b in range(TB):
                    dve.wait_ge(g_filled[b], C_ATT + n + 1)
                    dve.wait_ge(g_free[2 * n + b], 5)
                    ga = proj[:, b, GA + n * CHUNK:GA + (n + 1) * CHUNK]
                    V.tensor_tensor(ga, gemm[2 * n + b][:], ga, ALU.mult).then_inc(g_free[2 * n + b], 1)
            for n in range(2):
                lo_at(15 + n)
                for b in range(TB):
                    dve.wait_ge(g_filled[b], C_RET + n + 1)
                    gr = proj[:, b, GR + n * CHUNK:GR + (n + 1) * CHUNK]
                    V.tensor_tensor(gr, gemm[2 * n + b][:], gr, ALU.mult).then_inc(g_free[2 * n + b], 1)
                for b in range(TB):
                    dve.wait_ge(g_free[2 * n + b], (C_RET + n) // 2 + 1)
                    ga = proj[:, b, GA + n * CHUNK:GA + (n + 1) * CHUNK]
                    V.tensor_tensor(ga, ga, proj[:, b, GR + n * CHUNK:GR + (n + 1) * CHUNK], ALU.add).then_inc(merged_ready, 1)
                lo_columns("merged", (2 * n, 2 * n + 1))

            def residual(c, n):
                p = c % 2
                for b in range(TB):
                    dve.wait_ge(g_filled[b], c + 1)
                    xs = x_sb[:, b, n * CHUNK:(n + 1) * CHUNK]
                    V.tensor_tensor(xs, gemm[2 * p + b][:], xs, ALU.add).then_inc(g_free[2 * p + b], 1)

            for n in range(2):
                lo_at(17 + n)
                residual(C_OUT + n, n)
            for i in range(4):
                dve.wait_ge(g_free[i], C_OUT // 2 + 1)

            dve.wait_ge(ffn_landed, 16)
            row_norm("norm2", ffn_row, (xn, normed))
            lo_columns("norm2")

            def ff_up(c, par):
                for b in range(TB):
                    dve.wait_ge(ff_silu_ready, (c - C_FF) * 2 + (b + 1))
                    V.tensor_tensor(ff_rows[:, par, b, :], gemm[2 * par + b][:, 256:512], ff_silu[:, par, b, :], ALU.mult).then_inc(g_free[2 * par + b], 1)

            def ff_lo(f, par):
                p = (TR["ff"] + par) % 2
                dve.wait_ge(tr_hi, f + (SPLIT["ff"] + 1))
                V.tensor_tensor(ffT[1][:, ds(f * 2, 2), :].rearrange("p k t -> p (k t)"), trb[p][:],
                                ffT[0][:, ds(f * 2, 2), :].rearrange("p k t -> p (k t)").bitcast(f32), ALU.subtract).then_inc(tr_out[p], 1)

            lo_at(C_FF + 1)
            ff_up(C_FF, 0)
            with dve.Fori(0, 4) as i:
                for j in range(2):
                    lo(i * 2 + (C_FF + 1 + j), j)
                    ff_up(i * 2 + (C_FF + 1 + j), 1 - j)
                    ff_lo(i * 2 + j, j)
            lo_at(C_FF + 10)
            ff_up(C_FF + 9, 1)
            ff_lo(8, 0)
            lo_at(C_DOWN, n=512)
            ff_up(C_FF + 10, 0)
            ff_lo(9, 1)
            lo_at(C_DOWN + 1, n=512)
            ff_lo(10, 0)
            with dve.Fori(0, 4) as i:
                for j in range(2):
                    lo(i * 2 + (C_DOWN + 1 + j), (C_DOWN + 2 + j) % 2, n=512)
            lo_at(C_DOWN + 10, n=512)
            lo_at(C_IN2)
            for n in range(2):
                for b in range(TB):
                    dve.wait_ge(g_filled[b], C_IN2)
                    xs = x_sb[:, b, n * CHUNK:(n + 1) * CHUNK]
                    V.tensor_tensor(xs, gemm[2 * n + b][:], xs, ALU.add).then_inc(g_free[2 * n + b], len([c for c in range(C_DOWN, C_IN2) if c % 2 == n]))
            for n in range(2):
                for b in range(TB):
                    dve.wait_ge(g_free[2 * n + b], (C_IN2 - 2 + n) // 2 + 1)

            dve.wait_ge(late_landed, 6 * 16)
            row_norm("final", final_row, (x_sb, final_ready))
            dve.wait_ge(final_ready, 4)
            row_norm("norm3", mix2_row, (xn, normed))
            lo_columns("norm3")
            lo_at(C_IN2 + 1)
            lo_at(C_IN2 + 2)

            for n in range(2):
                for b in range(TB):
                    dve.wait_ge(g_free[2 * n + b], (C_IN2 + n) // 2 + 1)
            for b in range(TB):
                qk = proj2[:, b, D:2 * D]
                me.link(V.tensor_tensor(sq[:], qk, qk, ALU.mult))
                me.link(V.tensor_reduce(ss[:, 16 * b:16 * b + 16], sq[:].rearrange("p (h d) -> p h d", d=HD), axis=AX.X, op=ALU.add))
            V.tensor_scalar(var[:, 0:32], ss[:, 0:32], 1.0 / HD, EPS, ALU.mult, ALU.add).then_inc(var_ready, 1)
            inverse_root(0, 32, RS["band"])
            for b in range(TB):
                qk = proj2[:, b, D:2 * D].rearrange("p (h d) -> p h d", d=HD)
                V.tensor_tensor(qk, qk, rstd[:, 16 * b:16 * b + 16].unsqueeze(2).to_broadcast([P, 16, HD]), ALU.mult).then_inc(qk_normed, 1)
            lo_at(C_IN2 + 3)
            for n in range(8):
                b, is_k, four = n // 4, (n // 2) % 2, n % 2
                t = TR["qk_band"] + n
                if not is_k:
                    dve.wait_ge(tr_filled, t + 1)
                    V.tensor_scalar(qT[:, 4 * four:4 * four + 4, b * P:(b + 1) * P], trb[t % 2][0:HD, :].rearrange("p (h t) -> p h t", h=4),
                                    gains[0:HD, G_Q:G_Q + 1], HD_SCALE, ALU.mult, ALU.mult).then_inc(tr_out[t % 2], 1)
            for n, (b, h0, hn) in enumerate(SCORE_JOBS):
                m, w = MM["s_band"] + n, (b + 1) * P
                dve.wait_ge(mm_filled, m + 1)
                V.tensor_tensor(probs_of[b][:, h0:h0 + hn, :], mmb[m % 2][:].rearrange("p (h j) -> p h j", h=hn),
                                rel_toep[:, h0:h0 + hn, w - 1::-1] if w < 256 else rel_toep[:, h0:h0 + hn, ::-1], ALU.add).then_inc(mm_out[m % 2], 1)
            for p in range(2):
                dve.wait_ge(mm_out[p], (MM["s_band"] + 6) // 2)
            for b in range(TB):
                w = (b + 1) * P
                me.link(V.memset(probs_of[b][0:64, :, w - 64:w], MASKED))
                me.link(V.tensor_reduce(mx[:, b, :], probs_of[b], axis=AX.X, op=ALU.max))
                V.tensor_scalar(neg_mx[:, b, :], mx[:, b, :], -1.0, None, ALU.mult).then_inc(max_ready, 1)
            lo_at(C_IN2 + 4)
            dve.wait_ge(exp_done, 2 * TB * HEADS + 1)
            me.link(V.reciprocal(den[:], den[:]))
            finish_softmax()

            dve.wait_ge(squared, SQUARES["gate"] + 2)
            V.tensor_scalar(var[:, 0:TB], ss[:, 0:TB], 1.0 / HALF, EPS, ALU.mult, ALU.add).then_inc(var_ready, 1)
            inverse_root(0, TB, RS["gate"])
            for b in range(TB):
                V.scalar_tensor_tensor(out=proj2[:, b, HALF:D], in0=proj2[:, b, HALF:D], scalar=rstd[:, b:b + 1], in1=gate_row[:],
                                       op0=ALU.mult, op1=ALU.mult).then_inc(gate_v_ready, 1)
            lo_at(C_OUT2)
            for b in range(TB):
                m = MM["gate"] + b
                dve.wait_ge(mm_filled, m + 1)
                bank = mmb[m % 2][:].rearrange("p (g c) -> p g c", g=8)
                V.tensor_tensor(sq[:, b * HALF:(b + 1) * HALF].rearrange("p (g c) -> p g c", g=8), bank,
                                gains[:, G_BS:G_BS + 8].unsqueeze(2).to_broadcast([P, 8, HD]), ALU.add).then_inc(mm_out[m % 2], 1)
                dve.wait_ge(mm_out[m % 2], m // 2 + 1)
                dve.wait_ge(g_free[b], (C_IN2 + 4) // 2 + 1)
                V.tensor_tensor(proj2[:, b, 0:HALF], proj2[:, b, 0:HALF], sq[:, b * HALF:(b + 1) * HALF], ALU.mult).then_inc(mixed_a_ready, 1)
            lo_columns("mixed")
            for n in range(2):
                lo_at(C_OUT2 + n + 1)
                residual(C_OUT2 + n, n)
            for i in range(4):
                dve.wait_ge(g_free[i], (C_OUT2 + (i // 2 == 0)) // 2 + 1)

            row_norm("norm4", peer_row, (xn, normed))
            lo_columns("norm4")
            lo_at(C_QUERY + 1)
            lo_at(C_QUERY + 2)
            dve.sem_inc(u_free, RING)

            def top16(values, rest, top, ix):
                me.settle()
                dve.sem_inc(dve_held, 1)
                me.put(V.max(top[:, 0:8], values))
                me.settle()
                dve.sem_inc(dve_held, 1)
                me.put(V.max_index(ix[:, 0:8], top[:, 0:8], values))
                me.put(V.match_replace(rest, top[:, 0:8], values, -3.0e38))
                me.settle()
                dve.sem_inc(dve_held, 1)
                me.put(V.max(top[:, 8:16], rest))
                me.settle()
                dve.sem_inc(dve_held, 1)
                me.put(V.max_index(ix[:, 8:16], top[:, 8:16], rest))

            def select(n, par, scores):
                for bank, count in scores:
                    dve.wait_ge(mm_out[bank], MM["peer_s"] // 2 + count)
                me.put(V.tensor_copy(tk_work[:], peer_sc[:, ds(n, 1), :].rearrange("p a k -> p (a k)")))
                for a in range(2):
                    top16(tk_work[:, a * P:(a + 1) * P], tk_rest[:, a * P:(a + 1) * P], tk_top[:, a, :], tk_ix[:, a, :])
                me.settle()
                me.put(V.tensor_copy(tk_ixf[:], tk_ix[:]))
                me.put(V.tensor_tensor(cand[:].rearrange("p (i j) -> p i j", i=TOPK), tk_top[:, 0, :].unsqueeze(2).to_broadcast([P, TOPK, TOPK]),
                                        tk_top[:, 1, :].unsqueeze(1).to_broadcast([P, TOPK, TOPK]), ALU.add))
                top16(cand[:], cand_rest[:], best[par][:], pos[:])
                me.settle()
                V.tensor_scalar(neg_best[par][:], best[par][:, 0:1], -1.0, None, ALU.mult).then_inc(best_ready, 1)
                me.put(V.tensor_scalar(pos_ij[:, 0, :], pos[:], 4, None, ALU.logical_shift_right))
                me.link(V.tensor_scalar(pos_ij[:, 1, :], pos[:], TOPK - 1, None, ALU.bitwise_and))
                me.link(V.tensor_copy(pos_f[:], pos_ij[:]))
                for a in range(2):
                    me.link(V.tensor_tensor(hit[:], iota16[:].unsqueeze(1).to_broadcast([P, TOPK, TOPK]),
                                            pos_f[:, a, :].unsqueeze(2).to_broadcast([P, TOPK, TOPK]), ALU.is_equal))
                    me.link(V.tensor_tensor(hit[:], hit[:], tk_ixf[:, a, :].unsqueeze(1).to_broadcast([P, TOPK, TOPK]), ALU.mult))
                    me.link(V.tensor_reduce(picked[:, a, :], hit[:], axis=AX.X, op=ALU.add))
                me.link(V.scalar_tensor_tensor(out=eidx_f[:], in0=picked[:, 0, :], scalar=float(NKEYS), in1=picked[:, 1, :], op0=ALU.mult, op1=ALU.add))
                V.tensor_copy(expert[:, ds(n, 1), :].rearrange("p a k -> p (a k)"), eidx_f[:]).then_inc(expert_ready, 1)

            def hidden(n, par, b):
                for k in range(TOPK):
                    dve.wait_ge(u_landed[k % RING], n * 32 + 16 * (k // RING + 1))
                    V.tensor_tensor_reduce(out=u_ring[:, k % RING, :], in0=u_ring[:, k % RING, :], in1=xn[:, b, :], scale=1.0, scalar=0.0, op0=ALU.mult,
                                           op1=ALU.add, accum_out=hid[par][:, k:k + 1]).then_inc(u_free, 1)
                dve.wait_ge(gexp_done, n + 1)
                me.link(V.reciprocal(g_inv[:], g_sum[par][:]))
                dve.wait_ge(gelu_done, n + 1)
                V.scalar_tensor_tensor(out=wgt[par][:], in0=hid_g[par][:], scalar=g_inv[:], in1=g_exp[par][:], op0=ALU.mult, op1=ALU.mult).then_inc(wgt_ready, 1)

            steps = me.n
            select(0, 0, [(0, 1)])
            PER = me.n - steps + 1
            lo_at(C_QUERY + 3)
            dve.wait_ge(lo_ready, 4 * C_END)
            dve.sem_inc(v_free, RING)
            all_scores = [(0, 4), (1, 4)]
            with dve.Fori(0, 4) as i:
                me.enter(i, 2 * PER)
                for par in range(2):
                    select(i * 2 + (par + 1), 1 - par, all_scores if par else [])
                    hidden(i * 2 + par, par, 0)
            me.leave(4, 2 * PER)
            with dve.Fori(0, 3) as i:
                me.enter(i, 2 * PER)
                for par in range(2):
                    select(i * 2 + (par + 9), 1 - par, [])
                    hidden(i * 2 + (8 + par), par, 1)
            me.leave(3, 2 * PER)
            select(15, 1, [])
            hidden(14, 0, 1)
            hidden(15, 1, 1)
            for b in range(TB):
                dve.wait_ge(peer_summed, b + 1)
                if b == 0:
                    dve.wait_ge(u_free, RING + TB * PEER_HEADS * TOPK)
                for n in range(2):
                    ins = V.tensor_copy(xn[:, b, n * CHUNK:(n + 1) * CHUNK], gemm[2 * b + n][:])
                    if n == 0:
                        me.put(ins)
                ins.then_inc(out_ready, 1)

        @block.tensor
        def _(pe):
            def tr_bank(n):
                if n >= 2:
                    pe.wait_ge(tr_out[n % 2], n // 2)
                return trb[n % 2]

            def mm_bank(n):
                if n >= 2:
                    pe.wait_ge(mm_out[n % 2], n // 2)
                return mmb[n % 2]

            def tr_ready(n):
                pe.wait_ge(tr_out[n % 2], n // 2 + 1)

            def mm_ready(n):
                pe.wait_ge(mm_out[n % 2], n // 2 + 1)

            def turn(n, sources, rows=P):
                bank = tr_bank(n)
                for i, src in enumerate(sources):
                    last = nc.tensor.transpose(bank[0:rows, i * P:i * P + src.shape[0]], src, ident[0:src.shape[0], 0:src.shape[0]])
                last.then_inc(tr_filled, 1)

            def three(bank, act_k, w, b, first, last):
                cols = slice(b * P, (b + 1) * P)
                nc.tensor.matmul(bank, act_k[0][:, cols], w[0], start=first, stop=False)
                nc.tensor.matmul(bank, act_k[0][:, cols], w[1], start=False, stop=False)
                return nc.tensor.matmul(bank, act_k[1][:, cols], w[0], start=False, stop=last)

            def done(q, b, ins):
                if q == 3:
                    ins.then_inc(g_filled[b], 1)
                elif b == TB - 1:
                    ins.then_inc(w_used, 1)

            def product(c, par, free_at, lhs=hT, k_tiles=KD, width=CHUNK, before={}, ready=None):
                per = k_tiles // 4
                for q in range(4):
                    if q in before:
                        before[q]()
                    pe.wait_ge(lo_ready, c * 4 + (q + 1))
                    for b in range(TB):
                        if ready is not None:
                            ready(q, b)
                        if q == 0 and not (isinstance(free_at, int) and free_at == 0):
                            pe.wait_ge(g_free[2 * par + b], free_at)
                        for j in range(per):
                            k = q * per + j
                            last = three(gemm[2 * par + b][:, 0:width], [a[:, k, :] for a in lhs],
                                         [w[:, q, j * width:(j + 1) * width] for w in w_split], b, k == 0, k == k_tiles - 1)
                        done(q, b, last)

            def product_at(c, **kw):
                product(c, c % 2, c // 2, **kw)

            def columns(name, source, jobs):
                for n in jobs:
                    half, b = n // 2, n % 2
                    rows = source(n, half, b)
                    turn(TR[name] + n, [rows[:, i * P:(i + 1) * P] for i in range(4)])

            def columns_ready(name):
                def wait(q, b):
                    if q % 2 == 0:
                        tr_ready(TR[name] + q + b)
                return wait

            def product_of_norm(name, c, **kw):
                def rows(n, half, b):
                    pe.wait_ge(normed, 4 * NORM[name] + n + 1)
                    return xn[:, b, half * CHUNK:(half + 1) * CHUNK]
                product_at(c, before={0: lambda: columns(name, rows, (0, 1)), 1: lambda: columns(name, rows, (2, 3))}, ready=columns_ready(name), **kw)

            pe.wait_ge(consts_made, 7)
            product_of_norm("norm1", 0)
            pe.wait_ge(gains_landed, 4 * 16)
            turn(TR["gains"], [gain_rows[:]])
            pe.wait_ge(aux_landed, 16)
            for n in range(2):
                turn(TR["ws"] + n, [raw_ws[:, 4 * n + i, :] for i in range(4)])
            product_at(1, width=256)
            for b in range(TB):
                pe.wait_ge(g_free[b], 1)
            for n in range(4):
                b, four = n // 2, n % 2
                turn(TR["q_att"] + n, [proj[:, b, AQ + (4 * four + i) * HD:AQ + (4 * four + i + 1) * HD] for i in range(4)], rows=HD)
            for b in range(TB):
                pe.wait_ge(g_free[2 + b], 1)
            turn(TR["k_att"], [proj[:, b, AK + g * HD:AK + (g + 1) * HD] for g in range(KV_HEADS) for b in range(TB)], rows=HD)
            for n in range(4):
                tr_ready(TR["q_att"] + n)
            tr_ready(TR["k_att"])

            def scores(name, keys):
                for n, (b, h0, hn) in enumerate(SCORE_JOBS):
                    bank, w = mm_bank(MM[name] + n), (b + 1) * P
                    for h in range(hn):
                        last = nc.tensor.matmul(bank[:, h * w:(h + 1) * w], qT[:, h0 + h, b * P:(b + 1) * P], keys(h0 + h)[:, 0:w],
                                                start=True, stop=True)
                    last.then_inc(mm_filled, 1)

            scores("s_att", lambda h: kT[:, h // GROUP, :])
            with pe.Fori(0, 2) as i:
                for j in range(2):
                    product(i * 2 + (2 + j), j, i + 1)

            def turn_probs(p_name, first):
                for n, (b, h0, hn) in enumerate(SCORE_JOBS):
                    if n in (0, 2):
                        pe.wait_ge(probs_ready, first + b + 1)
                    turn(TR[p_name] + n, [probs_of[b][:, h0 + h, kb * P:(kb + 1) * P] for h in range(hn) for kb in range(b + 1)])

            def mix_values(p_name, o_name, values):
                for b in range(TB):
                    for n in ((0, 1), (2, 3, 4, 5))[b]:
                        tr_ready(TR[p_name] + n)
                    bank = mm_bank(MM[o_name] + b)
                    for h in range(HEADS):
                        for kb in range(b + 1):
                            last = nc.tensor.matmul(bank[:, h * HD:(h + 1) * HD], probs_t[:, (h if b == 0 else 8 + 2 * h + kb), :],
                                                    values(kb, h), start=(kb == 0), stop=(kb == b))
                    last.then_inc(mm_filled, 1)

            for j in range(2):
                for b in range(TB):
                    pe.wait_ge(g_free[2 * j + b], 3)
            for h in range(RH):
                turn(TR["ret_qk"] + h, [proj[:, b, at + h * RK:at + (h + 1) * RK] for at in (RQ, RKO) for b in range(TB)])
            turn_probs("p_att", 0)
            product_at(6)
            for h in range(RH):
                tr_ready(TR["ret_qk"] + h)
                bank = mm_bank(MM["ret_s"] + h)
                for c in range(TB):
                    last = nc.tensor.matmul(bank[:, c * P:(c + 1) * P], ret_qk[:, h, 1, c * P:(c + 1) * P], ret_qk[:, h, 0, c * P:(c + 1) * P],
                                            start=True, stop=True)
                last.then_inc(mm_filled, 1)
            mix_values("p_att", "o_att", lambda kb, h: proj[:, kb, AV + (h // GROUP) * HD:AV + (h // GROUP + 1) * HD])
            pe.wait_ge(ret_kd_ready, RH)
            for n in range(2):
                bank = mm_bank(MM["ret_state"] + n)
                for i in range(2):
                    h = 2 * n + i
                    last = nc.tensor.matmul(bank[:, i * RV:(i + 1) * RV], proj[:, 0, RKO + h * RK:RKO + (h + 1) * RK],
                                            proj[:, 0, RVO + h * RV:RVO + (h + 1) * RV], start=True, stop=True)
                last.then_inc(mm_filled, 1)
            product_at(7)
            for n in range(2):
                mm_ready(MM["ret_state"] + n)
            pe.wait_ge(ret_qd_ready, RH)
            for h in range(RH):
                mm_ready(MM["ret_s"] + h)
                bank = mm_bank(MM["ret_o"] + h)
                for c in range(TB):
                    last = nc.tensor.matmul(bank[:, c * RV:(c + 1) * RV], ret_s[:, h, c, :], proj[:, c, RVO + h * RV:RVO + (h + 1) * RV],
                                            start=True, stop=(c == 0))
                last = nc.tensor.matmul(bank[:, RV:2 * RV], ret_qk[:, h, 0, P:2 * P], state[:, h, :], start=False, stop=True)
                last.then_inc(mm_filled, 1)
            for b in range(TB):
                mm_ready(MM["o_att"] + b)
                turn(TR["att"] + b, [proj[:, b, i * P:(i + 1) * P] for i in range(4)])
            with pe.Fori(0, 2) as i:
                for j in range(2):
                    product(i * 2 + (8 + j), j, i + 4)

            def ret_rows(n, half, b):
                pe.wait_ge(ret_ready, n + 1)
                return proj[:, b, RVO + half * CHUNK:RVO + (half + 1) * CHUNK]

            def merged_rows(n, half, b):
                pe.wait_ge(merged_ready, n + 1)
                return proj[:, b, GA + half * CHUNK:GA + (half + 1) * CHUNK]

            for b in range(TB):
                tr_ready(TR["att"] + b)
            product_at(C_ATT, lhs=attT, k_tiles=4, before={0: lambda: columns("ret", ret_rows, (0, 1)), 2: lambda: columns("ret", ret_rows, (2, 3))})
            product_at(C_ATT + 1, lhs=attT, k_tiles=4)
            product_at(C_RET, ready=columns_ready("ret"))
            product_at(C_RET + 1, before={2: lambda: columns("merged", merged_rows, (0, 1))})
            product_at(C_OUT, before={0: lambda: columns("merged", merged_rows, (2, 3))}, ready=columns_ready("merged"))
            product_at(C_OUT + 1)

            n_ff = TR["ff"]

            def ff_rows_turned(i, par):
                p = (n_ff + par) % 2
                for b in range(TB):
                    pe.wait_ge(g_free[2 * par + b], i + (C_FF // 2 + 1))
                pe.wait_ge(tr_out[p], i + (n_ff + par) // 2)
                for fk in range(2):
                    for b in range(TB):
                        at = fk * S + b * P
                        last = nc.tensor.transpose(trb[p][:, at:at + P], ff_rows[:, par, b, fk * P:(fk + 1) * P], ident[:])
                last.then_inc(tr_filled, 1)

            product_of_norm("norm2", C_FF)
            with pe.Fori(0, 5) as i:
                product(i * 2 + (C_FF + 1), 1, i + (C_FF + 1) // 2)
                ff_rows_turned(i, 0)
                product(i * 2 + (C_FF + 2), 0, i + (C_FF + 2) // 2)
                ff_rows_turned(i, 1)

            for f in range(N_FF):
                c = C_DOWN + f
                for q in range(4):
                    k, n = q // 2, q % 2
                    pe.wait_ge(lo_ready, 4 * c + q + 1)
                    if q == 0:
                        tr_ready(n_ff + f)
                    for b in range(TB):
                        if f == 0 and k == 0:
                            pe.wait_ge(g_free[2 * n + b], C_DOWN // 2 + (1 - n))
                        last = three(gemm[2 * n + b][:], [a[:, 2 * f + k, :] for a in ffT], [w[:, q, 0:CHUNK] for w in w_split], b,
                                     f == 0 and k == 0, f == N_FF - 1 and k == 1)
                        done(q, b, last)
                if f == 0:
                    ff_rows_turned(5, 0)
                if f == 3:
                    pe.wait_ge(late_landed, 6 * 16)
                    for n in range(4):
                        turn(TR["keys"] + n, [raw_keys[:, 4 * n + i, :] for i in range(4)])

            product_of_norm("norm3", C_IN2)
            product_at(C_IN2 + 1)
            product_at(C_IN2 + 2)
            for n in range(8):
                b, is_k, four = n // 4, (n // 2) % 2, n % 2
                if n % 4 == 0:
                    pe.wait_ge(qk_normed, b + 1)
                at = D + HALF * is_k + 4 * four * HD
                turn(TR["qk_band"] + n, [proj2[:, b, at + i * HD:at + (i + 1) * HD] for i in range(4)], rows=HD)
            for n in range(6, 8):
                tr_ready(TR["qk_band"] + n)
            scores("s_band", lambda h: kT2[:, h, :])
            product_at(C_IN2 + 3)
            product_at(C_IN2 + 4)
            pe.wait_ge(gate_v_ready, TB)
            for b in range(TB):
                bank = mm_bank(MM["gate"] + b)
                for g in range(8):
                    last = nc.tensor.matmul(bank[:, g * HD:(g + 1) * HD], ws_t[:, g, :], proj2[:, b, HALF + g * HD:HALF + (g + 1) * HD],
                                            start=True, stop=True)
                last.then_inc(mm_filled, 1)
            turn_probs("p_band", 2)
            for b in range(TB):
                pe.wait_ge(g_free[b], (C_IN2 + 2) // 2 + 1)
            mix_values("p_band", "o_band", lambda kb, h: proj2[:, kb, 2 * D + h * HD:2 * D + (h + 1) * HD])

            def mixed_rows(n, half, b):
                if half == 0:
                    pe.wait_ge(mixed_a_ready, b + 1)
                else:
                    mm_ready(MM["o_band"] + b)
                return proj2[:, b, D * half:D * half + HALF]

            product_at(C_OUT2, before={0: lambda: columns("mixed", mixed_rows, (0, 1)), 1: lambda: columns("mixed", mixed_rows, (2, 3))},
                       ready=columns_ready("mixed"))
            product_at(C_OUT2 + 1)

            def turn_queries(n):
                c = C_QUERY + n
                for b in range(TB):
                    pe.wait_ge(g_free[2 * (c % 2) + b], c // 2 + 1)
                    turn(TR["query"] + 2 * n + b, [qp[:, n % 2, b, i * P:(i + 1) * P] for i in range(4)])

            def key_scores(n):
                for b in range(TB):
                    tr_ready(TR["query"] + 2 * n + b)
                    bank = mm_bank(MM["peer_s"] + 2 * n + b)
                    for i in range(4):
                        last = nc.tensor.matmul(bank[:, i * P:(i + 1) * P], qpT[:, n % 2, i, b * P:(b + 1) * P], keys_t[:, 4 * n + i, :],
                                                start=True, stop=True)
                    last.then_inc(mm_filled, 1)

            product_of_norm("norm4", C_QUERY)
            for n in range(3):
                product_at(C_QUERY + n + 1, before={1: lambda: turn_queries(n), 2: lambda: key_scores(n)})
            turn_queries(3)
            key_scores(3)

            for c in range(2):
                for b in range(TB):
                    pe.wait_ge(g_free[2 * c + b], (C_END - 1 - (1 - c if (C_END - 1) % 2 else c)) // 2 + 1)
            for b in range(TB):
                for n in range(2):
                    nc.tensor.matmul(gemm[2 * b + n][:], zeros[:], x_sb[:, b, n * CHUNK:(n + 1) * CHUNK], start=True, stop=False)
                with pe.Fori(0, PEER_HEADS) as i:
                    for k in range(TOPK):
                        pe.wait_ge(diag_ready, i * TOPK + (b * PEER_HEADS * TOPK + k + 1))
                        pe.wait_ge(v_landed[k % RING], i * 32 + (b * PEER_HEADS * 32 + 16 * (k // RING + 1)))
                        for n in range(2):
                            last = nc.tensor.matmul(gemm[2 * b + n][:], diag[k % 4][:], v_ring[:, k % RING, n * CHUNK:(n + 1) * CHUNK],
                                                    start=False, stop=False)
                        last.then_inc(v_free, 1)
                for n in range(2):
                    last = nc.tensor.matmul(gemm[2 * b + n][:], ident[:], x_sb[:, b, n * CHUNK:(n + 1) * CHUNK], start=False, stop=True)
                last.then_inc(peer_summed, 1)


NAMES = ["x", "norm_mix", "w_in", "att_sinks", "ret_gn_gain", "w_att_o", "w_ret_o", "w_out", "norm_ffn", "w_gate", "w_up", "w_down",
         "final_norm", "ln_mix_g_2", "w_in_2", "gmlp_norm_g_2", "gmlp_w_s_2", "gmlp_b_s_2", "q_norm_g_2", "k_norm_g_2", "rel_bias_2",
         "w_out_2", "ln_ffn_g_2", "peer_w_query_2", "peer_sub_keys_2", "peer_u_2", "peer_v_2"]


def kernel(**inputs):
    import numpy as np
    import concourse.bacc as bacc
    from concourse.bass_utils import run_bass_kernel_spmd

    nc = bacc.Bacc("TRN2", target_bir_lowering=False, num_devices=1)
    arrays, args = {}, []
    for name in NAMES:
        a = np.ascontiguousarray(inputs[name])
        arrays[f"in_{name}"] = a
        args.append(nc.dram_tensor(f"in_{name}", a.shape, mybir.dt.from_np(a.dtype), kind="ExternalInput").ap())
    out = nc.dram_tensor("out", inputs["x"].shape, mybir.dt.float32, kind="ExternalOutput").ap()
    two_block_kernel(nc, *args, out)
    result = run_bass_kernel_spmd(nc, [arrays], core_ids=[0])
    return result.results[0]["out"]
```

```python
import math
from contextlib import ExitStack

import concourse.bass as bass
from concourse import mybir


def two_block_kernel(
    nc, x, norm_mix, w_in, att_sinks, ret_gn_gain, w_att_o, w_ret_o, w_out, norm_ffn, w_gate, w_up, w_down,
    final_norm, ln_mix_g_2, w_in_2, gmlp_norm_g_2, gmlp_w_s_2, gmlp_b_s_2, q_norm_g_2, k_norm_g_2, rel_bias_2,
    w_out_2, ln_ffn_g_2, peer_w_query_2, peer_sub_keys_2, peer_u_2, peer_v_2, out,
):
    f32, f32r, u32 = mybir.dt.float32, mybir.dt.float32r, mybir.dt.uint32
    ALU, ACT, AX = mybir.AluOpType, mybir.ActivationFunctionType, mybir.AxisListType
    ds = bass.ds

    P = 128
    S, D = x.shape[1], x.shape[2]
    TB = S // P
    KD = D // P
    EPS = 1e-6
    MASKED = -1e30
    HEADS, KV_HEADS, HD = 8, 2, 64
    GROUP = HEADS // KV_HEADS
    RH, RK, RV = 4, 128, 256
    FF = w_gate.shape[2]
    IN2 = w_in_2.shape[2]
    HALF = D // 2
    NKEYS, TOPK, PEER_HEADS = 128, 16, 8
    HP = 2 * PEER_HEADS
    REL = rel_bias_2.shape[2]
    CHUNK = 512

    AQ, AK, AV, RQ, RKO, RVO = 0, 512, 640, 768, 1280, 1792
    RG, GA, GR = 2816, 3840, 4864
    IN1 = w_in.shape[2]

    slopes = [2.0 ** (-8.0 * (h + 1) / HEADS) for h in range(HEADS)]
    log_decay = [math.log(1.0 - 2.0 ** (-5.0 - h)) for h in range(RH)]
    RET_SCALE = RK ** -0.5
    HD_SCALE = HD ** -0.5

    C_IN, C_ATT, C_RET, C_OUT, C_FF, C_DOWN, C_IN2, C_OUT2, C_QUERY, C_END = 0, 12, 14, 16, 18, 29, 40, 45, 47, 51
    N_FF = FF // 256
    assert N_FF == C_DOWN - C_FF == C_IN2 - C_DOWN

    def numbered(*groups):
        at, first = 0, {}
        for name, count in groups:
            first[name] = at
            at += count
        return first

    TR = numbered(("norm1", 4), ("gains", 1), ("ws", 2), ("q_att", 4), ("k_att", 1), ("ret_qk", 4), ("p_att", 6),
                  ("att", 2), ("ret", 4), ("merged", 4), ("norm2", 4), ("ff", 11), ("keys", 4), ("norm3", 4),
                  ("qk_band", 8), ("p_band", 6), ("mixed", 4), ("norm4", 4), ("query", 8))
    SPLIT = numbered(("norm1", 4), ("att", 2), ("ret", 4), ("merged", 4), ("norm2", 4), ("ff", 11), ("norm3", 4), ("mixed", 4), ("norm4", 4))
    MM = numbered(("s_att", 6), ("ret_s", 4), ("o_att", 2), ("ret_state", 2), ("ret_o", 4),
                  ("s_band", 6), ("gate", 2), ("o_band", 2), ("peer_s", 8))
    RS = numbered(("norm1", 2), ("ret", 1), ("norm2", 2), ("final", 4), ("band", 1), ("gate", 1), ("norm4", 2))
    NORM = numbered(("norm1", 1), ("norm2", 1), ("norm3", 1), ("norm4", 1))
    SCORE_JOBS = [(0, 0, 4), (0, 4, 4), (1, 0, 2), (1, 2, 2), (1, 4, 2), (1, 6, 2)]
    G_RET, G_BS, G_Q, G_K, G_ROWS = 0, 8, 16, 17, 18

    PE_LAST = 11
    RING = 8

    ctx = ExitStack()
    with ctx:
        def sb(name, shape, dt=f32):
            return ctx.enter_context(nc.sbuf_tensor(name, shape, dt))

        def sem(name):
            return ctx.enter_context(nc.semaphore(name))

        RAW, BIG, ARENA = 4 * 2048, TB * IN1, 11776
        AT_RAW = 0
        AT_BIG = AT_RAW + RAW
        AT_ARENA = AT_BIG + BIG
        SLAB = AT_ARENA + ARENA
        slab_at = nc.sbuf_base + (-nc.sbuf_base) % 32
        ctx.enter_context(nc.sbuf_tensor("slab", [P, SLAB], f32))

        def at(name, offset, shape, dt=f32):
            return nc.alloc_sbuf_tensor_at(name, shape, dt, offset=slab_at + 4 * offset)

        x_sb = sb("x_sb", [P, TB, D])
        xn = sb("xn", [P, TB, D])
        hT = [sb("hT_hi", [P, KD, S], f32r), sb("hT_lo", [P, KD, S], f32r)]
        w_split = [sb("w_hi", [P, 4, 1024], f32r), sb("w_lo", [P, 4, 1024], f32r)]
        raw = at("raw", AT_RAW, [P, 2, 2, 2048])
        v_ring = at("v_ring", AT_RAW, [P, RING, D])
        proj = at("proj", AT_BIG, [P, TB, IN1])
        mix_row = at("mix_row", AT_BIG, [P, D])
        proj2 = at("proj2", AT_BIG, [P, TB, IN2])
        raw_keys = at("raw_keys", AT_BIG, [P, HP, P])
        ffn_row = at("ffn_row", AT_BIG + 2048, [P, D])
        mix2_row = at("mix2_row", AT_BIG + 3072, [P, D])
        rel_toep = at("rel_toep", AT_BIG + TB * IN2, [P, HEADS, 256])
        final_row = at("final_row", AT_BIG + 7168, [P, D])
        u_ring = at("u_ring", AT_BIG, [P, RING, D])
        gate_row = at("gate_row", AT_BIG + 8192, [P, HALF])
        peer_row = at("peer_row", AT_BIG + 8704, [P, D])
        keys_t = at("keys_t", AT_BIG + 9728, [P, HP, P])
        raw_ws = at("raw_ws", AT_ARENA, [P, 8, P])
        probs_of = [at("probs0", AT_ARENA, [P, HEADS, P])[:], at("probs1", AT_ARENA + 1024, [P, HEADS, 2 * P])[:]]
        probs_t = at("probs_t", AT_ARENA + 3072, [P, 24, P])
        qT = at("qT", AT_ARENA + 6144, [HD, HEADS, S])
        kT = at("kT", AT_ARENA + 8192, [HD, KV_HEADS, S])
        ret_qk = at("ret_qk", AT_ARENA + 8704, [P, RH, 2, S])
        attT = [at("attT_hi", AT_ARENA + 10752, [P, 4, S], f32r), at("attT_lo", AT_ARENA, [P, 4, S], f32r)]
        ret_s = xn[:, 0, :].rearrange("p (h c i) -> p h c i", h=RH, c=TB)
        state = xn[:, 1, :].rearrange("p (h v) -> p h v", h=RH)
        ffT = [at("ffT_hi", AT_ARENA, [P, 22, S], f32r), at("ffT_lo", AT_ARENA + 22 * S, [P, 22, S], f32r)]
        ff_rows = xn[:, 0, :].rearrange("p (a b n) -> p a b n", a=2, b=TB)
        ff_silu = xn[:, 1, :].rearrange("p (a b n) -> p a b n", a=2, b=TB)
        kT2 = at("kT2", AT_ARENA + 8192, [HD, HEADS, S])
        sq = at("sq", AT_ARENA + 10240, [P, D])
        qp = at("qp", AT_ARENA, [P, 2, TB, CHUNK])
        qpT = at("qpT", AT_ARENA + 2048, [P, 2, 4, S])
        v_sum = at("v_sum", AT_ARENA, [P, D])
        peer_sc = at("peer_sc", AT_ARENA + 4096, [P, TB * PEER_HEADS, 2 * P])
        ident = sb("ident", [P, P])
        gain_rows = sb("gain_rows", [G_ROWS, P])
        gains = sb("gains", [P, G_ROWS])
        neg_dist = sb("neg_dist", [P, 2 * P])
        age = sb("age", [P, P])
        q_pos = sb("q_pos", [P, P])
        k_age = sb("k_age", [P, 1])
        decay_t = sb("decay_t", [P, RH, P])
        decay_q = sb("decay_q", [P, RH, P])
        decay_k = sb("decay_k", [P, RH])
        sinks = sb("sinks", [P, HEADS])
        iota16 = sb("iota16", [P, TOPK])
        ws_t = sb("ws_t", [P, 8, P])
        rel_ext = sb("rel_ext", [HEADS, 512])
        rel_dram = nc.dram_tensor("rel_ext_dram", [HEADS, 512], f32)
        ss = sb("ss", [P, 32])
        var = sb("var", [P, 32])
        sd = sb("sd", [P, 32])
        rstd = sb("rstd", [P, 32])
        newton = sb("newton", [P, 32])
        mx = sb("mx", [P, TB, HEADS])
        neg_mx = sb("neg_mx", [P, TB, HEADS])
        sink_e = sb("sink_e", [P, TB, HEADS])
        den = sb("den", [P, TB, HEADS])
        bn = sb("bn", [P, TB * RH, 6])
        mv = sb("mv", [P, TB * RH, 2])
        T = AT_ARENA + 8192
        tk_work = at("tk_work", T, [P, 2 * P])
        tk_rest = at("tk_rest", T + 256, [P, 2 * P])
        cand = at("cand", T + 512, [P, TOPK * TOPK])
        cand_rest = at("cand_rest", T + 768, [P, TOPK * TOPK])
        hit = at("hit", T + 1024, [P, TOPK, TOPK])
        expert = at("expert", T + 1280, [P, TB * PEER_HEADS, TOPK], u32)
        diag = [at(f"diag{i}", T + 1536 + 128 * i, [P, P]) for i in range(4)]
        tk_top = sb("tk_top", [P, 2, TOPK])
        tk_ix = sb("tk_ix", [P, 2, TOPK], u32)
        tk_ixf = sb("tk_ixf", [P, 2, TOPK])
        best = [sb(f"best{i}", [P, TOPK]) for i in range(2)]
        pos = sb("pos", [P, TOPK], u32)
        pos_ij = sb("pos_ij", [P, 2, TOPK], u32)
        pos_f = sb("pos_f", [P, 2, TOPK])
        picked = sb("picked", [P, 2, TOPK])
        eidx_f = sb("eidx_f", [P, TOPK])
        neg_best = [sb(f"neg_best{i}", [P, 1]) for i in range(2)]
        g_exp = [sb(f"g_exp{i}", [P, TOPK]) for i in range(2)]
        g_sum = [sb(f"g_sum{i}", [P, 1]) for i in range(2)]
        g_inv = sb("g_inv", [P, 1])
        ix_now = [sb(f"ix_now{i}", [P, TOPK], u32) for i in range(2)]
        hid = [sb(f"hid{i}", [P, TOPK]) for i in range(2)]
        hid_g = [sb(f"hid_g{i}", [P, TOPK]) for i in range(2)]
        wgt = [sb(f"wgt{i}", [P, TOPK]) for i in range(2)]

        gemm = [ctx.enter_context(nc.psum_tensor(f"gemm{i}", [P, CHUNK], f32)) for i in range(4)]
        trb = [ctx.enter_context(nc.psum_tensor(f"trb{i}", [P, CHUNK], f32)) for i in range(2)]
        mmb = [ctx.enter_context(nc.psum_tensor(f"mmb{i}", [P, CHUNK], f32)) for i in range(2)]

        x_landed, ident_made = [sem("x_landed0"), sem("x_landed1")], sem("ident_made")
        gains_landed, aux_landed, sinks_landed = sem("gains_landed"), sem("aux_landed"), sem("sinks_landed")
        mix_landed, ffn_landed, late_landed = sem("mix_landed"), sem("ffn_landed"), sem("late_landed")
        w_landed = [[sem(f"w_landed{p}{h}") for h in range(2)] for p in range(2)]
        hi_ready, lo_ready = sem("hi_ready"), sem("lo_ready")
        w_used = sem("w_used")
        g_filled = [sem("g_filled0"), sem("g_filled1")]
        g_free = [sem(f"g_free{i}") for i in range(4)]
        tr_hi = sem("tr_hi")
        tr_filled = sem("tr_filled")
        tr_out = [sem("tr_out0"), sem("tr_out1")]
        mm_filled = sem("mm_filled")
        mm_out = [sem("mm_out0"), sem("mm_out1")]
        consts_made, decay_made, decay_masked, gains_zeroed = sem("consts_made"), sem("decay_made"), sem("decay_masked"), sem("gains_zeroed")
        var_ready, sd_ready = sem("var_ready"), sem("sd_ready")
        normed = sem("normed")
        squared = sem("squared")
        final_ready = sem("final_ready")
        max_ready, exp_done, probs_ready = sem("max_ready"), sem("exp_done"), sem("probs_ready")
        sink_ready = sem("sink_ready")
        ret_kd_ready, ret_qd_ready, ret_ready = sem("ret_kd_ready"), sem("ret_qd_ready"), sem("ret_ready")
        merged_ready, ff_silu_ready = sem("merged_ready"), sem("ff_silu_ready")
        gate_v_ready, mixed_a_ready, qk_normed = sem("gate_v_ready"), sem("mixed_a_ready"), sem("qk_normed")
        rel_filled, rel_stored, rel_loaded = sem("rel_filled"), sem("rel_stored"), sem("rel_loaded")
        expert_ready, best_ready, gexp_done = sem("expert_ready"), sem("best_ready"), sem("gexp_done")
        u_free, v_free = sem("u_free"), sem("v_free")
        u_landed = [sem(f"u_landed{i}") for i in range(RING)]
        v_landed = [sem(f"v_landed{i}") for i in range(RING)]
        gelu_done, wgt_ready, diag_ready = sem("gelu_done"), sem("wgt_ready"), sem("diag_ready")
        out_ready, stored = sem("out_ready"), sem("stored")
        pool_held, dve_held = sem("pool_held"), sem("dve_held")
        dve_step, pool_step = sem("dve_step"), sem("pool_step")

        class Steps:

            def __init__(self, engine, own):
                self.engine, self.own, self.n = engine, own, 0

            def put(self, ins):
                ins.then_inc(self.own, 1)
                self.n = self.n + 1

            def settle(self):
                self.engine.wait_ge(self.own, self.n)

            def link(self, ins):
                self.put(ins)
                self.settle()

            def enter(self, i, per, first=0):
                self.before = self.n
                self.n = self.n + (i - first) * per if first else self.n + i * per

            def leave(self, trips, per):
                self.n = self.before + trips * per

        block = ctx.enter_context(nc.Block())

        def landed(c):
            ffn_so_far = len([k for k in range(C_FF, C_DOWN) if k % 2 == c % 2 and k <= c])
            return 16 * (c // 2 + 1) + 16 * ffn_so_far

        def job_of(name, n):
            return (n % 2, n // 2) if name in NORM else (n // 2, n % 2)

        IN2_COLS = [D, D + CHUNK, 2 * D, HALF, 0]

        @block.sync
        def _(sp):
            def load_x(b):
                sp.dma_start(x_sb[:, b, :], x[0, b * P:(b + 1) * P, :]).then_inc(x_landed[b], 16)

            load_x(0)
            sp.dma_start(mix_row[:], norm_mix[0].partition_broadcast(P)).then_inc(mix_landed, 16)

            def half_free(c, half):
                if not (isinstance(c, int) and c < 2):
                    sp.wait_ge(lo_ready, (c - 2) * 4 + (2 * half + 2))

            def load(c, par, w, at, k_tiles=KD, width=CHUNK, halves=range(2)):
                kh = k_tiles // 2
                for half in halves:
                    half_free(c, half)
                    sp.dma_start(raw[:, par, half, 0:kh * width].rearrange("p (k n) -> p k n", k=kh),
                                 w.rearrange("(k p) n -> p k n", p=P)[:, half * kh:(half + 1) * kh, ds(at, width)]).then_inc(w_landed[par][half], 16)

            def load_ff(c, par, at):
                for half in range(2):
                    half_free(c, half)
                    dst = raw[:, par, half, :].rearrange("p (k n) -> p k n", k=KD // 2)
                    for off, w in ((0, w_gate[0]), (256, w_up[0])):
                        sp.dma_start(dst[:, :, off:off + 256], w.rearrange("(k p) n -> p k n", p=P)[:, half * 4:half * 4 + 4, ds(at, 256)]
                                     ).then_inc(w_landed[par][half], 16)

            def load_down(c, par, kk):
                for half in range(2):
                    half_free(c, half)
                    sp.dma_start(raw[:, par, half, 0:D].unsqueeze(1),
                                 w_down[0].rearrange("(k p) n -> p k n", p=P)[:, ds(kk + half, 1), :]).then_inc(w_landed[par][half], 16)

            load(0, 0, w_in[0], 0, halves=(0,))
            load_x(1)
            load(0, 0, w_in[0], 0, halves=(1,))
            load(1, 1, w_in[0], AK, width=256)
            with sp.Fori(0, 5) as i:
                for j in range(2):
                    load(i * 2 + (2 + j), j, w_in[0], i * (2 * CHUNK) + (RQ + j * CHUNK))
            for n in range(2):
                load(C_ATT + n, n, w_att_o[0], n * CHUNK, k_tiles=4)
            for n in range(2):
                load(C_RET + n, n, w_ret_o[0], n * CHUNK)
            for n in range(2):
                load(C_OUT + n, n, w_out[0], n * CHUNK)
            with sp.Fori(0, 5) as i:
                for j in range(2):
                    load_ff(i * 2 + (C_FF + j), j, i * 512 + 256 * j)
            load_ff(C_FF + 10, 0, 10 * 256)
            load_down(C_DOWN, 1, 0)
            with sp.Fori(0, 5) as i:
                for j in range(2):
                    load_down(i * 2 + (C_DOWN + 1 + j), j, i * 4 + (2 + 2 * j))
            for n in range(5):
                load(C_IN2 + n, n % 2, w_in_2[0], IN2_COLS[n])
            for n in range(2):
                load(C_OUT2 + n, (C_OUT2 + n) % 2, w_out_2[0], n * CHUNK)
            for n in range(4):
                load(C_QUERY + n, (C_QUERY + n) % 2, peer_w_query_2[0], n * CHUNK)
            for b in range(TB):
                sp.wait_ge(out_ready, b + 1)
                sp.dma_start(out[0, b * P:(b + 1) * P, :], xn[:, b, :]).then_inc(stored, 16)
            sp.wait_ge(stored, 16 * TB)

        @block.gpsimd
        def _(pool):
            me = Steps(pool, pool_step)
            me.link(nc.gpsimd.memset(ident[:], 0.0))
            nc.gpsimd.affine_select(out=ident[:], in_=ident[:], compare_op=ALU.not_equal, fill=1.0, base=0,
                                    pattern=[[-1, P]], channel_multiplier=1).then_inc(ident_made, 1)
            nc.gpsimd.iota(age[:], pattern=[[1, P]], base=0, channel_multiplier=-1, allow_small_or_imprecise_dtypes=True).then_inc(consts_made, 1)
            nc.gpsimd.iota(q_pos[:], pattern=[[1, P]], base=1, channel_multiplier=0, allow_small_or_imprecise_dtypes=True).then_inc(consts_made, 1)
            nc.gpsimd.iota(k_age[:], pattern=[[0, 1]], base=P - 1, channel_multiplier=-1, allow_small_or_imprecise_dtypes=True).then_inc(consts_made, 1)
            nc.gpsimd.iota(iota16[:], pattern=[[1, TOPK]], base=0, channel_multiplier=0, allow_small_or_imprecise_dtypes=True).then_inc(consts_made, 1)
            me.put(nc.gpsimd.iota(neg_dist[:], pattern=[[1, 2 * P]], base=-P, channel_multiplier=-1, allow_small_or_imprecise_dtypes=True))
            me.settle()
            me.link(nc.gpsimd.affine_select(out=neg_dist[:], in_=neg_dist[:], compare_op=ALU.is_ge, fill=MASKED, base=P,
                                            pattern=[[-1, 2 * P]], channel_multiplier=1))
            nc.gpsimd.affine_select(out=neg_dist[:], in_=neg_dist[:], compare_op=ALU.is_gt, fill=MASKED, base=0,
                                    pattern=[[1, 2 * P]], channel_multiplier=-1).then_inc(consts_made, 1)
            pool.wait_ge(gains_zeroed, 1)
            pool.dma_start(gain_rows[G_RET:G_RET + 8, :], ret_gn_gain[0].rearrange("(k p) -> k p", p=P)).then_inc(gains_landed, 16)
            pool.dma_start(gain_rows[G_BS:G_BS + 8, :], gmlp_b_s_2[0]).then_inc(gains_landed, 16)
            pool.dma_start(gain_rows[G_Q:G_Q + 1, 0:HD], q_norm_g_2).then_inc(gains_landed, 16)
            pool.dma_start(gain_rows[G_K:G_K + 1, 0:HD], k_norm_g_2).then_inc(gains_landed, 16)
            pool.dma_start(raw_ws[:], gmlp_w_s_2[0].rearrange("g i j -> i g j")).then_inc(aux_landed, 16)
            pool.dma_start(rel_ext[:, 127:127 + REL], rel_bias_2[0]).then_inc(rel_loaded, 16)
            pool.dma_start(sinks[:], att_sinks[0].partition_broadcast(P)).then_inc(sinks_landed, 16)
            pool.wait_ge(decay_made, RH)
            nc.gpsimd.affine_select(out=decay_t[:], in_=decay_t[:], compare_op=ALU.is_ge, fill=0.0, base=0,
                                    pattern=[[0, RH], [1, P]], channel_multiplier=-1).then_inc(decay_masked, 1)
            pool.wait_ge(rel_filled, 1)
            pool.dma_start(rel_dram[:], rel_ext[:]).then_inc(rel_stored, 16)
            pool.wait_ge(rel_stored, 16)
            pool.wait_ge(tr_filled, TR["merged"] + 4)
            pool.dma_start(ffn_row[:], norm_ffn[0].partition_broadcast(P)).then_inc(ffn_landed, 16)
            pool.dma_start(raw_keys[:], peer_sub_keys_2[0].rearrange("h a k d -> k (h a) d")).then_inc(late_landed, 16)
            pool.dma_start(rel_toep[:], bass.AP(tensor=rel_dram, offset=P, ap=[[1, P], [512, HEADS], [1, 256]])).then_inc(late_landed, 16)
            for dst, src in ((final_row, final_norm), (mix2_row, ln_mix_g_2[0]), (gate_row, gmlp_norm_g_2[0]), (peer_row, ln_ffn_g_2[0])):
                pool.dma_start(dst[:], src.partition_broadcast(P)).then_inc(late_landed, 16)

            def remainders(c, quarters):
                for q in quarters:
                    pool.wait_ge(hi_ready, 4 * c + q + 1)
                    pool.wait_ge(lo_ready, 4 * c + q)
                    nc.gpsimd.tensor_tensor(w_split[1][:, q, :], raw[:, c % 2, q // 2, (q % 2) * 1024:(q % 2 + 1) * 1024],
                                            w_split[0][:, q, :].bitcast(f32), ALU.subtract).then_inc(lo_ready, 1)

            remainders(C_FF, (2, 3))

            remainders(C_QUERY, (2, 3))
            remainders(C_QUERY + 1, (1, 2, 3))

            def gather(n, par):
                pool.wait_ge(expert_ready, n + 1)
                me.link(nc.gpsimd.tensor_copy(ix_now[par][:], expert[:, ds(n, 1), :].rearrange("p a k -> p (a k)")))
                for table, ring, free, there in ((peer_u_2, u_ring, u_free, u_landed), (peer_v_2, v_ring, v_free, v_landed)):
                    for k in range(TOPK):
                        pool.wait_ge(free, n * TOPK + (k + 1))
                        pool.sem_inc(pool_held, 1)
                        nc.gpsimd.indirect_dma_start(
                            out=ring[:, k % RING, :], out_offset=None, in_=table[0],
                            in_offset=bass.IndirectOffsetOnAxis(ap=ix_now[par][:, k:k + 1], axis=0),
                        ).then_inc(there[k % RING], 16)

            with pool.Fori(0, TB * PEER_HEADS // 2) as i:
                me.enter(i, 2)
                for par in range(2):
                    gather(i * 2 + par, par)
            me.leave(TB * PEER_HEADS // 2, 2)

        @block.scalar
        def _(act):
            nc.scalar.preload_act_table(ACT.Sqrt)

            def hi(prev, par, landed_at, n=1024, quarters=range(4)):
                for q in quarters:
                    if q % 2 == 0:
                        act.wait_ge(w_landed[par][q // 2], landed_at)
                    if prev is not None:
                        if q < 3:
                            act.wait_ge(w_used, prev * 3 + (q + 1))
                        else:
                            act.wait_ge(g_filled[1], prev + 1)
                    nc.scalar.activation(w_split[0][:, q, 0:n], raw[:, par, q // 2, (q % 2) * n:(q % 2 + 1) * n], ACT.Copy).then_inc(hi_ready, 1)

            def hi_at(c, **kw):
                hi(c - 1, c % 2, landed(c), **kw)

            def squares(b, half):
                cols = slice(half * CHUNK, (half + 1) * CHUNK)
                nc.scalar.activation(xn[:, b, cols], x_sb[:, b, cols], ACT.Square, scale=D ** -0.5,
                                     accum_out=ss[:, 2 * b + half:2 * b + half + 1]).then_inc(squared, 1)

            def residual_in(c, b):
                act.wait_ge(g_free[2 * (c % 2) + b], c // 2 + 1)

            def root_of(name, b):
                act.wait_ge(var_ready, RS[name] + b + 1)
                nc.scalar.activation(sd[:, b:b + 1], var[:, b:b + 1], ACT.Sqrt).then_inc(sd_ready, 1)

            def root(name, width):
                act.wait_ge(var_ready, RS[name] + 1)
                nc.scalar.activation(sd[:, 0:width], var[:, 0:width], ACT.Sqrt).then_inc(sd_ready, 1)

            def tile_out(c, par, b, dst, func=ACT.Copy, scale=1.0, width=CHUNK):
                act.wait_ge(g_filled[b], c + 1)
                nc.scalar.activation(dst, gemm[2 * par + b][:, 0:width], func, scale=scale).then_inc(g_free[2 * par + b], 1)

            def chunk_out(c, par, dst, func=ACT.Copy, scale=1.0, width=CHUNK):
                for b in range(TB):
                    tile_out(c, par, b, dst(b), func, scale, width)

            def softmax_exp(first, b):
                act.wait_ge(max_ready, first + b + 1)
                for h in range(HEADS):
                    nc.scalar.activation(probs_of[b][:, h, :], probs_of[b][:, h, :], ACT.Exp, bias=neg_mx[:, b, h:h + 1],
                                         accum_out=den[:, b, h:h + 1]).then_inc(exp_done, 1)

            def tr_out_copy(n, dst, rows=P, scale=1.0, tiles=4):
                act.wait_ge(tr_filled, n + 1)
                nc.scalar.activation(dst, trb[n % 2][0:rows, :].rearrange("p (k t) -> p k t", k=tiles), ACT.Copy, scale=scale).then_inc(tr_out[n % 2], 1)

            def mm_out_copy(n, dst):
                act.wait_ge(mm_filled, n + 1)
                nc.scalar.activation(dst, mmb[n % 2][:], ACT.Copy).then_inc(mm_out[n % 2], 1)

            def hi_columns(name, jobs=range(4), dst=hT[0], gain=None):
                for n in jobs:
                    half, b = job_of(name, n)
                    t = TR[name] + n
                    act.wait_ge(tr_filled, t + 1)
                    if gain is None:
                        nc.scalar.activation(dst[:, 4 * half:4 * half + 4, b * P:(b + 1) * P],
                                             trb[t % 2][:].rearrange("p (k t) -> p k t", k=4), ACT.Copy).then_inc(tr_hi, 1)
                    else:
                        for k in range(4):
                            ins = nc.scalar.activation(dst[:, 4 * half + k, b * P:(b + 1) * P], trb[t % 2][:, k * P:(k + 1) * P], ACT.Copy,
                                                       scale=gains[:, gain + 4 * half + k:gain + 4 * half + k + 1])
                        ins.then_inc(tr_hi, 1)

            def norm_behind(name, c):
                residual_in(c, 0)
                squares(0, 1)
                root_of(name, 0)
                hi_at(c + 1, quarters=(0, 1))
                hi_columns(name, (0, 1))
                hi_at(c + 1, quarters=(2, 3))
                residual_in(c, 1)
                squares(1, 1)
                root_of(name, 1)
                hi_columns(name, (2, 3))

            for b in range(TB):
                act.wait_ge(x_landed[b], 16)
                squares(b, 0)
                squares(b, 1)
                root_of("norm1", b)
                for half in range(2):
                    hi(None, 0, landed(0), quarters=(2 * b + half,))
                    if b == 0:
                        hi_columns("norm1", (half,))
            hi_columns("norm1", (2, 3))
            hi_at(1, n=512)
            chunk_out(0, 0, lambda b: proj[:, b, AQ:AQ + CHUNK], scale=HD_SCALE)
            act.wait_ge(consts_made, 5)
            for h in range(RH):
                nc.scalar.activation(decay_q[:, h, :], q_pos[:], ACT.Exp, scale=log_decay[h])
                nc.scalar.activation(decay_k[:, h:h + 1], k_age[:], ACT.Exp, scale=log_decay[h])
                nc.scalar.activation(decay_t[:, h, :], age[:], ACT.Exp, scale=log_decay[h]).then_inc(decay_made, 1)
            hi_at(2)
            chunk_out(1, 1, lambda b: proj[:, b, AK:AK + 256], width=256)
            hi_at(3)
            chunk_out(2, 0, lambda b: proj[:, b, RQ:RQ + CHUNK])
            hi_at(4, quarters=(0,))
            softmax_exp(0, 0)
            hi_at(4, quarters=(1, 2, 3))
            chunk_out(3, 1, lambda b: proj[:, b, RKO:RKO + CHUNK])
            softmax_exp(0, 1)
            act.wait_ge(sink_ready, 1)
            nc.scalar.activation(sink_e[:], sink_e[:], ACT.Exp).then_inc(exp_done, 1)
            for c in (4, 5):
                hi_at(c + 1)
                chunk_out(c, c % 2, lambda b: proj[:, b, RVO + (c - 4) * CHUNK:RVO + (c - 3) * CHUNK])
            for q in range(3):
                for n in (2 * q, 2 * q + 1):
                    tr_out_copy(TR["p_att"] + n, probs_t[:, 4 * n:4 * n + 4, :])
                hi_at(7, quarters=(q,))
            hi_at(7, quarters=(3,))
            chunk_out(6, 0, lambda b: proj[:, b, RG:RG + CHUNK], ACT.Silu)
            for b in range(TB):
                hi_at(8, quarters=(b,))
                mm_out_copy(MM["o_att"] + b, proj[:, b, AQ:AQ + CHUNK])
            hi_at(8, quarters=(2,))
            for h in range(2):
                mm_out_copy(MM["ret_state"] + h, state[:, 2 * h:2 * h + 2, :].rearrange("p h v -> p (h v)"))
            hi_at(8, quarters=(3,))
            chunk_out(7, 1, lambda b: proj[:, b, RG + CHUNK:RG + 2 * CHUNK], ACT.Silu)
            hi_at(9, quarters=(0, 1, 2))
            for b in range(TB):
                t = TR["att"] + b
                act.wait_ge(tr_filled, t + 1)
                nc.scalar.activation(attT[0][:, :, b * P:(b + 1) * P], trb[t % 2][:].rearrange("p (k t) -> p k t", k=4), ACT.Copy).then_inc(tr_hi, 1)
            hi_at(9, quarters=(3,))
            for c in (8, 9, 10, 11):
                if c > 8:
                    hi_at(c + 1, n=(1024 if c + 1 < C_ATT else 512))
                chunk_out(c, c % 2, lambda b: proj[:, b, GA + (c - 8) * CHUNK:GA + (c - 7) * CHUNK], ACT.Sigmoid)
                if c == 8:
                    root("ret", TB * RH)
            hi_columns("ret", gain=G_RET)
            nc.scalar.preload_act_table(ACT.Sqrt)
            hi_at(13, n=512)
            hi_at(14)
            hi_at(15)
            hi_columns("merged", (0, 1))
            hi_at(16)
            hi_columns("merged", (2, 3))
            hi_at(17)
            for b in range(TB):
                residual_in(C_OUT, b)
                squares(b, 0)
            norm_behind("norm2", C_OUT + 1)
            nc.scalar.preload_act_table(ACT.Silu)

            def ff_gate(c, par):
                for b in range(TB):
                    act.wait_ge(g_filled[b], c + 1)
                    nc.scalar.activation(ff_silu[:, par, b, :], gemm[2 * par + b][:, 0:256], ACT.Silu).then_inc(ff_silu_ready, 1)

            def ff_hi(f, par):
                p = (TR["ff"] + par) % 2
                act.wait_ge(tr_filled, f + (TR["ff"] + 1))
                nc.scalar.activation(ffT[0][:, ds(f * 2, 2), :].rearrange("p k t -> p (k t)"), trb[p][:], ACT.Copy).then_inc(tr_hi, 1)

            hi_at(C_FF + 1)
            ff_gate(C_FF, 0)
            with act.Fori(0, 4) as i:
                for j in range(2):
                    hi(i * 2 + (C_FF + 1 + j), j, i * 32 + landed(C_FF + 2 + j))
                    ff_gate(i * 2 + (C_FF + 1 + j), 1 - j)
                    ff_hi(i * 2 + j, j)
            hi_at(C_FF + 10)
            ff_gate(C_FF + 9, 1)
            ff_hi(8, 0)
            hi_at(C_DOWN, n=512)
            ff_gate(C_FF + 10, 0)
            ff_hi(9, 1)
            hi_at(C_DOWN + 1, n=512)
            ff_hi(10, 0)
            nc.scalar.preload_act_table(ACT.Sqrt)
            for n in range(2, 4):
                hi_at(C_DOWN + n, n=512)
            with act.Fori(0, 3) as i:
                for j in range(2):
                    hi(i * 2 + (C_DOWN + 3 + j), (C_DOWN + 4 + j) % 2, i * 16 + landed(C_DOWN + 4 + j), n=512)
            hi_at(C_DOWN + 10, n=512)
            def squares_of(b, src, junk, at, ready):
                for half in range(2):
                    ready(half)
                    j = 2 * (2 * b + half)
                    nc.scalar.activation(junk[:, j:j + 2, :].rearrange("p k t -> p (k t)"), src[:, b, half * CHUNK:(half + 1) * CHUNK], ACT.Square,
                                         scale=D ** -0.5, accum_out=ss[:, at + 2 * b + half:at + 2 * b + half + 1]).then_inc(squared, 1)

            def key_columns(jobs):
                for n in jobs:
                    tr_out_copy(TR["keys"] + n, keys_t[:, 4 * n:4 * n + 4, :])

            def root_at(at, job):
                act.wait_ge(var_ready, job + 1)
                nc.scalar.activation(sd[:, at:at + 1], var[:, at:at + 1], ACT.Sqrt).then_inc(sd_ready, 1)

            for b in range(TB):
                squares_of(b, x_sb, hT[0], 0, lambda half: act.wait_ge(g_free[2 * half + b], (C_IN2 - 2 + half) // 2 + 1))
                if b == 1:
                    key_columns((2, 3))
                    hi_columns("norm3", (0,))
                root_at(b, RS["final"] + 2 * b)
                squares_of(b, xn, hT[1], 4, lambda half: act.wait_ge(final_ready, 2 * b + half + 1))
                if b == 1:
                    hi_columns("norm3", (1,))
                if b == 0:
                    key_columns((0, 1))
                hi_at(C_IN2, quarters=(b,))
                root_at(2 + b, RS["final"] + 2 * b + 1)
            hi_at(C_IN2, quarters=(2, 3))
            hi_columns("norm3", (2, 3))

            for n in range(3):
                hi_at(C_IN2 + n + 1)
                chunk_out(C_IN2 + n, n % 2, lambda b: proj2[:, b, IN2_COLS[n]:IN2_COLS[n] + CHUNK])
                if n == 1:
                    root("band", 32)
            for n in range(8):
                b, is_k, four = n // 4, (n // 2) % 2, n % 2
                if is_k:
                    tr_out_copy(TR["qk_band"] + n, kT2[:, 4 * four:4 * four + 4, b * P:(b + 1) * P], rows=HD, scale=gains[0:HD, G_K:G_K + 1])
            hi_at(C_IN2 + 4, quarters=(0,))
            softmax_exp(2, 0)
            hi_at(C_IN2 + 4, quarters=(1,))
            softmax_exp(2, 1)
            hi_at(C_IN2 + 4, quarters=(2, 3))
            chunk_out(C_IN2 + 3, 1, lambda b: proj2[:, b, HALF:D], ACT.Gelu_apprx_tanh)
            for b in range(TB):
                act.wait_ge(g_free[2 + b], (C_IN2 + 3) // 2 + 1)
                nc.scalar.activation(xn[:, b, 0:HALF], proj2[:, b, HALF:D], ACT.Square, accum_out=ss[:, b:b + 1]).then_inc(squared, 1)
            root("gate", TB)
            nc.scalar.preload_act_table(ACT.Gelu_apprx_tanh)
            hi_at(C_OUT2)
            chunk_out(C_IN2 + 4, 0, lambda b: proj2[:, b, 0:HALF], ACT.Gelu_apprx_tanh)
            for n in range(6):
                tr_out_copy(TR["p_band"] + n, probs_t[:, 4 * n:4 * n + 4, :])
            for b in range(TB):
                mm_out_copy(MM["o_band"] + b, proj2[:, b, D:D + HALF])
            hi_columns("mixed")
            nc.scalar.preload_act_table(ACT.Sqrt)
            hi_at(C_OUT2 + 1)
            for b in range(TB):
                residual_in(C_OUT2, b)
                squares(b, 0)
            norm_behind("norm4", C_OUT2 + 1)

            def queries_out(n, b):
                c = C_QUERY + n
                tile_out(c, c % 2, b, qp[:, n % 2, b, :])

            def query_columns(n, b):
                tr_out_copy(TR["query"] + 2 * n + b, qpT[:, n % 2, :, b * P:(b + 1) * P])

            def scores_out(n, b):
                at = b * PEER_HEADS + 2 * n
                mm_out_copy(MM["peer_s"] + 2 * n + b, peer_sc[:, at:at + 2, :].rearrange("p n k -> p (n k)"))

            def best_exp(n, par):
                act.wait_ge(best_ready, n + 1)
                nc.scalar.activation(g_exp[par][:], best[par][:], ACT.Exp, bias=neg_best[par][:], accum_out=g_sum[par][:]).then_inc(gexp_done, 1)

            queries_out(0, 0)
            query_columns(0, 0)
            hi_at(C_QUERY + 1, quarters=(0,))
            scores_out(0, 0)
            hi_at(C_QUERY + 1, quarters=(1, 2, 3))
            queries_out(0, 1)
            query_columns(0, 1)
            scores_out(0, 1)
            for n in range(1, 4):
                if n < 3:
                    hi_at(C_QUERY + n + 1)
                else:
                    best_exp(0, 0)
                    nc.scalar.preload_act_table(ACT.Gelu_apprx_tanh)
                for step in (queries_out, query_columns, scores_out):
                    for b in range(TB):
                        step(n, b)

            def weigh(n, par, rows=TOPK):
                act.wait_ge(u_free, n * TOPK + (RING + TOPK))
                nc.scalar.activation(hid_g[par][:], hid[par][:], ACT.Gelu_apprx_tanh).then_inc(gelu_done, 1)
                act.wait_ge(wgt_ready, n + 1)
                for k in range(rows):
                    act.wait_ge(v_free, n * TOPK + (RING + k - 3))
                    nc.scalar.activation(diag[k % 4][:], ident[:], ACT.Copy, scale=wgt[par][:, k:k + 1]).then_inc(diag_ready, 1)

            weigh(0, 0)
            best_exp(1, 1)
            weigh(1, 1)
            with act.Fori(0, TB * PEER_HEADS // 2 - 2) as i:
                for par in range(2):
                    best_exp(i * 2 + (2 + par), par)
                    weigh(i * 2 + (2 + par), par)
            best_exp(14, 0)
            weigh(14, 0)
            best_exp(15, 1)
            weigh(15, 1, rows=PE_LAST)

        @block.vector
        def _(dve):
            me = Steps(dve, dve_step)
            V = nc.vector
            V.memset(gain_rows[:], 0.0).then_inc(gains_zeroed, 1)

            def lo(prev, par, n=1024, quarters=range(4)):
                for q in quarters:
                    dve.wait_ge(hi_ready, prev * 4 + (q + 5) if prev is not None else q + 1)
                    V.tensor_tensor(w_split[1][:, q, 0:n], raw[:, par, q // 2, (q % 2) * n:(q % 2 + 1) * n],
                                    w_split[0][:, q, 0:n].bitcast(f32), ALU.subtract).then_inc(lo_ready, 1)

            def lo_at(c, **kw):
                lo(c - 1, c % 2, **kw)

            def lo_columns(name, jobs=range(4), gain=None):
                for n in jobs:
                    half, b = job_of(name, n)
                    t = TR[name] + n
                    dve.wait_ge(tr_hi, SPLIT[name] + n + 1)
                    if gain is None:
                        V.tensor_tensor(hT[1][:, 4 * half:4 * half + 4, b * P:(b + 1) * P], trb[t % 2][:].rearrange("p (k t) -> p k t", k=4),
                                        hT[0][:, 4 * half:4 * half + 4, b * P:(b + 1) * P].bitcast(f32), ALU.subtract).then_inc(tr_out[t % 2], 1)
                    else:
                        for k in range(4):
                            g = gain + 4 * half + k
                            ins = V.scalar_tensor_tensor(out=hT[1][:, 4 * half + k, b * P:(b + 1) * P], in0=trb[t % 2][:, k * P:(k + 1) * P],
                                                         scalar=gains[:, g:g + 1], in1=hT[0][:, 4 * half + k, b * P:(b + 1) * P].bitcast(f32),
                                                         op0=ALU.mult, op1=ALU.subtract)
                        ins.then_inc(tr_out[t % 2], 1)

            def copy_out_tr(n, dst, src):
                dve.wait_ge(tr_filled, n + 1)
                V.tensor_copy(dst, src).then_inc(tr_out[n % 2], 1)

            def inverse_root(at, width, job):
                dve.wait_ge(sd_ready, job + 1)
                r, t, v = rstd[:, at:at + width], newton[:, at:at + width], var[:, at:at + width]
                me.link(V.reciprocal(r, sd[:, at:at + width]))
                if width == 1:
                    me.link(V.tensor_scalar(t, r, r, v, ALU.mult, ALU.mult))
                else:
                    me.link(V.tensor_tensor(t, r, r, ALU.mult))
                    me.link(V.tensor_tensor(t, t, v, ALU.mult))
                me.link(V.tensor_scalar(t, t, -0.5, 1.5, ALU.mult, ALU.add))
                me.link(V.tensor_tensor(r, r, t, ALU.mult))

            SQUARES = numbered(("norm1", 4), ("norm2", 4), ("final", 8), ("gate", 2), ("norm4", 4))

            def variance(name, b, after):
                dve.wait_ge(squared, SQUARES[name] + after)
                V.tensor_scalar(var[:, b:b + 1], ss[:, 2 * b:2 * b + 1], ss[:, 2 * b + 1:2 * b + 2], EPS, ALU.add, ALU.add).then_inc(var_ready, 1)

            def normed_rows(name, b, row, dst, done):
                inverse_root(b, 1, RS[name] + b)
                for half in range(2):
                    cols = slice(half * CHUNK, (half + 1) * CHUNK)
                    V.scalar_tensor_tensor(out=dst[:, b, cols], in0=x_sb[:, b, cols], scalar=rstd[:, b:b + 1], in1=row[:, cols],
                                           op0=ALU.mult, op1=ALU.mult).then_inc(done, 1)

            dve.wait_ge(x_landed[0], 16)
            variance("norm1", 0, 2)
            dve.wait_ge(mix_landed, 16)
            normed_rows("norm1", 0, mix_row, xn, normed)
            lo(None, 0, quarters=(0,))
            lo_columns("norm1", (0,))
            lo(None, 0, quarters=(1,))
            lo_columns("norm1", (1,))
            dve.wait_ge(x_landed[1], 16)
            variance("norm1", 1, 4)
            normed_rows("norm1", 1, mix_row, xn, normed)
            lo(None, 0, quarters=(2, 3))
            lo_columns("norm1", (2, 3))
            dve.wait_ge(tr_filled, TR["gains"] + 1)
            V.tensor_copy(gains[:], trb[TR["gains"] % 2][:, 0:G_ROWS]).then_inc(tr_out[TR["gains"] % 2], 1)
            dve.wait_ge(tr_out[TR["gains"] % 2], TR["gains"] // 2 + 1)
            for n in range(2):
                t = TR["ws"] + n
                dve.wait_ge(tr_filled, t + 1)
                me.link(V.tensor_copy(ws_t[:, 4 * n:4 * n + 4, :].rearrange("p g i -> p (g i)"), trb[t % 2][:]))
                V.memset(ws_t[64:P, 4 * n:4 * n + 4, 0:64], 0.0).then_inc(tr_out[t % 2], 1)
                lo_at(1, n=512, quarters=(2 * n, 2 * n + 1))

            def query_heads(jobs):
                for n in jobs:
                    b, four = n // 2, n % 2
                    t = TR["q_att"] + n
                    copy_out_tr(t, qT[:, 4 * four:4 * four + 4, b * P:(b + 1) * P], trb[t % 2][0:HD, :].rearrange("p (h t) -> p h t", h=4))

            query_heads((0, 1))
            dve.wait_ge(rel_loaded, 16)
            me.put(V.tensor_copy(rel_ext[:, 0:127], rel_ext[:, 127:128].to_broadcast([HEADS, 127])))
            V.tensor_copy(rel_ext[:, 127 + REL:512], rel_ext[:, 126 + REL:127 + REL].to_broadcast([HEADS, 512 - 127 - REL])).then_inc(rel_filled, 1)
            lo_at(2)
            query_heads((2, 3))
            lo_at(3, quarters=(0,))
            t = TR["k_att"]
            copy_out_tr(t, kT[:].rearrange("p h t -> p (h t)"), trb[t % 2][0:HD, :])
            lo_at(3, quarters=(1, 2, 3))

            def finish_softmax():
                for b in range(TB):
                    w = (b + 1) * P
                    V.tensor_tensor(probs_of[b], probs_of[b], den[:, b, :].unsqueeze(2).to_broadcast([P, HEADS, w]),
                                    ALU.mult).then_inc(probs_ready, 1)

            dve.wait_ge(consts_made, 5)
            dve.wait_ge(sinks_landed, 16)
            def alibi_scores(jobs):
                for n in jobs:
                    b, h0, hn = SCORE_JOBS[n]
                    m, w = MM["s_att"] + n, (b + 1) * P
                    dve.wait_ge(mm_filled, m + 1)
                    for h in range(hn):
                        ins = V.scalar_tensor_tensor(out=probs_of[b][:, h0 + h, :], in0=neg_dist[:, 2 * P - w:2 * P], scalar=slopes[h0 + h],
                                                     in1=mmb[m % 2][:, h * w:(h + 1) * w], op0=ALU.mult, op1=ALU.add)
                        if h < hn - 1:
                            me.put(ins)
                        else:
                            ins.then_inc(mm_out[m % 2], 1)

            def row_max(b, jobs_out):
                for p in range(2):
                    dve.wait_ge(mm_out[p], (MM["s_att"] + jobs_out) // 2)
                me.link(V.tensor_reduce(mx[:, b, :], probs_of[b], axis=AX.X, op=ALU.max))
                me.link(V.tensor_tensor(mx[:, b, :], mx[:, b, :], sinks[:], ALU.max))
                V.tensor_scalar(neg_mx[:, b, :], mx[:, b, :], -1.0, None, ALU.mult).then_inc(max_ready, 1)

            alibi_scores((0, 1))
            row_max(0, 2)
            alibi_scores((2, 3))
            lo_at(4, quarters=(0,))
            alibi_scores((4, 5))
            row_max(1, 6)
            for b in range(TB):
                ins = V.tensor_tensor(sink_e[:, b, :], sinks[:], mx[:, b, :], ALU.subtract)
                if b < TB - 1:
                    me.put(ins)
            ins.then_inc(sink_ready, 1)
            lo_at(4, quarters=(1, 2, 3))
            dve.wait_ge(exp_done, TB * HEADS + 1)
            me.link(V.tensor_tensor(den[:], den[:], sink_e[:], ALU.add))
            me.link(V.reciprocal(den[:], den[:]))
            lo_at(5, quarters=(0, 1))
            finish_softmax()
            lo_at(5, quarters=(2, 3))

            dve.wait_ge(decay_masked, 1)
            for b in range(TB):
                dve.wait_ge(g_free[2 + b], 2)
            for h in range(RH):
                if h % 2 == 0:
                    lo_at(6, quarters=(h // 2,))
                k_cols = proj[:, 0, RKO + h * RK:RKO + (h + 1) * RK]
                t = TR["ret_qk"] + h
                copy_out_tr(t, ret_qk[:, h, :, :].rearrange("p a t -> p (a t)"), trb[t % 2][:])
                V.tensor_scalar(k_cols, k_cols, decay_k[:, h:h + 1], RET_SCALE, ALU.mult, ALU.mult).then_inc(ret_kd_ready, 1)
            lo_at(6, quarters=(2, 3))
            lo_at(7, quarters=(0, 1, 2))
            for h in range(RH):
                if h == 2:
                    lo_at(7, quarters=(3,))
                m = MM["ret_s"] + h
                dve.wait_ge(mm_filled, m + 1)
                for c in range(TB):
                    ins = V.scalar_tensor_tensor(out=ret_s[:, h, c, :], in0=mmb[m % 2][:, c * P:(c + 1) * P], scalar=RET_SCALE,
                                                 in1=decay_t[:, h, :], op0=ALU.mult, op1=ALU.mult)
                    if c < TB - 1:
                        me.put(ins)
                ins.then_inc(mm_out[m % 2], 1)
                q2 = ret_qk[:, h, 0, P:2 * P]
                V.tensor_tensor(q2, q2, decay_q[:, h, :], ALU.mult).then_inc(ret_qd_ready, 1)
            lo_at(8)
            for h in range(RH):
                if h % 2 == 0:
                    lo_at(9, quarters=(h // 2,))
                m = MM["ret_o"] + h
                dve.wait_ge(mm_filled, m + 1)
                for c in range(TB):
                    me.put(V.bn_stats(bn[:, 2 * h + c, :], mmb[m % 2][:, c * RV:(c + 1) * RV]))
                V.tensor_copy(proj[:, :, RVO + h * RV:RVO + (h + 1) * RV], mmb[m % 2][:].rearrange("p (c v) -> p c v", c=TB)).then_inc(mm_out[m % 2], 1)
            lo_at(9, quarters=(2,))
            for b in range(TB):
                t = TR["att"] + b
                dve.wait_ge(tr_hi, SPLIT["att"] + b + 1)
                V.tensor_tensor(attT[1][:, :, b * P:(b + 1) * P], trb[t % 2][:].rearrange("p (k t) -> p k t", k=4),
                                attT[0][:, :, b * P:(b + 1) * P].bitcast(f32), ALU.subtract).then_inc(tr_out[t % 2], 1)
            lo_at(9, quarters=(3,))
            me.settle()
            for n in range(TB * RH):
                me.put(V.bn_aggr(mv[:, n, :], bn[:, n, :]))
            me.settle()
            V.tensor_scalar(var[:, 0:TB * RH], mv[:, :, 1], EPS, None, ALU.add).then_inc(var_ready, 1)
            inverse_root(0, TB * RH, RS["ret"])
            lo_at(10)
            for p in range(2):
                dve.wait_ge(mm_out[p], (MM["ret_o"] + RH) // 2)
            for h in range(RH):
                for c in range(TB):
                    o = proj[:, c, RVO + h * RV:RVO + (h + 1) * RV]
                    n = 2 * h + c
                    me.put(V.tensor_scalar(o, o, mv[:, n, 0:1], rstd[:, n:n + 1], ALU.subtract, ALU.mult))
            me.settle()
            for half in range(2):
                for b in range(TB):
                    dve.wait_ge(g_free[2 * half + b], 4)
                    o = proj[:, b, RVO + half * CHUNK:RVO + (half + 1) * CHUNK]
                    V.tensor_tensor(o, o, proj[:, b, RG + half * CHUNK:RG + (half + 1) * CHUNK], ALU.mult).then_inc(ret_ready, 1)
            lo_at(11)
            lo_at(12, n=512)
            lo_columns("ret", gain=G_RET)
            lo_at(13, n=512)
            for n in range(2):
                if n == 1:
                    lo_at(14)
                for b in range(TB):
                    dve.wait_ge(g_filled[b], C_ATT + n + 1)
                    dve.wait_ge(g_free[2 * n + b], 5)
                    ga = proj[:, b, GA + n * CHUNK:GA + (n + 1) * CHUNK]
                    V.tensor_tensor(ga, gemm[2 * n + b][:], ga, ALU.mult).then_inc(g_free[2 * n + b], 1)
            for n in range(2):
                lo_at(15 + n)
                for b in range(TB):
                    dve.wait_ge(g_filled[b], C_RET + n + 1)
                    gr = proj[:, b, GR + n * CHUNK:GR + (n + 1) * CHUNK]
                    V.tensor_tensor(gr, gemm[2 * n + b][:], gr, ALU.mult).then_inc(g_free[2 * n + b], 1)
                for b in range(TB):
                    dve.wait_ge(g_free[2 * n + b], (C_RET + n) // 2 + 1)
                    ga = proj[:, b, GA + n * CHUNK:GA + (n + 1) * CHUNK]
                    V.tensor_tensor(ga, ga, proj[:, b, GR + n * CHUNK:GR + (n + 1) * CHUNK], ALU.add).then_inc(merged_ready, 1)
                lo_columns("merged", (2 * n, 2 * n + 1))

            def residual(c, n, tiles=range(TB)):
                p = c % 2
                for b in tiles:
                    dve.wait_ge(g_filled[b], c + 1)
                    xs = x_sb[:, b, n * CHUNK:(n + 1) * CHUNK]
                    V.tensor_tensor(xs, gemm[2 * p + b][:], xs, ALU.add).then_inc(g_free[2 * p + b], 1)

            def norm_behind(name, c, row):
                residual(c, 1, (0,))
                dve.wait_ge(g_free[2 * (c % 2)], c // 2 + 1)
                dve.wait_ge(g_free[2 * (1 - c % 2)], (c - 1) // 2 + 1)
                variance(name, 0, 3)
                normed_rows(name, 0, row, xn, normed)
                lo_at(c + 1, quarters=(0, 1))
                lo_columns(name, (0, 1))
                residual(c, 1, (1,))
                dve.wait_ge(g_free[2 * (c % 2) + 1], c // 2 + 1)
                dve.wait_ge(g_free[2 * (1 - c % 2) + 1], (c - 1) // 2 + 1)
                variance(name, 1, 4)
                normed_rows(name, 1, row, xn, normed)
                lo_columns(name, (2, 3))
                dve.wait_ge(lo_ready, 4 * (c + 2))

            lo_at(C_OUT + 1)
            residual(C_OUT, 0)
            dve.wait_ge(ffn_landed, 16)
            norm_behind("norm2", C_OUT + 1, ffn_row)

            def ff_up(c, par):
                for b in range(TB):
                    dve.wait_ge(ff_silu_ready, (c - C_FF) * 2 + (b + 1))
                    V.tensor_tensor(ff_rows[:, par, b, :], gemm[2 * par + b][:, 256:512], ff_silu[:, par, b, :], ALU.mult).then_inc(g_free[2 * par + b], 1)

            def ff_lo(f, par):
                p = (TR["ff"] + par) % 2
                dve.wait_ge(tr_hi, f + (SPLIT["ff"] + 1))
                V.tensor_tensor(ffT[1][:, ds(f * 2, 2), :].rearrange("p k t -> p (k t)"), trb[p][:],
                                ffT[0][:, ds(f * 2, 2), :].rearrange("p k t -> p (k t)").bitcast(f32), ALU.subtract).then_inc(tr_out[p], 1)

            lo_at(C_FF + 1)
            ff_up(C_FF, 0)
            with dve.Fori(0, 4) as i:
                for j in range(2):
                    lo(i * 2 + (C_FF + 1 + j), j)
                    ff_up(i * 2 + (C_FF + 1 + j), 1 - j)
                    ff_lo(i * 2 + j, j)
            lo_at(C_FF + 10)
            ff_up(C_FF + 9, 1)
            ff_lo(8, 0)
            lo_at(C_DOWN, n=512)
            ff_up(C_FF + 10, 0)
            ff_lo(9, 1)
            lo_at(C_DOWN + 1, n=512)
            ff_lo(10, 0)
            with dve.Fori(0, 4) as i:
                for j in range(2):
                    lo(i * 2 + (C_DOWN + 1 + j), (C_DOWN + 2 + j) % 2, n=512)
            lo_at(C_DOWN + 10, n=512)
            dve.wait_ge(late_landed, 6 * 16)
            def down_in(b, halves=range(2)):
                dve.wait_ge(g_filled[b], C_IN2)
                for n in halves:
                    xs = x_sb[:, b, n * CHUNK:(n + 1) * CHUNK]
                    V.tensor_tensor(xs, gemm[2 * n + b][:], xs, ALU.add).then_inc(g_free[2 * n + b], len([c for c in range(C_DOWN, C_IN2) if c % 2 == n]))

            def times_gain(b, halves=range(2)):
                for n in halves:
                    dve.wait_ge(g_free[2 * n + b], (C_IN2 - 2 + n) // 2 + 1)
                    cols = slice(n * CHUNK, (n + 1) * CHUNK)
                    V.tensor_tensor(xn[:, b, cols], x_sb[:, b, cols], final_row[:, cols], ALU.mult).then_inc(final_ready, 1)

            def final_variance(b):
                dve.wait_ge(squared, SQUARES["final"] + 4 * b + 2)
                V.tensor_scalar(var[:, b:b + 1], ss[:, 2 * b:2 * b + 1], ss[:, 2 * b + 1:2 * b + 2], EPS, ALU.add, ALU.add).then_inc(var_ready, 1)

            def next_variance(b):
                inverse_root(b, 1, RS["final"] + 2 * b)
                dve.wait_ge(squared, SQUARES["final"] + 4 * b + 4)
                v, r = var[:, 2 + b:3 + b], rstd[:, b:b + 1]
                me.link(V.tensor_scalar(v, ss[:, 4 + 2 * b:5 + 2 * b], ss[:, 5 + 2 * b:6 + 2 * b], r, ALU.add, ALU.mult))
                V.tensor_scalar(v, v, r, EPS, ALU.mult, ALU.add).then_inc(var_ready, 1)

            def next_rows(b):
                inverse_root(2 + b, 1, RS["final"] + 2 * b + 1)
                both = newton[:, 4 + b:5 + b]
                me.link(V.tensor_tensor(both, rstd[:, b:b + 1], rstd[:, 2 + b:3 + b], ALU.mult))
                for n in range(2):
                    cols = slice(n * CHUNK, (n + 1) * CHUNK)
                    V.scalar_tensor_tensor(out=xn[:, b, cols], in0=xn[:, b, cols], scalar=both, in1=mix2_row[:, cols],
                                           op0=ALU.mult, op1=ALU.mult).then_inc(normed, 1)

            down_in(0)
            times_gain(0)
            final_variance(0)
            down_in(1, (0,))
            next_variance(0)
            down_in(1, (1,))
            times_gain(1, (0,))
            next_rows(0)
            times_gain(1, (1,))
            final_variance(1)
            lo_at(C_IN2, quarters=(0,))
            lo_columns("norm3", (0,))
            next_variance(1)
            lo_columns("norm3", (1,))
            lo_at(C_IN2, quarters=(1,))
            next_rows(1)
            lo_at(C_IN2, quarters=(2, 3))
            lo_columns("norm3", (2, 3))
            for b in range(TB):
                me.put(V.scalar_tensor_tensor(out=x_sb[:, b, :], in0=x_sb[:, b, :], scalar=rstd[:, b:b + 1], in1=final_row[:],
                                              op0=ALU.mult, op1=ALU.mult))
            lo_at(C_IN2 + 1)
            lo_at(C_IN2 + 2)

            for n in range(2):
                for b in range(TB):
                    dve.wait_ge(g_free[2 * n + b], (C_IN2 + n) // 2 + 1)
            for b in range(TB):
                qk = proj2[:, b, D:2 * D]
                me.link(V.tensor_tensor(sq[:], qk, qk, ALU.mult))
                me.link(V.tensor_reduce(ss[:, 16 * b:16 * b + 16], sq[:].rearrange("p (h d) -> p h d", d=HD), axis=AX.X, op=ALU.add))
            V.tensor_scalar(var[:, 0:32], ss[:, 0:32], 1.0 / HD, EPS, ALU.mult, ALU.add).then_inc(var_ready, 1)
            inverse_root(0, 32, RS["band"])
            for b in range(TB):
                qk = proj2[:, b, D:2 * D].rearrange("p (h d) -> p h d", d=HD)
                V.tensor_tensor(qk, qk, rstd[:, 16 * b:16 * b + 16].unsqueeze(2).to_broadcast([P, 16, HD]), ALU.mult).then_inc(qk_normed, 1)
            for n in range(8):
                b, is_k, four = n // 4, (n // 2) % 2, n % 2
                t = TR["qk_band"] + n
                if not is_k:
                    dve.wait_ge(tr_filled, t + 1)
                    V.tensor_scalar(qT[:, 4 * four:4 * four + 4, b * P:(b + 1) * P], trb[t % 2][0:HD, :].rearrange("p (h t) -> p h t", h=4),
                                    gains[0:HD, G_Q:G_Q + 1], HD_SCALE, ALU.mult, ALU.mult).then_inc(tr_out[t % 2], 1)
                elif four:
                    lo_at(C_IN2 + 3, quarters=(2 * b, 2 * b + 1))
            for n, (b, h0, hn) in enumerate(SCORE_JOBS):
                m, w = MM["s_band"] + n, (b + 1) * P
                dve.wait_ge(mm_filled, m + 1)
                V.tensor_tensor(probs_of[b][:, h0:h0 + hn, :], mmb[m % 2][:].rearrange("p (h j) -> p h j", h=hn),
                                rel_toep[:, h0:h0 + hn, w - 1::-1] if w < 256 else rel_toep[:, h0:h0 + hn, ::-1], ALU.add).then_inc(mm_out[m % 2], 1)
            for p in range(2):
                dve.wait_ge(mm_out[p], (MM["s_band"] + 6) // 2)
            for b in range(TB):
                w = (b + 1) * P
                me.link(V.memset(probs_of[b][0:64, :, w - 64:w], MASKED))
                me.link(V.tensor_reduce(mx[:, b, :], probs_of[b], axis=AX.X, op=ALU.max))
                V.tensor_scalar(neg_mx[:, b, :], mx[:, b, :], -1.0, None, ALU.mult).then_inc(max_ready, 1)
            lo_at(C_IN2 + 4)
            dve.wait_ge(exp_done, 2 * TB * HEADS + 1)
            me.link(V.reciprocal(den[:], den[:]))
            finish_softmax()

            dve.wait_ge(squared, SQUARES["gate"] + 2)
            V.tensor_scalar(var[:, 0:TB], ss[:, 0:TB], 1.0 / HALF, EPS, ALU.mult, ALU.add).then_inc(var_ready, 1)
            inverse_root(0, TB, RS["gate"])
            for b in range(TB):
                V.scalar_tensor_tensor(out=proj2[:, b, HALF:D], in0=proj2[:, b, HALF:D], scalar=rstd[:, b:b + 1], in1=gate_row[:],
                                       op0=ALU.mult, op1=ALU.mult).then_inc(gate_v_ready, 1)
            lo_at(C_OUT2)
            for b in range(TB):
                m = MM["gate"] + b
                dve.wait_ge(mm_filled, m + 1)
                bank = mmb[m % 2][:].rearrange("p (g c) -> p g c", g=8)
                V.tensor_tensor(sq[:, b * HALF:(b + 1) * HALF].rearrange("p (g c) -> p g c", g=8), bank,
                                gains[:, G_BS:G_BS + 8].unsqueeze(2).to_broadcast([P, 8, HD]), ALU.add).then_inc(mm_out[m % 2], 1)
                dve.wait_ge(mm_out[m % 2], m // 2 + 1)
                dve.wait_ge(g_free[b], (C_IN2 + 4) // 2 + 1)
                V.tensor_tensor(proj2[:, b, 0:HALF], proj2[:, b, 0:HALF], sq[:, b * HALF:(b + 1) * HALF], ALU.mult).then_inc(mixed_a_ready, 1)
            lo_columns("mixed")
            lo_at(C_OUT2 + 1)
            me.settle()
            residual(C_OUT2, 0)

            norm_behind("norm4", C_OUT2 + 1, peer_row)
            lo_at(C_QUERY + 1, quarters=(0,))
            dve.sem_inc(u_free, RING)

            def top16(values, rest, top, ix):
                me.settle()
                dve.sem_inc(dve_held, 1)
                me.put(V.max(top[:, 0:8], values))
                me.settle()
                dve.sem_inc(dve_held, 1)
                me.put(V.max_index(ix[:, 0:8], top[:, 0:8], values))
                me.put(V.match_replace(rest, top[:, 0:8], values, -3.0e38))
                me.settle()
                dve.sem_inc(dve_held, 1)
                me.put(V.max(top[:, 8:16], rest))
                me.settle()
                dve.sem_inc(dve_held, 1)
                me.put(V.max_index(ix[:, 8:16], top[:, 8:16], rest))

            def select(n, par, scores):
                for bank, count in scores:
                    dve.wait_ge(mm_out[bank], MM["peer_s"] // 2 + count)
                me.put(V.tensor_copy(tk_work[:], peer_sc[:, ds(n, 1), :].rearrange("p a k -> p (a k)")))
                for a in range(2):
                    top16(tk_work[:, a * P:(a + 1) * P], tk_rest[:, a * P:(a + 1) * P], tk_top[:, a, :], tk_ix[:, a, :])
                me.settle()
                me.put(V.tensor_copy(tk_ixf[:], tk_ix[:]))
                me.put(V.tensor_tensor(cand[:].rearrange("p (i j) -> p i j", i=TOPK), tk_top[:, 0, :].unsqueeze(2).to_broadcast([P, TOPK, TOPK]),
                                        tk_top[:, 1, :].unsqueeze(1).to_broadcast([P, TOPK, TOPK]), ALU.add))
                top16(cand[:], cand_rest[:], best[par][:], pos[:])
                me.settle()
                V.tensor_scalar(neg_best[par][:], best[par][:, 0:1], -1.0, None, ALU.mult).then_inc(best_ready, 1)
                me.put(V.tensor_scalar(pos_ij[:, 0, :], pos[:], 4, None, ALU.logical_shift_right))
                me.link(V.tensor_scalar(pos_ij[:, 1, :], pos[:], TOPK - 1, None, ALU.bitwise_and))
                me.link(V.tensor_copy(pos_f[:], pos_ij[:]))
                for a in range(2):
                    me.link(V.tensor_tensor(hit[:], iota16[:].unsqueeze(1).to_broadcast([P, TOPK, TOPK]),
                                            pos_f[:, a, :].unsqueeze(2).to_broadcast([P, TOPK, TOPK]), ALU.is_equal))
                    me.link(V.tensor_tensor(hit[:], hit[:], tk_ixf[:, a, :].unsqueeze(1).to_broadcast([P, TOPK, TOPK]), ALU.mult))
                    me.link(V.tensor_reduce(picked[:, a, :], hit[:], axis=AX.X, op=ALU.add))
                me.link(V.scalar_tensor_tensor(out=eidx_f[:], in0=picked[:, 0, :], scalar=float(NKEYS), in1=picked[:, 1, :], op0=ALU.mult, op1=ALU.add))
                V.tensor_copy(expert[:, ds(n, 1), :].rearrange("p a k -> p (a k)"), eidx_f[:]).then_inc(expert_ready, 1)

            def dots(n, par, b, rows=range(TOPK)):
                for k in rows:
                    dve.wait_ge(u_landed[k % RING], n * 32 + 16 * (k // RING + 1))
                    V.tensor_tensor_reduce(out=u_ring[:, k % RING, :], in0=u_ring[:, k % RING, :], in1=xn[:, b, :], scale=1.0, scalar=0.0, op0=ALU.mult,
                                           op1=ALU.add, accum_out=hid[par][:, k:k + 1]).then_inc(u_free, 1)

            def weights(n, par):
                dve.wait_ge(gexp_done, n + 1)
                me.link(V.reciprocal(g_inv[:], g_sum[par][:]))
                dve.wait_ge(gelu_done, n + 1)
                V.scalar_tensor_tensor(out=wgt[par][:], in0=hid_g[par][:], scalar=g_inv[:], in1=g_exp[par][:], op0=ALU.mult, op1=ALU.mult).then_inc(wgt_ready, 1)

            def expert_head(n, par, b, scores=()):
                select(n, par, scores)
                dots(n, par, b)
                weights(n, par)

            select(0, 0, [(0, 1)])
            dve.wait_ge(lo_ready, 4 * (C_QUERY + 2))
            split = [(C_QUERY + n, half) for n in (2, 3) for half in range(2)]
            for k in range(0, RING, 2):
                c, half = split[k // 2]
                lo_at(c, quarters=(2 * half, 2 * half + 1))
                dots(0, 0, 0, (k, k + 1))
            dve.wait_ge(lo_ready, 4 * C_END)
            dve.sem_inc(v_free, RING)
            dots(0, 0, 0, range(RING, TOPK))
            weights(0, 0)
            steps = me.n
            expert_head(1, 1, 0, [(0, 4), (1, 4)])
            PER = me.n - steps
            with dve.Fori(0, 3) as i:
                me.enter(i, 2 * PER)
                for par in range(2):
                    expert_head(i * 2 + (2 + par), par, 0)
            me.leave(3, 2 * PER)
            with dve.Fori(0, 4) as i:
                me.enter(i, 2 * PER)
                for par in range(2):
                    expert_head(i * 2 + (8 + par), par, 1)
            me.leave(4, 2 * PER)
            dve.wait_ge(wgt_ready, TB * PEER_HEADS)
            for k in range(PE_LAST, TOPK):
                dve.wait_ge(v_landed[k % RING], TB * PEER_HEADS * 32 - 32 + 16 * (k // RING + 1))
                if k == PE_LAST:
                    me.link(V.tensor_scalar(v_sum[:], v_ring[:, k % RING, :], wgt[1][:, k:k + 1], None, ALU.mult))
                else:
                    me.link(V.scalar_tensor_tensor(out=v_sum[:], in0=v_ring[:, k % RING, :], scalar=wgt[1][:, k:k + 1], in1=v_sum[:],
                                                   op0=ALU.mult, op1=ALU.add))
            for b in range(TB):
                dve.wait_ge(v_free, RING + (b + 1) * PEER_HEADS * TOPK - (TOPK - PE_LAST if b == TB - 1 else 0))
                if b == 0:
                    dve.wait_ge(u_free, RING + TB * PEER_HEADS * TOPK)
                for n in range(2):
                    cols = slice(n * CHUNK, (n + 1) * CHUNK)
                    if b == TB - 1:
                        ins = V.tensor_tensor(xn[:, b, cols], gemm[2 * b + n][:], v_sum[:, cols], ALU.add)
                    else:
                        ins = V.tensor_copy(xn[:, b, cols], gemm[2 * b + n][:])
                    if n == 0:
                        me.put(ins)
                ins.then_inc(out_ready, 1)

        @block.tensor
        def _(pe):
            def tr_bank(n):
                if n >= 2:
                    pe.wait_ge(tr_out[n % 2], n // 2)
                return trb[n % 2]

            def mm_bank(n):
                if n >= 2:
                    pe.wait_ge(mm_out[n % 2], n // 2)
                return mmb[n % 2]

            def tr_ready(n):
                pe.wait_ge(tr_out[n % 2], n // 2 + 1)

            def mm_ready(n):
                pe.wait_ge(mm_out[n % 2], n // 2 + 1)

            def turn(n, sources, rows=P):
                bank = tr_bank(n)
                for i, src in enumerate(sources):
                    last = nc.tensor.transpose(bank[0:rows, i * P:i * P + src.shape[0]], src, ident[0:src.shape[0], 0:src.shape[0]])
                last.then_inc(tr_filled, 1)

            def three(bank, act_k, w, b, first, last):
                cols = slice(b * P, (b + 1) * P)
                nc.tensor.matmul(bank, act_k[0][:, cols], w[0], start=first, stop=False)
                nc.tensor.matmul(bank, act_k[0][:, cols], w[1], start=False, stop=False)
                return nc.tensor.matmul(bank, act_k[1][:, cols], w[0], start=False, stop=last)

            def done(q, b, ins):
                if q == 3:
                    ins.then_inc(g_filled[b], 1)
                elif b == TB - 1:
                    ins.then_inc(w_used, 1)

            def product(c, par, free_at, lhs=hT, k_tiles=KD, width=CHUNK, before={}, ready=None, by_tile=False):
                per = k_tiles // 4
                for q, b in [(q, b) for b in range(TB) for q in range(4)] if by_tile else [(q, b) for q in range(4) for b in range(TB)]:
                    if (q, b) in before:
                        before[q, b]()
                    if b == 0:
                        pe.wait_ge(lo_ready, c * 4 + (q + 1))
                    if ready is not None:
                        ready(q, b)
                    if q == 0 and not (isinstance(free_at, int) and free_at == 0):
                        pe.wait_ge(g_free[2 * par + b], free_at)
                    for j in range(per):
                        k = q * per + j
                        last = three(gemm[2 * par + b][:, 0:width], [a[:, k, :] for a in lhs],
                                     [w[:, q, j * width:(j + 1) * width] for w in w_split], b, k == 0, k == k_tiles - 1)
                    done(q, b, last)

            def product_at(c, **kw):
                product(c, c % 2, c // 2, **kw)

            def columns(name, source, jobs):
                for n in jobs:
                    half, b = job_of(name, n)
                    rows = source(n, half, b)
                    turn(TR[name] + n, [rows[:, i * P:(i + 1) * P] for i in range(4)])

            def columns_ready(name):
                def wait(q, b):
                    if q % 2 == 0:
                        tr_ready(TR[name] + [n for n in range(4) if job_of(name, n) == (q // 2, b)][0])
                return wait

            def norm_columns(name, b):
                def rows(n, half, b):
                    pe.wait_ge(normed, 4 * NORM[name] + n + 1)
                    return xn[:, b, half * CHUNK:(half + 1) * CHUNK]
                return lambda: columns(name, rows, (2 * b, 2 * b + 1))

            pe.wait_ge(ident_made, 1)
            def spatial_weights(jobs):
                pe.wait_ge(aux_landed, 16)
                for n in jobs:
                    turn(TR["ws"] + n, [raw_ws[:, 4 * n + i, :] for i in range(4)])

            def gain_columns():
                pe.wait_ge(gains_landed, 4 * 16)
                turn(TR["gains"], [gain_rows[:]])
                spatial_weights((0,))

            product_at(0, by_tile=True, ready=columns_ready("norm1"),
                       before={(0, 0): norm_columns("norm1", 0), (3, 0): norm_columns("norm1", 1), (1, 1): gain_columns, (3, 1): lambda: spatial_weights((1,))})

            def turn_query_heads(jobs):
                for b in range(TB):
                    pe.wait_ge(g_free[b], 1)
                for n in jobs:
                    b, four = n // 2, n % 2
                    turn(TR["q_att"] + n, [proj[:, b, AQ + (4 * four + i) * HD:AQ + (4 * four + i + 1) * HD] for i in range(4)], rows=HD)

            def turn_key_heads():
                for b in range(TB):
                    pe.wait_ge(g_free[2 + b], 1)
                turn(TR["k_att"], [proj[:, b, AK + g * HD:AK + (g + 1) * HD] for g in range(KV_HEADS) for b in range(TB)], rows=HD)

            def scores(name, keys, jobs=range(6)):
                for n in jobs:
                    b, h0, hn = SCORE_JOBS[n]
                    bank, w = mm_bank(MM[name] + n), (b + 1) * P
                    for h in range(hn):
                        last = nc.tensor.matmul(bank[:, h * w:(h + 1) * w], qT[:, h0 + h, b * P:(b + 1) * P], keys(h0 + h)[:, 0:w],
                                                start=True, stop=True)
                    last.then_inc(mm_filled, 1)

            def att_scores(jobs):
                if 0 in jobs:
                    for n in range(4):
                        tr_ready(TR["q_att"] + n)
                    tr_ready(TR["k_att"])
                scores("s_att", lambda h: kT[:, h // GROUP, :], jobs)

            def turn_ret(heads):
                for j in range(2):
                    for b in range(TB):
                        pe.wait_ge(g_free[2 * j + b], 2)
                for h in heads:
                    turn(TR["ret_qk"] + h, [proj[:, b, at + h * RK:at + (h + 1) * RK] for at in (RQ, RKO) for b in range(TB)])

            product_at(1, width=256, before={(2, 0): lambda: turn_query_heads((0, 1))})
            product_at(2, before={(1, 0): lambda: turn_query_heads((2, 3)), (2, 0): turn_key_heads})
            product_at(3, before={(q, 0): (lambda q=q: att_scores((2 * q, 2 * q + 1))) for q in range(3)})
            product_at(4)
            product_at(5, before={(1, 0): lambda: turn_ret((0, 1)), (2, 0): lambda: turn_ret((2, 3))})

            def turn_probs(p_name, first, jobs=range(6)):
                for n in jobs:
                    b, h0, hn = SCORE_JOBS[n]
                    if n in (0, 2):
                        pe.wait_ge(probs_ready, first + b + 1)
                    turn(TR[p_name] + n, [probs_of[b][:, h0 + h, kb * P:(kb + 1) * P] for h in range(hn) for kb in range(b + 1)])

            def mix_values(p_name, o_name, values, tiles=range(TB)):
                for b in tiles:
                    for n in ((0, 1), (2, 3, 4, 5))[b]:
                        tr_ready(TR[p_name] + n)
                    bank = mm_bank(MM[o_name] + b)
                    for h in range(HEADS):
                        for kb in range(b + 1):
                            last = nc.tensor.matmul(bank[:, h * HD:(h + 1) * HD], probs_t[:, (h if b == 0 else 8 + 2 * h + kb), :],
                                                    values(kb, h), start=(kb == 0), stop=(kb == b))
                    last.then_inc(mm_filled, 1)

            def ret_scores(heads):
                for h in heads:
                    tr_ready(TR["ret_qk"] + h)
                    bank = mm_bank(MM["ret_s"] + h)
                    for c in range(TB):
                        last = nc.tensor.matmul(bank[:, c * P:(c + 1) * P], ret_qk[:, h, 1, c * P:(c + 1) * P], ret_qk[:, h, 0, c * P:(c + 1) * P],
                                                start=True, stop=True)
                    last.then_inc(mm_filled, 1)

            def att_values(b):
                mix_values("p_att", "o_att", lambda kb, h: proj[:, kb, AV + (h // GROUP) * HD:AV + (h // GROUP + 1) * HD], (b,))

            def ret_state():
                pe.wait_ge(ret_kd_ready, RH)
                for j in range(2):
                    pe.wait_ge(g_free[2 * j], 3)
                for n in range(2):
                    bank = mm_bank(MM["ret_state"] + n)
                    for i in range(2):
                        h = 2 * n + i
                        last = nc.tensor.matmul(bank[:, i * RV:(i + 1) * RV], proj[:, 0, RKO + h * RK:RKO + (h + 1) * RK],
                                                proj[:, 0, RVO + h * RV:RVO + (h + 1) * RV], start=True, stop=True)
                    last.then_inc(mm_filled, 1)

            def ret_out(heads):
                for n in range(2):
                    mm_ready(MM["ret_state"] + n)
                for j in range(2):
                    pe.wait_ge(g_free[2 * j + 1], 3)
                for h in heads:
                    pe.wait_ge(ret_qd_ready, h + 1)
                    mm_ready(MM["ret_s"] + h)
                    bank = mm_bank(MM["ret_o"] + h)
                    for c in range(TB):
                        last = nc.tensor.matmul(bank[:, c * RV:(c + 1) * RV], ret_s[:, h, c, :], proj[:, c, RVO + h * RV:RVO + (h + 1) * RV],
                                                start=True, stop=(c == 0))
                    last = nc.tensor.matmul(bank[:, RV:2 * RV], ret_qk[:, h, 0, P:2 * P], state[:, h, :], start=False, stop=True)
                    last.then_inc(mm_filled, 1)

            def turn_att():
                for b in range(TB):
                    mm_ready(MM["o_att"] + b)
                    turn(TR["att"] + b, [proj[:, b, i * P:(i + 1) * P] for i in range(4)])

            product_at(6, before={**{(q, 0): (lambda q=q: turn_probs("p_att", 0, (2 * q, 2 * q + 1))) for q in range(3)}, (3, 0): lambda: ret_scores((0, 1))})
            product_at(7, before={(0, 0): lambda: ret_scores((2, 3)), (1, 0): lambda: att_values(0), (2, 0): lambda: att_values(1), (3, 0): ret_state})
            product_at(8, before={(1, 0): lambda: ret_out((0, 1)), (2, 0): lambda: ret_out((2, 3)), (3, 0): turn_att})
            for c in range(9, C_ATT):
                product_at(c)

            def ret_rows(n, half, b):
                pe.wait_ge(ret_ready, n + 1)
                return proj[:, b, RVO + half * CHUNK:RVO + (half + 1) * CHUNK]

            def merged_rows(n, half, b):
                pe.wait_ge(merged_ready, n + 1)
                return proj[:, b, GA + half * CHUNK:GA + (half + 1) * CHUNK]

            for b in range(TB):
                tr_ready(TR["att"] + b)
            product_at(C_ATT, lhs=attT, k_tiles=4, before={(0, 0): lambda: columns("ret", ret_rows, (0, 1)), (2, 0): lambda: columns("ret", ret_rows, (2, 3))})
            product_at(C_ATT + 1, lhs=attT, k_tiles=4)
            product_at(C_RET, ready=columns_ready("ret"))
            product_at(C_RET + 1, before={(2, 0): lambda: columns("merged", merged_rows, (0, 1))})
            product_at(C_OUT, before={(1, 1): lambda: columns("merged", merged_rows, (2, 3))}, ready=columns_ready("merged"))
            product_at(C_OUT + 1, by_tile=True, before={(3, 1): norm_columns("norm2", 0)})

            n_ff = TR["ff"]

            def ff_rows_turned(i, par):
                p = (n_ff + par) % 2
                for b in range(TB):
                    pe.wait_ge(g_free[2 * par + b], i + (C_FF // 2 + 1))
                pe.wait_ge(tr_out[p], i + (n_ff + par) // 2)
                for fk in range(2):
                    for b in range(TB):
                        at = fk * S + b * P
                        last = nc.tensor.transpose(trb[p][:, at:at + P], ff_rows[:, par, b, fk * P:(fk + 1) * P], ident[:])
                last.then_inc(tr_filled, 1)

            product_at(C_FF, by_tile=True, ready=columns_ready("norm2"), before={(3, 0): norm_columns("norm2", 1)})
            with pe.Fori(0, 5) as i:
                product(i * 2 + (C_FF + 1), 1, i + (C_FF + 1) // 2)
                ff_rows_turned(i, 0)
                product(i * 2 + (C_FF + 2), 0, i + (C_FF + 2) // 2)
                ff_rows_turned(i, 1)

            for f in range(N_FF):
                c = C_DOWN + f
                last_f = f == N_FF - 1
                for q, b in [(q, b) for b in range(TB) for q in range(4)] if last_f else [(q, b) for q in range(4) for b in range(TB)]:
                    k, n = q // 2, q % 2
                    if b == 0:
                        pe.wait_ge(lo_ready, 4 * c + q + 1)
                    if q == 0:
                        tr_ready(n_ff + f)
                    if f == 0 and k == 0:
                        pe.wait_ge(g_free[2 * n + b], C_DOWN // 2 + (1 - n))
                    last = three(gemm[2 * n + b][:], [a[:, 2 * f + k, :] for a in ffT], [w[:, q, 0:CHUNK] for w in w_split], b,
                                 f == 0 and k == 0, last_f and k == 1)
                    done(q, b, last)
                if f == 0:
                    ff_rows_turned(5, 0)
            pe.wait_ge(late_landed, 6 * 16)
            for n in range(4):
                turn(TR["keys"] + n, [raw_keys[:, 4 * n + i, :] for i in range(4)])

            product_at(C_IN2, by_tile=True, ready=columns_ready("norm3"), before={(0, 0): norm_columns("norm3", 0), (3, 0): norm_columns("norm3", 1)})
            product_at(C_IN2 + 1)
            product_at(C_IN2 + 2)
            for n in range(8):
                b, is_k, four = n // 4, (n // 2) % 2, n % 2
                if n % 4 == 0:
                    pe.wait_ge(qk_normed, b + 1)
                at = D + HALF * is_k + 4 * four * HD
                turn(TR["qk_band"] + n, [proj2[:, b, at + i * HD:at + (i + 1) * HD] for i in range(4)], rows=HD)
            for n in range(6, 8):
                tr_ready(TR["qk_band"] + n)
            scores("s_band", lambda h: kT2[:, h, :])
            product_at(C_IN2 + 3)
            product_at(C_IN2 + 4)
            pe.wait_ge(gate_v_ready, TB)
            for b in range(TB):
                bank = mm_bank(MM["gate"] + b)
                for g in range(8):
                    last = nc.tensor.matmul(bank[:, g * HD:(g + 1) * HD], ws_t[:, g, :], proj2[:, b, HALF + g * HD:HALF + (g + 1) * HD],
                                            start=True, stop=True)
                last.then_inc(mm_filled, 1)
            turn_probs("p_band", 2)
            for b in range(TB):
                pe.wait_ge(g_free[b], (C_IN2 + 2) // 2 + 1)
            mix_values("p_band", "o_band", lambda kb, h: proj2[:, kb, 2 * D + h * HD:2 * D + (h + 1) * HD])

            def mixed_rows(n, half, b):
                if half == 0:
                    pe.wait_ge(mixed_a_ready, b + 1)
                else:
                    mm_ready(MM["o_band"] + b)
                return proj2[:, b, D * half:D * half + HALF]

            product_at(C_OUT2, before={(0, 0): lambda: columns("mixed", mixed_rows, (0, 1)), (1, 0): lambda: columns("mixed", mixed_rows, (2, 3))},
                       ready=columns_ready("mixed"))
            product_at(C_OUT2 + 1, by_tile=True, before={(3, 1): norm_columns("norm4", 0)})

            def turn_queries(n, tiles=range(TB)):
                c = C_QUERY + n
                for b in tiles:
                    pe.wait_ge(g_free[2 * (c % 2) + b], c // 2 + 1)
                    turn(TR["query"] + 2 * n + b, [qp[:, n % 2, b, i * P:(i + 1) * P] for i in range(4)])

            def key_scores(n, tiles=range(TB)):
                for b in tiles:
                    tr_ready(TR["query"] + 2 * n + b)
                    bank = mm_bank(MM["peer_s"] + 2 * n + b)
                    for i in range(4):
                        last = nc.tensor.matmul(bank[:, i * P:(i + 1) * P], qpT[:, n % 2, i, b * P:(b + 1) * P], keys_t[:, 4 * n + i, :],
                                                start=True, stop=True)
                    last.then_inc(mm_filled, 1)

            product_at(C_QUERY, by_tile=True, ready=columns_ready("norm4"),
                       before={(3, 0): norm_columns("norm4", 1), (1, 1): lambda: turn_queries(0, (0,)), (2, 1): lambda: key_scores(0, (0,))})
            for n in range(3):
                tiles = (1,) if n == 0 else range(TB)
                product_at(C_QUERY + n + 1, before={(1, 0): lambda: turn_queries(n, tiles), (2, 0): lambda: key_scores(n, tiles)})
            turn_queries(3)
            key_scores(3)

            for c in range(2):
                for b in range(TB):
                    pe.wait_ge(g_free[2 * c + b], (C_END - 1 - (1 - c if (C_END - 1) % 2 else c)) // 2 + 1)
            def add_rows(b, i, rows=TOPK, end=False):
                for k in range(rows):
                    pe.wait_ge(diag_ready, i * TOPK + (b * PEER_HEADS * TOPK + k + 1))
                    pe.wait_ge(v_landed[k % RING], i * 32 + (b * PEER_HEADS * 32 + 16 * (k // RING + 1)))
                    for n in range(2):
                        last = nc.tensor.matmul(gemm[2 * b + n][:], diag[k % 4][:], v_ring[:, k % RING, n * CHUNK:(n + 1) * CHUNK],
                                                start=False, stop=(end and k == rows - 1))
                    last.then_inc(v_free, 1)

            for b in range(TB):
                for n in range(2):
                    nc.tensor.matmul(gemm[2 * b + n][:], ident[:], x_sb[:, b, n * CHUNK:(n + 1) * CHUNK], start=True, stop=False)
                with pe.Fori(0, PEER_HEADS - 1) as i:
                    add_rows(b, i)
                add_rows(b, PEER_HEADS - 1, TOPK if b < TB - 1 else PE_LAST, end=True)


NAMES = ["x", "norm_mix", "w_in", "att_sinks", "ret_gn_gain", "w_att_o", "w_ret_o", "w_out", "norm_ffn", "w_gate", "w_up", "w_down",
         "final_norm", "ln_mix_g_2", "w_in_2", "gmlp_norm_g_2", "gmlp_w_s_2", "gmlp_b_s_2", "q_norm_g_2", "k_norm_g_2", "rel_bias_2",
         "w_out_2", "ln_ffn_g_2", "peer_w_query_2", "peer_sub_keys_2", "peer_u_2", "peer_v_2"]


def kernel(**inputs):
    import numpy as np
    import concourse.bacc as bacc
    from concourse.bass_utils import run_bass_kernel_spmd

    nc = bacc.Bacc("TRN2", target_bir_lowering=False, num_devices=1)
    arrays, args = {}, []
    for name in NAMES:
        a = np.ascontiguousarray(inputs[name])
        arrays[f"in_{name}"] = a
        args.append(nc.dram_tensor(f"in_{name}", a.shape, mybir.dt.from_np(a.dtype), kind="ExternalInput").ap())
    out = nc.dram_tensor("out", inputs["x"].shape, mybir.dt.float32, kind="ExternalOutput").ap()
    two_block_kernel(nc, *args, out)
    result = run_bass_kernel_spmd(nc, [arrays], core_ids=[0])
    return result.results[0]["out"]
```
